# Optimizing a Trainium2 kernel written in Bass

```python
import jax, jax.numpy as jnp
from jax import lax
import numpy as np

D_MODEL = 1024
BATCH = 1
SEQ = 2048
DEPTH = 1
DEC_BATCH = 8
DEC_SEQ = 16
PAST_LEN = 1024

CHUNK = 64
POOL_WIDTH = D_MODEL // 4
POOL_GROUPS = 4
POOL_GROUP_DIM = POOL_WIDTH // POOL_GROUPS
POOL_WINDOWS = (2, 4, 8, 16)
POOL_HIST = max(POOL_WINDOWS) - 1
ATT_WIDTH = D_MODEL - POOL_WIDTH
HEAD_DIM = 64
N_HEADS = ATT_WIDTH // HEAD_DIM
MIX_WIDTH = POOL_WIDTH + ATT_WIDTH
IN_COLS = POOL_WIDTH + 3 * ATT_WIDTH + N_HEADS
D_FF = 4 * D_MODEL
Q_BLOCK = 128
EPS = 1e-6
FORGET_W_SCALE = 0.1

kernel_name = "hymba_pool_fox_stream_step"

def rms_norm(x):
    xf = x.astype(jnp.float32)
    return (xf * lax.rsqrt(jnp.mean(xf * xf, axis=-1, keepdims=True) + EPS)).astype(x.dtype)

def modulate(x, shift, scale):
    return x * (1 + scale[:, None, :]) + shift[:, None, :]

def pool_mixer(u, hist, pos0, w_pool, pool_scale):
    B, T, _ = u.shape
    z = jnp.concatenate([hist.astype(u.dtype), u], axis=1)
    zf = z.astype(jnp.float32)
    cs = jnp.concatenate([jnp.zeros_like(zf[:, :1]), jnp.cumsum(zf, axis=1)], axis=1)
    pos = (pos0 + jnp.arange(T)).astype(jnp.float32)
    end = POOL_HIST + 1
    uf = u.astype(jnp.float32)
    outs = []
    for g, w in enumerate(POOL_WINDOWS):
        sl = slice(g * POOL_GROUP_DIM, (g + 1) * POOL_GROUP_DIM)
        win_sum = cs[:, end:end + T, sl] - cs[:, end - w:end - w + T, sl]
        count = jnp.minimum(pos + 1.0, float(w))[None, :, None]
        outs.append(win_sum / count - uf[..., sl])
    mixed = jnp.stack(outs, axis=2).astype(u.dtype)
    y = jnp.einsum('btgc,gcd->btgd', mixed, w_pool).reshape(B, T, POOL_WIDTH)
    return y * pool_scale, z[:, -POOL_HIST:]

def fox_block(q, k, v, fq, fk, q_pos, k_pos):
    s = jnp.einsum('bqhd,bkhd->bhqk', q, k, preferred_element_type=jnp.float32) * (HEAD_DIM ** -0.5)
    s = s + jnp.swapaxes(fq, 1, 2)[..., :, None] - jnp.swapaxes(fk, 1, 2)[..., None, :]
    mask = (k_pos[None, :] <= q_pos[:, None])[None, None]
    p = jax.nn.softmax(jnp.where(mask, s, -jnp.inf), axis=-1)
    return jnp.einsum('bhqk,bkhd->bqhd', p.astype(v.dtype), v)

def fox_prompt(q, k, v, F):
    B, T = q.shape[:2]
    nb = T // Q_BLOCK
    qb = q.reshape(B, nb, Q_BLOCK, N_HEADS, HEAD_DIM).swapaxes(0, 1)
    fb = F.reshape(B, nb, Q_BLOCK, N_HEADS).swapaxes(0, 1)
    pb = jnp.arange(T).reshape(nb, Q_BLOCK)
    k_pos = jnp.arange(T)
    out = lax.map(lambda a: fox_block(a[0], k, v, a[1], F, a[2], k_pos), (qb, fb, pb))
    return out.swapaxes(0, 1).reshape(B, T, N_HEADS, HEAD_DIM)

def trunk_layer(x, c, pool_hist, past_k, past_v, past_logf, pos0,
                w_mod, b_mod, w_in, b_f, q_gain, k_gain, w_pool, pool_scale, w_out, w_up, w_down):
    B, T, _ = x.shape

    mod = jax.nn.silu(c) @ w_mod + b_mod
    sh1, sc1, g1, sh2, sc2, g2 = jnp.split(mod, 6, axis=-1)

    h = modulate(rms_norm(x), sh1, sc1)
    proj = h @ w_in
    u = proj[..., :POOL_WIDTH]
    o = POOL_WIDTH
    q = proj[..., o:o + ATT_WIDTH].reshape(B, T, N_HEADS, HEAD_DIM)
    k = proj[..., o + ATT_WIDTH:o + 2 * ATT_WIDTH].reshape(B, T, N_HEADS, HEAD_DIM)
    v = proj[..., o + 2 * ATT_WIDTH:o + 3 * ATT_WIDTH].reshape(B, T, N_HEADS, HEAD_DIM)
    f_logit = proj[..., o + 3 * ATT_WIDTH:]
    q = rms_norm(q) * q_gain
    k = rms_norm(k) * k_gain
    logf = jax.nn.log_sigmoid(f_logit.astype(jnp.float32) + b_f.astype(jnp.float32))

    pool_y, pool_state = pool_mixer(u, pool_hist, pos0, w_pool, pool_scale)

    if past_k is None:
        att = fox_prompt(q, k, v, jnp.cumsum(logf, axis=1))
    else:
        P = past_k.shape[1]
        k_all = jnp.concatenate([past_k.astype(k.dtype), k], axis=1)
        v_all = jnp.concatenate([past_v.astype(v.dtype), v], axis=1)
        F_all = jnp.cumsum(jnp.concatenate([past_logf.astype(jnp.float32), logf], axis=1), axis=1)
        att = fox_block(q, k_all, v_all, F_all[:, P:], F_all, P + jnp.arange(T), jnp.arange(P + T))

    mix = jnp.concatenate([pool_y, att.reshape(B, T, ATT_WIDTH)], axis=-1)
    x = x + g1[:, None, :] * (mix @ w_out)

    h2 = modulate(rms_norm(x), sh2, sc2)
    ff = jnp.square(jax.nn.relu(h2 @ w_up)) @ w_down
    x = x + g2[:, None, :] * ff
    return x, k, v, logf.astype(x.dtype), pool_state

def setup_inputs(seed: int = 0) -> dict:
    key = jax.random.key(seed)
    ks = jax.random.split(key, 20)
    f32 = jnp.float32

    def nrm(k, shape, s=1.0):
        return s * jax.random.normal(k, shape, f32)

    head_bias = jnp.linspace(1.0, 7.0, N_HEADS, dtype=f32)
    w_in = nrm(ks[10], (DEPTH, D_MODEL, IN_COLS), D_MODEL ** -0.5)
    w_in = w_in.at[..., POOL_WIDTH + 3 * ATT_WIDTH:].multiply(FORGET_W_SCALE)
    b_f = head_bias[None, :] + nrm(ks[11], (DEPTH, N_HEADS), 0.1)
    cache_logf = jax.nn.log_sigmoid(head_bias + nrm(ks[6], (DEPTH, DEC_BATCH, PAST_LEN, N_HEADS), 0.3))
    return {
        'x_prompt': nrm(ks[0], (BATCH, SEQ, D_MODEL)),
        'x_sample': nrm(ks[1], (DEC_BATCH, DEC_SEQ, D_MODEL)),
        'c_prompt': nrm(ks[2], (BATCH, D_MODEL)),
        'c_sample': nrm(ks[3], (DEC_BATCH, D_MODEL)),
        'cache_k': nrm(ks[4], (DEPTH, DEC_BATCH, PAST_LEN, N_HEADS, HEAD_DIM)),
        'cache_v': nrm(ks[5], (DEPTH, DEC_BATCH, PAST_LEN, N_HEADS, HEAD_DIM)),
        'cache_logf': cache_logf,
        'cache_pool': nrm(ks[7], (DEPTH, DEC_BATCH, POOL_HIST, POOL_WIDTH)),
        'w_mod': nrm(ks[8], (DEPTH, D_MODEL, 6 * D_MODEL), 0.5 * D_MODEL ** -0.5),
        'b_mod': nrm(ks[9], (DEPTH, 6 * D_MODEL), 0.02),
        'w_in': w_in,
        'b_f': b_f,
        'q_gain': 1.0 + nrm(ks[12], (DEPTH, HEAD_DIM), 0.02),
        'k_gain': 1.0 + nrm(ks[13], (DEPTH, HEAD_DIM), 0.02),
        'w_pool': nrm(ks[14], (DEPTH, POOL_GROUPS, POOL_GROUP_DIM, POOL_GROUP_DIM), POOL_GROUP_DIM ** -0.5),
        'pool_scale': 1.0 + nrm(ks[15], (DEPTH, POOL_WIDTH), 0.02),
        'w_out': nrm(ks[16], (DEPTH, MIX_WIDTH, D_MODEL), MIX_WIDTH ** -0.5),
        'w_up': nrm(ks[17], (DEPTH, D_MODEL, D_FF), D_MODEL ** -0.5),
        'w_down': nrm(ks[18], (DEPTH, D_FF, D_MODEL), D_FF ** -0.5),
    }

def reference(x_prompt, x_sample, c_prompt, c_sample, cache_k, cache_v, cache_logf, cache_pool,
              w_mod, b_mod, w_in, b_f, q_gain, k_gain, w_pool, pool_scale, w_out, w_up, w_down):
    y_prompt, y_sample = x_prompt, x_sample
    k_p, v_p, f_p, p_p = [], [], [], []
    k_s, v_s, f_s, p_s = [], [], [], []
    past = cache_k.shape[2]
    pool_zero = jnp.zeros((x_prompt.shape[0], POOL_HIST, POOL_WIDTH), x_prompt.dtype)
    for l in range(DEPTH):
        wts = (w_mod[l], b_mod[l], w_in[l], b_f[l], q_gain[l], k_gain[l],
               w_pool[l], pool_scale[l], w_out[l], w_up[l], w_down[l])
        y_prompt, kl, vl, fl, pl = trunk_layer(y_prompt, c_prompt, pool_zero, None, None, None, 0, *wts)
        k_p.append(kl); v_p.append(vl); f_p.append(fl); p_p.append(pl)
        y_sample, kl, vl, fl, pl = trunk_layer(y_sample, c_sample, cache_pool[l], cache_k[l], cache_v[l],
                                               cache_logf[l], past, *wts)
        k_s.append(kl); v_s.append(vl); f_s.append(fl); p_s.append(pl)
    return (y_prompt, y_sample,
            jnp.stack(k_p), jnp.stack(v_p), jnp.stack(f_p), jnp.stack(p_p),
            jnp.stack(k_s), jnp.stack(v_s), jnp.stack(f_s), jnp.stack(p_s))


_drawn_inputs = setup_inputs


def setup_inputs(seed=0):
    import zlib

    import numpy as np

    out = dict(_drawn_inputs(seed))
    spreads = {}
    factors = {}
    for name, (base, spread) in spreads.items():
        noise = np.random.default_rng([zlib.crc32(name.encode()), seed]).standard_normal(out[name].shape)
        drawn = base * np.exp(spread * noise) if base else spread * noise
        out[name] = __import__('jax').numpy.asarray(drawn.astype(out[name].dtype))
    for name, factor in factors.items():
        out[name] = (out[name] * factor).astype(out[name].dtype)
    return out
```

```python
import concourse.bass as bass
from concourse import mybir
from contextlib import ExitStack

F32 = mybir.dt.float32
F32R = mybir.dt.float32r
ALU = mybir.AluOpType
ACT = mybir.ActivationFunctionType
AX_X = mybir.AxisListType.X

P = 128
D = 1024
KT = D // P
SEQ = 2048
STREAMS = 8
NEW = 16
PAST = 1024
ROWS = SEQ + STREAMS * NEW
QT = SEQ // P
HEADS = 12
HD = 64
ATT = HEADS * HD
POOL = 256
HIST = 15
IN_COLS = POOL + 3 * ATT + HEADS
FF = 4096
EPS = 1e-6

BLOCKS = 4
TILES0, TILES = 5, 4


def n_tiles(b):
    return TILES0 if isinstance(b, int) and b == 0 else TILES


def tiles_before(b):
    return 0 if isinstance(b, int) and b == 0 else b * TILES + 1


def blocks(eng, body):
    body(0, 1)
    with eng.Fori(1, BLOCKS - 1) as b:
        body(b, b + 1)
    body(BLOCKS - 1, None)


def prompt_row(b, r):
    return (b * TILES + r) * P


def is_streams(b, r):
    return isinstance(b, int) and b == 0 and r == TILES0 - 1


def modulation(nc, t, sems):
    C = 1 + STREAMS
    NG, W, CT = 3, 512, 4
    DEPTH = 3
    with ExitStack() as ctx:
        sb = lambda name, shape, dt=F32: ctx.enter_context(nc.sbuf_tensor(name, shape, dt))
        c = sb("m_c", [C, D])
        e = sb("m_e", [C, D])
        cT = sb("m_cT", [P, KT, C])
        wm = sb("m_w", [P, DEPTH, CT * W])
        bm = sb("m_b", [P, NG, W])
        mo = sb("m_out", [P, NG, W])
        ident = sb("m_ident", [P, P])
        ps_c = ctx.enter_context(nc.psum_tensor("m_psc", [P, KT, C], F32))
        ps = [ctx.enter_context(nc.psum_tensor(f"m_ps{i}", [P, W], F32)) for i in range(NG)]
        c_in = sems("m_c_in")
        b_in = sems("m_b_in")
        w_in = [sems(f"m_w_in{i}") for i in range(DEPTH)]
        ident0 = sems("m_ident0")
        ident_ready = sems("m_ident_ready")
        e_ready = sems("m_e_ready")
        silu_ready = sems("m_silu_ready")
        chained = sems("m_chained")
        cT_psum = sems("m_cT_psum")
        cT_ready = sems("m_cT_ready")
        w_used = sems("m_w_used")
        mod_ready = sems("m_mod_ready")
        stored = sems("m_stored")

        block = ctx.enter_context(nc.Block())

        @block.sync
        def _(sp):
            sp.dma_start(c[0:1, :], t["c_prompt"]).then_inc(c_in, 16)
            sp.dma_start(c[1:C, :], t["c_sample"]).then_inc(c_in, 16)
            bias = t["b_mod"].rearrange("o (g j n) -> (o j) g n", g=NG, j=CT)
            for j in range(CT):
                sp.dma_start(bm[32 * j:32 * j + C, :, :],
                             bias[j:j + 1].broadcast_to([C, NG, W])).then_inc(b_in, 16)
            for n in range(NG * KT):
                g, k = divmod(n, KT)
                if n >= DEPTH:
                    sp.wait_ge(w_used, n - DEPTH + 1)
                sp.dma_start(wm[:, n % DEPTH, :],
                             t["w_mod"][0, k * P:(k + 1) * P, g * CT * W:(g + 1) * CT * W]
                             ).then_inc(w_in[n % DEPTH], 16)
            for g in range(NG):
                sp.wait_ge(mod_ready, CT * (g + 1))
                for j in range(CT):
                    col = (g * CT + j) * W
                    sp.dma_start(t["mod"][:, col:col + W], mo[32 * j:32 * j + C, g, :]).then_inc(stored, 16)
            sp.wait_ge(stored, 16 * NG * CT)

        @block.gpsimd
        def _(pool):
            pool.memset(ident[:], 0.0).then_inc(ident0, 1)
            pool.wait_ge(ident0, 1)
            pool.affine_select(out=ident[:], in_=ident[:], compare_op=ALU.not_equal, fill=1.0, base=0,
                               pattern=[[-1, P]], channel_multiplier=1).then_inc(ident_ready, 1)

        @block.scalar
        def _(act):
            act.wait_ge(c_in, 32)
            act.activation(e[:], c[:], ACT.Exp, scale=-1.0).then_inc(e_ready, 1)

        @block.vector
        def _(dve):
            dve.wait_ge(e_ready, 1)
            dve.tensor_scalar(e[:], e[:], 1.0, None, ALU.add).then_inc(chained, 1)
            dve.wait_ge(chained, 1)
            dve.reciprocal(e[:], e[:]).then_inc(chained, 1)
            dve.wait_ge(chained, 2)
            dve.tensor_tensor(c[:], c[:], e[:], ALU.mult).then_inc(silu_ready, 1)
            dve.wait_ge(cT_psum, 1)
            dve.tensor_copy(cT[:], ps_c[:]).then_inc(cT_ready, 1)
            dve.wait_ge(b_in, 16 * CT)
            for g in range(NG):
                dve.wait_ge(w_used, KT * (g + 1))
                for j in range(CT):
                    one = 1.0 if (g * CT + j) // 2 in (1, 4) else 0.0
                    rows = slice(32 * j, 32 * j + C)
                    dve.scalar_tensor_tensor(mo[rows, g, :], ps[g][rows, :], one, bm[rows, g, :],
                                             ALU.add, ALU.add).then_inc(mod_ready, 1)

        @block.tensor
        def _(pe):
            pe.wait_ge(ident_ready, 1)
            pe.wait_ge(silu_ready, 1)
            for k in range(KT):
                last = pe.transpose(ps_c[:, k, :], c[:, k * P:(k + 1) * P], ident[0:C, 0:C])
            last.then_inc(cT_psum, 1)
            pe.wait_ge(cT_ready, 1)
            for n in range(NG * KT):
                g, k = divmod(n, KT)
                pe.wait_ge(w_in[n % DEPTH], 16 * (n // DEPTH + 1))
                for j in range(CT):
                    last = pe.matmul(ps[g][32 * j:32 * j + C, :], cT[:, k, :], wm[:, n % DEPTH, j * W:(j + 1) * W],
                                     start=(k == 0), stop=(k == KT - 1), tile_position=(0, 32 * j))
                last.then_inc(w_used, 1)


HG = 6
QKV_W = HG * HD
UF_W = POOL + HEADS
CHUNKS = [("q", 0), ("q", 1), ("k", 0), ("k", 1), ("v", 0), ("v", 1), ("uf", 0)]
NCH = len(CHUNKS)
UF = NCH - 1


def tile_no(b, r):
    return tiles_before(b) + r


def tile_slot(b, r):
    return (r if isinstance(b, int) and b == 0 else TILES0 - TILES + r) % 2


def tile_half(b, r):
    return r // 2 if isinstance(b, int) and b == 0 else 2 * b + (1 + r) // 2


def step_taken(b, c, r):
    return not (isinstance(b, int) and b == 0 and c == 0 and r < 2)


def step_no(b, c, r):
    return NCH * tiles_before(b) + c * n_tiles(b) + r


def step_mod(b, c, r, n):
    first = 0 if isinstance(b, int) and b == 0 else NCH * (TILES0 - TILES)
    return (first + c * n_tiles(b) + r) % n


def step_half(b, c, r):
    if isinstance(b, int) and b == 0:
        return (c * TILES0 + r) // 2
    return b * (NCH * TILES // 2) + (NCH + c * TILES + r) // 2


def block_steps(b, following):
    R = n_tiles(b)
    for c in range(NCH):
        if c == UF and following is not None:
            yield "weights", following, 0, 0
            yield "normalize", following, 0, 0
        for r in range(R):
            yield "project", b, c, r
            if r == 0 and c + 1 < NCH:
                yield "weights", b, c + 1, 0
            if c == UF and following is not None:
                if r + 1 < TILES:
                    yield "normalize", following, 0, r + 1
                if r < TILES:
                    yield "transpose", following, 0, r


def projection(nc, t, sems):
    with ExitStack() as ctx:
        sb = lambda name, shape, dt=F32: ctx.enter_context(nc.sbuf_tensor(name, shape, dt))
        x = sb("p_x", [P, 2, D])
        h = sb("p_h", [P, 2, D])
        hT_hi = sb("p_hT_hi", [P, KT, TILES0 * P], F32R)
        hT_lo = sb("p_hT_lo", [P, KT, TILES0 * P], F32R)
        widths = [QKV_W, QKV_W, UF_W]
        raw = [sb(f"p_raw{i}", [P, KT, w]) for i, w in enumerate(widths)]
        w_hi = [sb(f"p_whi{i}", [P, KT, w], F32R) for i, w in enumerate(widths)]
        w_lo = [sb(f"p_wlo{i}", [P, KT, w], F32R) for i, w in enumerate(widths)]
        scale1 = sb("p_scale", [P, 2, D])
        shift1 = sb("p_shift", [P, 2, D])
        gain = {"q": sb("p_qgain", [P, HD]), "k": sb("p_kgain", [P, HD])}
        bf = sb("p_bf", [P, HEADS])
        ident = sb("p_ident", [P, P])
        ssq = sb("p_ssq", [P, 2])
        rstd = sb("p_rstd", [P, 2])
        eps = sb("p_eps", [P, 1])
        CONSTS = 2 * (1 + STREAMS) + 3
        square = sb("p_square", [P, QKV_W])
        ssh = sb("p_ssh", [P, HG])
        rh = sb("p_rh", [P, HG])
        fz = sb("p_fz", [P, QT + 1, HEADS])
        fa = sb("p_fa", [P, QT + 1, HEADS])
        nat = sb("p_nat", [P, 2, QKV_W])
        split = [sb(f"p_split{i}", [P, HG, 2, HD], F32R) for i in range(2)]
        ps_x = [ctx.enter_context(nc.psum_tensor(f"p_psx{i}", [P, KT, P], F32)) for i in range(2)]
        ps_m = [ctx.enter_context(nc.psum_tensor(f"p_psm{i}", [P, 512], F32)) for i in range(4)]

        consts_in, ident0, ident_ready = sems("p_consts_in"), sems("p_ident0"), sems("p_ident_ready")
        consts_ready = sems("p_consts_ready")
        x_in = [sems(f"p_x_in{i}") for i in range(2)]
        squared, rms_ready, rstd_ready = sems("p_squared"), sems("p_rms_ready"), sems("p_rstd_ready")
        scaled, h_ready, hT_psum = sems("p_scaled"), sems("p_h_ready"), sems("p_hT_psum")
        hT_hi_ready, hT_ready = sems("p_hT_hi_ready"), sems("p_hT_ready")
        raw_in = [sems(f"p_raw_in{i}") for i in range(3)]
        w_hi_ready, w_ready, projected = sems("p_w_hi_ready"), sems("p_w_ready"), sems("p_projected")
        sq_ready, ss_ready, rmsh_ready, rh_ready = sems("p_sq_ready"), sems("p_ss_ready"), sems("p_rmsh_ready"), sems("p_rh_ready")
        normed, gained, hi_ready = sems("p_normed"), sems("p_gained"), sems("p_hi_ready")
        u_copied, f_chain, log1p_f = sems("p_u_copied"), sems("p_f_chain"), sems("p_log1p_f")
        staged = sems("p_staged")
        stored = [sems(f"p_stored{i}") for i in range(2)]

        def w_slot(c):
            return 2 if c == UF else c % 2

        def w_uses(b, c):
            return b if c == UF else 3 * b + c // 2

        def slot_taken(b, c):
            return not (isinstance(b, int) and b == 0 and (c < 2 or c == UF))

        def chunk_before(b, c):
            if 2 <= c < UF:
                return b * NCH + c - 2
            return b * NCH - (NCH - UF if c == UF else NCH - 4 - c)

        def steps_before(b, c):
            if 2 <= c < UF:
                return NCH * tiles_before(b) + (c - 1) * n_tiles(b)
            return NCH * tiles_before(b) - (0 if c == UF else NCH - 5 - c) * TILES

        def x_tile_taken(b, r):
            return not (isinstance(b, int) and b == 0 and r < 2)

        block = ctx.enter_context(nc.Block())

        @block.sync
        def _(sp):
            for to, col in ((scale1, D), (shift1, 0)):
                sp.dma_start(to[:, 0, :], t["mod"][0:1, col:col + D].broadcast_to([P, D])).then_inc(consts_in, 16)
                for s in range(STREAMS):
                    sp.dma_start(to[NEW * s:NEW * (s + 1), 1, :],
                                 t["mod"][1 + s:2 + s, col:col + D].broadcast_to([NEW, D])
                                 ).then_inc(consts_in, 16)
            sp.dma_start(gain["q"][:], t["q_gain"].broadcast_to([P, HD])).then_inc(consts_in, 16)
            sp.dma_start(gain["k"][:], t["k_gain"].broadcast_to([P, HD])).then_inc(consts_in, 16)
            sp.dma_start(bf[:], t["b_f"].broadcast_to([P, HEADS])).then_inc(consts_in, 16)

            def load_x(b, r):
                s = tile_slot(b, r)
                if x_tile_taken(b, r):
                    sp.wait_ge(scaled, tile_no(b, r) - 1)
                if is_streams(b, r):
                    src = t["x_sample"].rearrange("b n d -> (b n) d")
                else:
                    src = t["x_prompt"][0, bass.ds(prompt_row(b, r), P), :]
                sp.dma_start(x[:, s, :], src).then_inc(x_in[s], 16)

            def load_weights(b, c):
                s = w_slot(c)
                if slot_taken(b, c):
                    sp.wait_ge(w_ready, chunk_before(b, c) + 1)
                kind, half = CHUNKS[c]
                w = t["w_in"][0].rearrange("(k p) n -> p k n", p=P)
                if kind == "uf":
                    sp.dma_start(raw[s][:, :, 0:POOL], w[:, :, 0:POOL]).then_inc(raw_in[s], 16)
                    sp.dma_start(raw[s][:, :, POOL:UF_W], w[:, :, IN_COLS - HEADS:IN_COLS]).then_inc(raw_in[s], 16)
                else:
                    col = POOL + "qkv".index(kind) * ATT + half * QKV_W
                    sp.dma_start(raw[s][:], w[:, :, col:col + QKV_W]).then_inc(raw_in[s], 16)

            def store(b, c, r):
                s = step_mod(b, c, r, 2)
                kind, half = CHUNKS[c]
                streams = is_streams(b, r)
                rows = slice(SEQ, ROWS) if streams else bass.ds(prompt_row(b, r), P)
                sp.wait_ge(staged, step_no(b, c, r) + 1)
                if kind == "uf":
                    for part in (slice(0, POOL // 2), slice(POOL // 2, POOL)):
                        sp.dma_start(t["u"][rows, part], nat[:, s, part]).then_inc(stored[s], 16)
                    return
                heads, cols = slice(half * HG, (half + 1) * HG), slice(half * QKV_W, (half + 1) * QKV_W)
                dst = t[kind + "_split"][rows, heads, :].bitcast(F32)
                sp.dma_start(dst, split[s][:].rearrange("p h a d -> p h (a d)").bitcast(F32)).then_inc(stored[s], 16)
                if kind == "q":
                    dst = t["q_nat"][rows, cols]
                else:
                    dst = t[kind + "_s"][:, cols] if streams else t[kind + "_p"][rows, cols]
                sp.dma_start(dst, nat[:, s, :]).then_inc(stored[s], 16)

            load_x(0, 0)
            load_weights(0, 0)
            load_x(0, 1)
            load_weights(0, 1)
            for r in range(2, TILES0):
                load_x(0, r)

            def body(b, following):
                for what, blk, c, r in block_steps(b, following):
                    if what == "weights":
                        if c + 1 < NCH:
                            load_weights(blk, c + 1)
                        if c == UF - 1 and following is not None:
                            load_x(following, 0)
                            load_x(following, 1)
                        if c == UF and following is not None:
                            load_weights(following, 0)
                    elif what == "normalize":
                        if 2 <= r + 2 < TILES:
                            load_x(blk, r + 2)
                    elif what == "project":
                        store(blk, c, r)
            blocks(sp, body)
            sp.wait_ge(f_chain, 3)
            logf = t["logf_p"].rearrange("(n p) h -> p n h", p=P)
            sp.dma_start(logf[:, 0:TILES, :], fz[:, 0:TILES, :]).then_inc(consts_in, 16)
            sp.dma_start(logf[:, TILES:, :], fz[:, TILES0:, :]).then_inc(consts_in, 16)
            sp.dma_start(t["logf_s"], fz[:, TILES0 - 1, :]).then_inc(consts_in, 16)
            sp.wait_ge(consts_in, 16 * (CONSTS + 3))
            last = BLOCKS - 1, UF, TILES - 1
            for s in range(2):
                uses = step_half(*last) + (1 if s <= step_mod(*last, 2) else 0)
                sp.wait_ge(stored[s], 32 * uses)

        @block.gpsimd
        def _(pool):
            pool.memset(ident[:], 0.0).then_inc(ident0, 1)
            pool.wait_ge(ident0, 1)
            pool.affine_select(out=ident[:], in_=ident[:], compare_op=ALU.not_equal, fill=1.0, base=0,
                               pattern=[[-1, P]], channel_multiplier=1).then_inc(ident_ready, 1)


        @block.scalar
        def _(act):
            def split_weights(b, c):
                s = w_slot(c)
                act.wait_ge(raw_in[s], (32 if c == UF else 16) * (w_uses(b, c) + 1))
                if slot_taken(b, c):
                    act.wait_ge(projected, steps_before(b, c))
                act.activation(w_hi[s][:], raw[s][:], ACT.Copy).then_inc(w_hi_ready, 1)

            def normalize(b, r):
                n, s = tile_no(b, r), tile_slot(b, r)
                act.wait_ge(x_in[s], 16 * (tile_half(b, r) + 1))
                if x_tile_taken(b, r):
                    act.wait_ge(hT_psum, n - 1)
                act.activation(h[:, s, :], x[:, s, :], ACT.Square, accum_out=ssq[:, s:s + 1]).then_inc(squared, 1)
                act.wait_ge(squared, n + 1)
                act.activation(rstd[:, s:s + 1], ssq[:, s:s + 1], ACT.Sqrt, scale=1.0 / D, bias=eps[:]).then_inc(rms_ready, 1)

            def transposed(b, r):
                s = tile_slot(b, r)
                act.wait_ge(hT_psum, tile_no(b, r) + 1)
                if not (isinstance(b, int) and b == 0):
                    act.wait_ge(projected, NCH * tiles_before(b) - TILES + r + 1)
                act.activation(hT_hi[:, :, r * P:(r + 1) * P], ps_x[s][:], ACT.Copy).then_inc(hT_hi_ready, 1)

            def project(b, c, r):
                kind, half = CHUNKS[c]
                s = step_mod(b, c, r, 2)
                bank = ps_m[step_mod(b, c, r, 4)]
                act.wait_ge(projected, step_no(b, c, r) + 1)
                if kind in "qk":
                    n = 4 * tiles_before(b) + c * n_tiles(b) + r
                    act.activation(square[:], bank[:, 0:QKV_W], ACT.Square).then_inc(sq_ready, 1)
                    act.wait_ge(ss_ready, n + 1)
                    act.activation(rh[:], ssh[:], ACT.Sqrt, scale=1.0 / HD, bias=eps[:]).then_inc(rmsh_ready, 1)
                    act.wait_ge(gained, n + 1)
                    act.activation(split[s][:, :, 0, :], nat[:, s, :].rearrange("p (h d) -> p h d", d=HD),
                                   ACT.Copy).then_inc(hi_ready, 1)
                    return
                if step_taken(b, c, r):
                    act.wait_ge(stored[s], 32 * step_half(b, c, r))
                if kind == "v":
                    act.activation(nat[:, s, :], bank[:, 0:QKV_W], ACT.Copy)
                    act.activation(split[s][:, :, 0, :], bank[:, 0:QKV_W].rearrange("p (h d) -> p h d", d=HD),
                                   ACT.Copy).then_inc(hi_ready, 1)
                else:
                    act.activation(nat[:, s, 0:POOL], bank[:, 0:POOL], ACT.Copy).then_inc(u_copied, 1)

            act.wait_ge(consts_ready, 1)
            split_weights(0, 0)
            normalize(0, 0)
            for r in range(TILES0):
                if r + 1 < TILES0:
                    normalize(0, r + 1)
                transposed(0, r)

            def body(b, following):
                for what, blk, c, r in block_steps(b, following):
                    if what == "weights":
                        split_weights(blk, c)
                    elif what == "normalize":
                        normalize(blk, r)
                    elif what == "transpose":
                        transposed(blk, r)
                    else:
                        project(blk, c, r)
            blocks(act, body)
            act.wait_ge(f_chain, 2)
            act.activation(fa[:], fa[:], ACT.Exp, scale=-1.0).then_inc(log1p_f, 1)
            act.wait_ge(log1p_f, 1)
            act.activation(fa[:], fa[:], ACT.Ln, bias=1.0).then_inc(log1p_f, 1)

        @block.vector
        def _(dve):
            def split_weights(b, c):
                s = w_slot(c)
                dve.wait_ge(w_hi_ready, b * NCH + c + 1)
                dve.tensor_tensor(w_lo[s][:], raw[s][:], w_hi[s][:].bitcast(F32), ALU.subtract).then_inc(w_ready, 1)

            def normalize(b, r):
                n, s = tile_no(b, r), tile_slot(b, r)
                which = 1 if is_streams(b, r) else 0
                dve.wait_ge(rms_ready, n + 1)
                dve.reciprocal(rstd[:, s:s + 1], rstd[:, s:s + 1]).then_inc(rstd_ready, 1)
                dve.wait_ge(rstd_ready, n + 1)
                dve.scalar_tensor_tensor(h[:, s, :], x[:, s, :], rstd[:, s:s + 1], scale1[:, which, :],
                                         ALU.mult, ALU.mult).then_inc(scaled, 1)
                dve.wait_ge(scaled, n + 1)
                dve.tensor_tensor(h[:, s, :], h[:, s, :], shift1[:, which, :], ALU.add).then_inc(h_ready, 1)

            def transposed(b, r):
                s = tile_slot(b, r)
                dve.wait_ge(hT_hi_ready, tile_no(b, r) + 1)
                cols = slice(r * P, (r + 1) * P)
                dve.tensor_tensor(hT_lo[:, :, cols], ps_x[s][:], hT_hi[:, :, cols].bitcast(F32),
                                  ALU.subtract).then_inc(hT_ready, 1)

            def project(b, c, r):
                kind, half = CHUNKS[c]
                s = step_mod(b, c, r, 2)
                bank = ps_m[step_mod(b, c, r, 4)]
                if kind in "qk":
                    n = 4 * tiles_before(b) + c * n_tiles(b) + r
                    by_head = lambda ap: ap.rearrange("p (h d) -> p h d", d=HD)
                    dve.wait_ge(sq_ready, n + 1)
                    dve.reduce_sum(ssh[:], by_head(square[:]), AX_X).then_inc(ss_ready, 1)
                    dve.wait_ge(rmsh_ready, n + 1)
                    dve.reciprocal(rh[:], rh[:]).then_inc(rh_ready, 1)
                    dve.wait_ge(rh_ready, n + 1)
                    dve.tensor_tensor(by_head(square[:]), by_head(bank[:, 0:QKV_W]),
                                      rh[:].unsqueeze(2).broadcast_to([P, HG, HD]), ALU.mult
                                      ).then_inc(normed, 1)
                    dve.wait_ge(normed, n + 1)
                    if step_taken(b, c, r):
                        dve.wait_ge(stored[s], 32 * step_half(b, c, r))
                    g = gain[kind][:].unsqueeze(1).broadcast_to([P, HG, HD])
                    dve.tensor_tensor(by_head(nat[:, s, :]), by_head(square[:]), g, ALU.mult).then_inc(gained, 1)
                    dve.wait_ge(hi_ready, 6 * tiles_before(b) + c * n_tiles(b) + r + 1)
                    dve.tensor_tensor(split[s][:, :, 1, :], by_head(nat[:, s, :]),
                                      split[s][:, :, 0, :].bitcast(F32), ALU.subtract).then_inc(staged, 1)
                elif kind == "v":
                    dve.wait_ge(hi_ready, 6 * tiles_before(b) + c * n_tiles(b) + r + 1)
                    dve.tensor_tensor(split[s][:, :, 1, :], bank[:, 0:QKV_W].rearrange("p (h d) -> p h d", d=HD),
                                      split[s][:, :, 0, :].bitcast(F32), ALU.subtract).then_inc(staged, 1)
                else:
                    n = tile_no(b, r)
                    dve.wait_ge(u_copied, n + 1)
                    dve.tensor_tensor(fz[:, bass.ds(n, 1), :].rearrange("p o h -> p (o h)"), bank[:, POOL:UF_W], bf[:],
                                      ALU.add).then_inc(staged, 1)

            dve.memset(eps[:], EPS).then_inc(consts_ready, 1)
            dve.wait_ge(consts_in, 16 * CONSTS)
            dve.tensor_scalar(gain["q"][:], gain["q"][:], HD ** -0.5, None, ALU.mult).then_inc(consts_ready, 1)
            dve.wait_ge(consts_ready, 2)
            split_weights(0, 0)
            normalize(0, 0)
            for r in range(TILES0):
                if r + 1 < TILES0:
                    normalize(0, r + 1)
                transposed(0, r)

            def body(b, following):
                for what, blk, c, r in block_steps(b, following):
                    if what == "weights":
                        split_weights(blk, c)
                    elif what == "normalize":
                        normalize(blk, r)
                    elif what == "transpose":
                        transposed(blk, r)
                    else:
                        project(blk, c, r)
            blocks(dve, body)
            dve.wait_ge(staged, NCH * (QT + 1))
            dve.tensor_scalar(fa[:], fz[:], -1.0, None, ALU.mult).then_inc(f_chain, 1)
            dve.wait_ge(f_chain, 1)
            dve.tensor_tensor(fa[:], fz[:], fa[:], ALU.max).then_inc(f_chain, 1)
            dve.wait_ge(log1p_f, 2)
            dve.scalar_tensor_tensor(fz[:], fz[:], 0.0, fa[:], ALU.min, ALU.subtract).then_inc(f_chain, 1)

        @block.tensor
        def _(pe):
            def transpose(b, r):
                n, s = tile_no(b, r), tile_slot(b, r)
                pe.wait_ge(h_ready, n + 1)
                if x_tile_taken(b, r):
                    pe.wait_ge(hT_ready, n - 1)
                for k in range(KT):
                    last = pe.transpose(ps_x[s][:, k, :], h[:, s, k * P:(k + 1) * P], ident[:])
                last.then_inc(hT_psum, 1)

            def project(b, c, r):
                bank = ps_m[step_mod(b, c, r, 4)]
                s, w = w_slot(c), (UF_W if c == UF else QKV_W)
                if r == 0:
                    pe.wait_ge(w_ready, b * NCH + c + 1)
                if c == 0:
                    pe.wait_ge(hT_ready, tile_no(b, r) + 1)
                if not (isinstance(b, int) and b == 0 and c == 0 and r < 4):
                    pe.wait_ge(staged, step_no(b, c, r) - 3)
                rows = slice(r * P, (r + 1) * P)
                for k in range(KT):
                    for i, (a, wt) in enumerate(((hT_hi, w_hi), (hT_hi, w_lo), (hT_lo, w_hi))):
                        last = pe.matmul(bank[:, 0:w], a[:, k, rows], wt[s][:, k, :],
                                         start=(k == 0 and i == 0), stop=(k == KT - 1 and i == 2))
                last.then_inc(projected, 1)

            pe.wait_ge(ident_ready, 1)
            for r in range(TILES0):
                transpose(0, r)

            def body(b, following):
                for what, blk, c, r in block_steps(b, following):
                    if what == "transpose":
                        transpose(blk, r)
                    elif what == "project":
                        project(blk, c, r)
            blocks(pe, body)


def pooling(nc, t, sems):
    L = HIST + SEQ
    SL = HIST + NEW
    WINDOWS = (2, 4, 8, 16)
    KEYS = PAST + NEW
    GD = POOL // len(WINDOWS)
    with ExitStack() as ctx:
        sb = lambda name, shape, dt=F32: ctx.enter_context(nc.sbuf_tensor(name, shape, dt))
        u = sb("o_u", [P, QT + 1, POOL])
        hist = sb("o_hist", [STREAMS * HIST, POOL])
        z = sb("o_z", [P, 2, L])
        zs = sb("o_zs", [P, 2, STREAMS, SL])
        sums = sb("o_sums", [P, 2, L])
        sumss = sb("o_sumss", [P, 2, STREAMS, SL])
        mixed = sb("o_mixed", [P, 2, ROWS])
        y = sb("o_y", [P, 2, ROWS])
        count = sb("o_count", [P, 2, HIST])
        w = sb("o_w", [P, 2, P])
        pscale = sb("o_pscale", [P, 2])
        ident = sb("o_ident", [P, P])
        lf = sb("o_lf", [P, QT, HEADS])
        lc = sb("o_lc", [P, PAST // P, STREAMS, HEADS])
        nl = sb("o_nl", [HEADS, SEQ])
        nf = sb("o_nf", [HEADS, SEQ])
        nls = sb("o_nls", [STREAMS * HEADS, KEYS])
        nfs = sb("o_nfs", [STREAMS * HEADS, KEYS])
        zero = sb("o_zero", [P, SEQ])
        ps = [ctx.enter_context(nc.psum_tensor(f"o_ps{i}", [P, 4 * P], F32)) for i in range(8)]

        u_in, hist_in, w_in, lf_in, lc_in, new_in = (sems("o_" + n) for n in (
            "u_in", "hist_in", "w_in", "lf_in", "lc_in", "new_in"))
        zeroed, ident0, ready, turned, out_of_bank = (sems("o_" + n) for n in (
            "zeroed", "ident0", "ready", "turned", "out_of_bank"))
        chain, mixed_ready, product, y_ready, nf_ready, stored = (sems("o_" + n) for n in (
            "chain", "mixed_ready", "product", "y_ready", "nf_ready", "stored"))

        turns = [("u", half, g) for g in range(QT // 4) for half in range(2)]
        turns += [("s", 0, 0), ("s", 1, 0), ("hist", 0, 0), ("hist", 1, 0)]
        turns += [("lf", 0, g) for g in range(QT // 4)] + [("lc", 0, g) for g in range(PAST // P // 4)]
        n_z = turns.index(("lf", 0, 0))
        block = ctx.enter_context(nc.Block())

        @block.sync
        def _(sp):
            sp.dma_start(u[:], t["u"].rearrange("(n p) c -> p n c", p=P)).then_inc(u_in, 16)
            sp.dma_start(hist[:], t["cache_pool"][0].rearrange("b n c -> (b n) c")).then_inc(hist_in, 16)
            sp.dma_start(lf[:], t["logf_p"].rearrange("(n p) h -> p n h", p=P)).then_inc(lf_in, 16)
            sp.wait_ge(zeroed, 1)
            for g in range(len(WINDOWS)):
                part = slice(GD * (g % 2), GD * (g % 2) + GD)
                sp.dma_start(w[part, g // 2, part], t["w_pool"][0, g]).then_inc(w_in, 16)
            sp.dma_start(pscale[:], t["pool_scale"][0].rearrange("(a p) -> p a", p=P),
                         allow_slow_non_contiguous=True).then_inc(w_in, 16)
            sp.dma_start(t["pool_p"], t["u"][SEQ - HIST:SEQ, :]).then_inc(stored, 16)
            sp.dma_start(t["pool_s"], t["u"][SEQ:ROWS, :].rearrange("(b n) c -> b n c", n=NEW)[:, 1:, :]
                         ).then_inc(stored, 16)
            for half in range(2):
                for a, b in ((0, 1024), (1024, ROWS)):
                    sp.wait_ge(y_ready, 5 * half + (2 if a == 0 else 5))
                    sp.dma_start(t["mixT"][P * half:P * half + P, a:b], y[:, half, a:b]).then_inc(stored, 16)
            sp.wait_ge(nf_ready, 2)
            sp.dma_start(t["nF_p"], nf[:]).then_inc(stored, 16)
            sp.dma_start(t["nF_s"], nfs[:]).then_inc(stored, 16)
            sp.wait_ge(stored, 16 * 8)

        @block.gpsimd
        def _(pool):
            for tt in range(PAST // P):
                pool.dma_start(lc[:, tt, :, :], t["cache_logf"][0, :, tt * P:(tt + 1) * P, :].rearrange("b p h -> p b h")
                               ).then_inc(lc_in, 16)
            for b in range(STREAMS):
                pool.dma_start(nls[HEADS * b:HEADS * (b + 1), PAST:KEYS],
                               t["logf_s"][NEW * b:NEW * (b + 1), :].rearrange("n h -> h n"),
                               allow_slow_non_contiguous=True).then_inc(new_in, 16)
            pool.memset(w[:], 0.0).then_inc(zeroed, 1)
            pool.memset(zero[:], 0.0).then_inc(ready, 1)
            pool.memset(z[:, :, 0:HIST], 0.0).then_inc(ready, 1)
            for i in range(HIST):
                pool.memset(count[:, :, i:i + 1], float(i + 1)).then_inc(ready, 1)
            pool.memset(ident[:], 0.0).then_inc(ident0, 1)
            pool.wait_ge(ident0, 1)
            pool.affine_select(out=ident[:], in_=ident[:], compare_op=ALU.not_equal, fill=1.0, base=0,
                               pattern=[[-1, P]], channel_multiplier=1).then_inc(ident0, 1)

        @block.tensor
        def _(pe):
            pe.wait_ge(ident0, 2)
            for n, (kind, half, g) in enumerate(turns):
                bank = ps[n % 4]
                if n >= 4:
                    pe.wait_ge(out_of_bank, n - 3)
                cols = slice(P * half, P * half + P)
                if kind == "u":
                    if n == 0:
                        pe.wait_ge(u_in, 16)
                    for i in range(4):
                        tile = 4 * g + i
                        last = pe.transpose(bank[:, P * i:P * i + P], u[:, tile, cols], ident[:])
                elif kind == "s":
                    last = pe.transpose(bank[:, 0:P], u[:, QT, cols], ident[:])
                elif kind == "hist":
                    pe.wait_ge(hist_in, 16)
                    m = STREAMS * HIST
                    last = pe.transpose(bank[:, 0:m], hist[:, cols], ident[0:m, 0:m])
                elif kind == "lf":
                    pe.wait_ge(lf_in, 16)
                    for i in range(4):
                        last = pe.transpose(bank[0:HEADS, P * i:P * i + P], lf[:, 4 * g + i, :], ident[:])
                else:
                    pe.wait_ge(lc_in, 16 * (PAST // P))
                    for i in range(4):
                        last = pe.transpose(bank[0:STREAMS * HEADS, P * i:P * i + P],
                                            lc[:, 4 * g + i, :, :].rearrange("p b h -> p (b h)"), ident[:])
                last.then_inc(turned, 1)
            pe.wait_ge(w_in, 16 * 5)
            for half in range(2):
                pe.wait_ge(mixed_ready, half + 1)
                for i in range(5):
                    n = 5 * half + i
                    bank = ps[4 + n % 4]
                    if n >= 4:
                        pe.wait_ge(y_ready, n - 3)
                    a, b = 512 * i, min(512 * i + 512, ROWS)
                    pe.matmul(bank[:, 0:b - a], w[:, half, :], mixed[:, half, a:b], start=True, stop=True
                              ).then_inc(product, 1)

        @block.scalar
        def _(act):
            for half in range(2):
                for i in range(5):
                    n = 5 * half + i
                    act.wait_ge(product, n + 1)
                    a, b = 512 * i, min(512 * i + 512, ROWS)
                    act.activation(y[:, half, a:b], ps[4 + n % 4][:, 0:b - a], ACT.Copy,
                                   scale=pscale[:, half:half + 1]).then_inc(y_ready, 1)

        @block.vector
        def _(dve):
            done = 0

            def link(ins):
                nonlocal done
                ins.then_inc(chain, 1)
                done += 1
                dve.wait_ge(chain, done)

            for n, (kind, half, g) in enumerate(turns):
                bank = ps[n % 4]
                dve.wait_ge(turned, n + 1)
                if kind == "u":
                    dst, src = z[:, half, HIST + 4 * P * g:HIST + 4 * P * (g + 1)], bank[:]
                elif kind == "s":
                    dst, src = zs[:, half, :, HIST:], bank[:, 0:P].rearrange("p (b n) -> p b n", n=NEW)
                elif kind == "hist":
                    dst = zs[:, half, :, 0:HIST]
                    src = bank[:, 0:STREAMS * HIST].rearrange("p (b n) -> p b n", n=HIST)
                elif kind == "lf":
                    dst, src = nl[:, 4 * P * g:4 * P * (g + 1)], bank[0:HEADS, :]
                else:
                    dst, src = nls[:, 4 * P * g:4 * P * (g + 1)], bank[0:STREAMS * HEADS, :]
                sign = -1.0 if kind in ("lf", "lc") else 1.0
                dve.tensor_scalar(dst, src, sign, None, ALU.mult).then_inc(out_of_bank, 1)
            dve.wait_ge(out_of_bank, len(turns))
            dve.wait_ge(ready, 2 + HIST)
            dve.wait_ge(new_in, 16 * STREAMS)
            for g, win in enumerate(WINDOWS):
                part = slice(GD * (g % 2), GD * (g % 2) + GD)
                link(dve.tensor_scalar(count[part, g // 2, :], count[part, g // 2, :], float(win), None, ALU.min))
            link(dve.reciprocal(count[:], count[:]))
            for half in range(2):
                src, srcs = z[:, half, :], zs[:, half, :, :]
                for level, (step, g) in enumerate(((1, 0), (2, 1), (4, 2), (8, 3))):
                    if 2 * step > WINDOWS[2 * half + 1]:
                        break
                    lo = 2 * step - 1
                    dst, dsts = sums[:, level % 2, :], sumss[:, level % 2, :, :]
                    link(dve.tensor_tensor(dst[:, lo:L], src[:, lo:L], src[:, lo - step:L - step], ALU.add))
                    link(dve.tensor_tensor(dsts[:, :, lo:SL], srcs[:, :, lo:SL], srcs[:, :, lo - step:SL - step], ALU.add))
                    src, srcs = dst, dsts
                    if g // 2 == half:
                        part = slice(GD * (g % 2), GD * (g % 2) + GD)
                        inv = 1.0 / (2 * step)
                        out = mixed[part, half, :]
                        link(dve.scalar_tensor_tensor(out[:, HIST:SEQ], dst[part, 2 * HIST:L], inv,
                                                      z[part, half, 2 * HIST:L], ALU.mult, ALU.subtract))
                        link(dve.tensor_tensor(out[:, 0:HIST], dst[part, HIST:2 * HIST], count[part, half, :], ALU.mult))
                        link(dve.tensor_tensor(out[:, 0:HIST], out[:, 0:HIST], z[part, half, HIST:2 * HIST], ALU.subtract))
                        last = dve.scalar_tensor_tensor(out[:, SEQ:ROWS].rearrange("p (b n) -> p b n", n=NEW),
                                                        dsts[part, :, HIST:], inv, zs[part, half, :, HIST:],
                                                        ALU.mult, ALU.subtract)
                        if 2 * step == WINDOWS[2 * half + 1]:
                            last.then_inc(mixed_ready, 1)
                        else:
                            link(last)
            link(dve.tensor_scalar(nls[:, PAST:KEYS], nls[:, PAST:KEYS], -1.0, None, ALU.mult))
            dve.tensor_tensor_scan(nf[:], nl[:], zero[0:HEADS, :], 0.0, ALU.add, ALU.add).then_inc(nf_ready, 1)
            dve.tensor_tensor_scan(nfs[:], nls[:], zero[0:STREAMS * HEADS, 0:KEYS], 0.0, ALU.add, ALU.add
                                   ).then_inc(nf_ready, 1)


QB = 4
NB = QT // QB
WIDE = 1024


def wait_past(eng, sem, value):
    if not isinstance(value, int) or value > 0:
        eng.wait_ge(sem, value)


def pairs(eng, body):
    n = HEADS // 2
    body(0, 1)
    with eng.Fori(1, n - 1) as j:
        body(j, j + 1)
    body(n - 1, None)


def turns_before(b):
    return sum(QB * (i + 1) for i in range(b))


TURNS = turns_before(NB)


def chunks_of(i):
    w = (i + 1) * P
    return [(a, min(a + WIDE, w)) for a in range(0, w, WIDE)]


def chunks_before(i):
    return sum(len(chunks_of(n)) for n in range(i))


def attention_steps(j, following):
    order = [(j, e, b) for e in range(2) for b in range(NB)]
    after = order[1:] + ([(following, 0, 0)] if following is not None else [None])
    for n, (now, nxt) in enumerate(zip(order, after)):
        _, e, b = now
        keys = QB * (b + 1)
        last = n == len(order) - 1
        before = order[n - 1] if n else ((j - 1, 1, NB - 1) if not (isinstance(j, int) and j == 0) else None)
        yield "turn", now, 0
        yield "turn", now, 1
        made = 0
        for kt in range(keys):
            want = (kt + 1) * QB // keys
            if nxt is not None:
                while made < want:
                    yield "scores", nxt, nxt[2] * QB + made
                    made += 1
            yield "values", now, kt
            if kt + 2 < keys:
                yield "turn", now, kt + 2
            if kt == 0 and before is not None:
                yield "divisor", before, 0
            if kt == 1 and before is not None:
                yield "divide", before, 0
            if b == 2 and 3 <= kt < 11:
                head = (j, 1) if e == 0 else (following, 0)
                if head[0] is not None:
                    yield "prepare", head, kt - 3
        yield "sum", now, 0
    if following is None:
        yield "divisor", order[-1], 0
        yield "divide", order[-1], 0


def prompt_attention(nc, t, sems):
    with ExitStack() as ctx:
        sb = lambda name, shape, dt=F32: ctx.enter_context(nc.sbuf_tensor(name, shape, dt))
        qT = [sb(f"a_qT{e}", [P, SEQ], F32R) for e in range(2)]
        kT = [sb(f"a_kT{e}", [P, SEQ], F32R) for e in range(2)]
        kX = [sb(f"a_kX{e}", [P, SEQ], F32R) for e in range(2)]
        v = [sb(f"a_v{e}", [P, QT, P], F32R) for e in range(2)]
        rows_q = sb("a_rows_q", [P, QT, P])
        rows_k = sb("a_rows_k", [P, QT, P])
        bias = [sb(f"a_bias{e}", [P, SEQ]) for e in range(2)]
        dbias = [sb(f"a_dbias{e}", [P, QT, P]) for e in range(2)]
        probs = [sb(f"a_probs{i}", [P, QB, w]) for i, w in enumerate((1536, 2048))]
        pT_hi = [sb(f"a_pTh{i}", [P, QB * P], F32R) for i in range(4)]
        pT_lo = [sb(f"a_pTl{i}", [P, QB * P], F32R) for i in range(4)]
        ident = sb("a_ident", [P, P])
        mask = sb("a_mask", [P, P])
        nmax = sb("a_nmax", [P, 2, QB, 3])
        total = sb("a_total", [P, 2, QB])
        inv = sb("a_inv", [P, QB])
        inv2 = sb("a_inv2", [P, 2 * QB], F32R)
        invT = sb("a_invT", [2 * QB, P])
        pick = sb("a_pick", [2 * QB, QB, P])
        spread = sb("a_spread", [2 * QB, QB, P], F32R)
        ones = sb("a_ones", [2 * QB, P], F32R)
        onesf = sb("a_onesf", [2 * QB, P])
        rest = sb("a_rest", [HD, QB * P])
        both = sb("a_both", [HD, QB * P])
        out = sb("a_out", [HD, 2, QB * P])
        ps_s = [ctx.enter_context(nc.psum_tensor(f"a_pss{i}", [P, WIDE], F32)) for i in range(2)]
        ps_t = [ctx.enter_context(nc.psum_tensor(f"a_pst{i}", [P, QB * P], F32)) for i in range(2)]
        ps_o = ctx.enter_context(nc.psum_tensor("a_pso", [P, QB * P], F32))
        ps_x = ctx.enter_context(nc.psum_tensor("a_psx", [P, QB * P], F32))

        names = ("waited rows_in v_in0 v_in1 bias_in0 bias_in1 swapped0 swapped1 made consts ones_ready rows_turned prepared "
                 "dbias_ready scored chunk_out least exped turned hi_ready lo_ready valued inv_chain inv2_ready "
                 "inv_turned invT_ready spread_ready divisors rest_ready summed divided "
                 "stored0 stored1").split()
        S = {n: sems("a_" + n) for n in names}
        v_in, bias_in = [S["v_in0"], S["v_in1"]], [S["bias_in0"], S["bias_in1"]]
        swapped, stored = [S["swapped0"], S["swapped1"]], [S["stored0"], S["stored1"]]

        head = lambda who: 2 * who[0] + who[1]
        block_no = lambda who: NB * head(who) + who[2]

        def turn_no(who, kt):
            return TURNS * head(who) + turns_before(who[2]) + kt

        def chunk_no(who, i, c):
            return chunks_before(QT) * head(who) + chunks_before(i) + c

        def parts_of(i, a, b):
            return ([(a, min(b, i * P))] if a < i * P else []) + ([(i * P, b)] if b == (i + 1) * P else [])

        def n_parts(i):
            return sum(len(parts_of(i, a, b)) for a, b in chunks_of(i))

        def firsts_before(i):
            return sum(any(len(parts_of(n, a, b)) == 2 for a, b in chunks_of(n)) for n in range(i))

        def diag_of(who, kt):
            return max(0, kt - QB * who[2])

        block = ctx.enter_context(nc.Block())

        @block.sync
        def _(sp):
            def load(who):
                h, e = 2 * who[0] + who[1], who[1]
                wait_past(sp, S["rows_turned"], 8 * h)
                for to, name in ((rows_q, "q"), (rows_k, "k")):
                    src = t[name + "_split"][0:SEQ, bass.ds(h, 1), :].rearrange("(n p) o d -> p (n o) d", p=P)
                    sp.dma_start(to[:], src.bitcast(F32)).then_inc(S["rows_in"], 16)
                wait_past(sp, S["chunk_out"], chunks_before(QT) * (h - 1))
                sp.dma_start(bias[e][:], t["nF_p"][bass.ds(h, 1), :].broadcast_to([P, SEQ])).then_inc(bias_in[e], 16)
                wait_past(sp, S["valued"], TURNS * (h - 1))
                src = t["v_split"][0:SEQ, bass.ds(h, 1), :].rearrange("(n p) o d -> p (n o) d", p=P)
                sp.dma_start(v[e][:].bitcast(F32), src.bitcast(F32)).then_inc(v_in[e], 16)

            def swap(who):
                h, e = 2 * who[0] + who[1], who[1]
                sp.wait_ge(S["prepared"], 8 * h + 8)
                for a, b in ((0, HD), (HD, 0)):
                    sp.dma_start(kX[e][a:a + HD, :].bitcast(F32), kT[e][b:b + HD, :].bitcast(F32)).then_inc(swapped[e], 16)

            load((0, 0))
            swap((0, 0))

            def body(j, following):
                for what, who, n in attention_steps(j, following):
                    if what == "turn" and who[2] == 1 and n == 0:
                        if who[1] == 0:
                            load((j, 1))
                        elif following is not None:
                            load((following, 0))
                    elif what == "prepare" and n == 7:
                        swap(who)
                    elif what == "divide":
                        h, s = head(who), who[2] % 2
                        sp.wait_ge(S["divided"], block_no(who) + 1)
                        rows = bass.ds(POOL + HD * h, HD)
                        sp.dma_start(t["mixT"][rows, QB * P * who[2]:QB * P * (who[2] + 1)], out[:, s, :]
                                     ).then_inc(stored[s], 16)
            pairs(sp, body)
            for s in range(2):
                sp.wait_ge(stored[s], 16 * HEADS * NB // 2)

        @block.gpsimd
        def _(pool):
            pool.memset(ident[:], 0.0).then_inc(S["made"], 1)
            pool.memset(mask[:], 0.0).then_inc(S["made"], 1)
            pool.memset(pick[:], 1.0).then_inc(S["made"], 1)
            pool.memset(onesf[:], 1.0).then_inc(S["made"], 1)
            pool.wait_ge(S["made"], 4)
            pool.affine_select(out=ident[:], in_=ident[:], compare_op=ALU.not_equal, fill=1.0, base=0,
                               pattern=[[-1, P]], channel_multiplier=1).then_inc(S["consts"], 1)
            pool.affine_select(out=mask[:], in_=mask[:], compare_op=ALU.is_ge, fill=-1e30, base=0,
                               pattern=[[-1, P]], channel_multiplier=1).then_inc(S["consts"], 1)
            pool.affine_select(out=pick[:], in_=pick[:], compare_op=ALU.is_ge, fill=0.0, base=0,
                               pattern=[[-1, QB], [0, P]], channel_multiplier=1).then_inc(S["consts"], 1)
            pool.wait_ge(S["consts"], 3)
            for d in range(1, QB):
                pool.affine_select(out=pick[:], in_=pick[:], compare_op=ALU.not_equal, fill=0.0, base=-d,
                                   pattern=[[-1, QB], [0, P]], channel_multiplier=1).then_inc(S["consts"], 1)
                pool.wait_ge(S["consts"], 3 + d)
            for d in range(QB + 1, 2 * QB):
                pool.affine_select(out=pick[:], in_=pick[:], compare_op=ALU.not_equal, fill=0.0, base=-d,
                                   pattern=[[-1, QB], [0, P]], channel_multiplier=1).then_inc(S["consts"], 1)
                pool.wait_ge(S["consts"], 2 + d)

            def diagonal(who):
                h, e = 2 * who[0] + who[1], who[1]
                pool.wait_ge(bias_in[e], 16 * (who[0] + 1))
                wait_past(pool, S["chunk_out"], chunks_before(QT) * (h - 1))
                pool.tensor_tensor(dbias[e][:], bias[e][:].rearrange("p (n k) -> p n k", k=P),
                                   mask[:].unsqueeze(1).broadcast_to([P, QT, P]), ALU.add
                                   ).then_inc(S["dbias_ready"], 1)

            diagonal((0, 0))

            def body(j, following):
                for what, who, n in attention_steps(j, following):
                    if what == "prepare" and n == 0:
                        diagonal(who)
                    elif what == "divisor":
                        m = block_no(who)
                        pool.wait_ge(S["invT_ready"], m + 1)
                        wait_past(pool, S["divisors"], m)
                        pool.tensor_tensor(spread[:], invT[:].unsqueeze(1).broadcast_to([2 * QB, QB, P]), pick[:],
                                           ALU.mult).then_inc(S["spread_ready"], 1)
            pairs(pool, body)

        @block.scalar
        def _(act):
            def prepare(who, g):
                h, e = 2 * who[0] + who[1], who[1]
                act.wait_ge(S["rows_turned"], 8 * h + g + 1)
                to, cols = (qT if g < 4 else kT)[e], slice(512 * (g % 4), 512 * (g % 4) + 512)
                if g == 0:
                    wait_past(act, S["scored"], chunks_before(QT) * (h - 1))
                if g == 4:
                    wait_past(act, swapped[e], 32 * who[0])
                act.activation(to[:, cols], ps_x[:], ACT.Copy).then_inc(S["prepared"], 1)

            def scores(who, i):
                s, q = who[2] % 2, i % QB
                act.wait_ge(S["chunk_out"], chunk_no(who, i, len(chunks_of(i))))
                w = (i + 1) * P
                k = n_parts(i) - 1
                act.activation(probs[s][:, q, 0:w], probs[s][:, q, 0:w], ACT.Exp, scale=-1.0,
                               bias=nmax[:, s, q, k:k + 1], accum_out=total[:, s, q:q + 1]).then_inc(S["exped"], 1)

            def turn(who, kt):
                n = turn_no(who, kt)
                slot = (turns_before(who[2]) + kt) % 4
                act.wait_ge(S["turned"], n + 1)
                wait_past(act, S["valued"], n - 3)
                a = P * diag_of(who, kt)
                act.activation(pT_hi[slot][:, a:], ps_t[slot % 2][:, a:], ACT.Copy).then_inc(S["hi_ready"], 1)

            def body(j, following):
                for what, who, n in attention_steps(j, following):
                    if what == "prepare":
                        prepare(who, n)
                    elif what == "scores":
                        scores(who, n)
                    elif what == "turn":
                        turn(who, n)
                    elif what == "sum":
                        m = block_no(who)
                        act.wait_ge(S["valued"], TURNS * head(who) + turns_before(who[2] + 1))
                        wait_past(act, S["summed"], m)
                        act.activation(rest[:], ps_o[HD:P, :], ACT.Copy).then_inc(S["rest_ready"], 1)
                    elif what == "divisor":
                        m = block_no(who)
                        act.wait_ge(S["inv_turned"], m + 1)
                        wait_past(act, S["spread_ready"], m)
                        act.activation(invT[:], ps_x[0:2 * QB, 0:P], ACT.Copy).then_inc(S["invT_ready"], 1)
            for g in range(8):
                prepare((0, 0), g)
            for i in range(QB):
                scores((0, 0, 0), i)
            pairs(act, body)

        @block.vector
        def _(dve):
            def scores(who, i):
                e, s, q = who[1], who[2] % 2, i % QB
                if q == 0:
                    before = TURNS * head(who) + turns_before(who[2]) - QB * (who[2] if who[2] else NB)
                    wait_past(dve, S["turned"], before)
                    if who[2] == 0:
                        dve.wait_ge(bias_in[e], 16 * (who[0] + 1))
                        dve.wait_ge(S["dbias_ready"], head(who) + 1)
                k = 0
                for c, (a, b) in enumerate(chunks_of(i)):
                    n = chunk_no(who, i, c)
                    bank = ps_s[(chunks_before(i) + c) % 2]
                    dve.wait_ge(S["scored"], n + 1)
                    parts = parts_of(i, a, b)
                    for x0, x1 in parts:
                        dve.sem_inc(S["waited"], 1)
                        first = 3e38 if k == 0 else nmax[:, s, q, k - 1:k]
                        bs = dbias[e][:, i, :] if x0 == i * P else bias[e][:, x0:x1]
                        ins = dve.tensor_tensor_reduce(out=probs[s][:, q, x0:x1], in0=bank[:, x0 - a:x1 - a],
                                                       in1=bs, scale=-1.0, scalar=first, op0=ALU.add, op1=ALU.min,
                                                       accum_out=nmax[:, s, q, k:k + 1])
                        k += 1
                        if x1 == b:
                            ins.then_inc(S["chunk_out"], 1)
                            if b < (i + 1) * P:
                                dve.wait_ge(S["chunk_out"], n + 1)
                        else:
                            ins.then_inc(S["least"], 1)
                            dve.wait_ge(S["least"], firsts_before(QT) * head(who) + firsts_before(i) + 1)

            def turn(who, kt):
                n = turn_no(who, kt)
                slot = (turns_before(who[2]) + kt) % 4
                dve.wait_ge(S["hi_ready"], n + 1)
                a = P * diag_of(who, kt)
                dve.tensor_tensor(pT_lo[slot][:, a:], ps_t[slot % 2][:, a:], pT_hi[slot][:, a:].bitcast(F32),
                                  ALU.subtract).then_inc(S["lo_ready"], 1)

            def body(j, following):
                for what, who, n in attention_steps(j, following):
                    if what == "scores":
                        scores(who, n)
                    elif what == "turn":
                        turn(who, n)
                    elif what == "sum":
                        m, s = block_no(who), who[2] % 2
                        dve.wait_ge(S["rest_ready"], m + 1)
                        wait_past(dve, S["divided"], m)
                        dve.tensor_tensor(both[:], ps_o[0:HD, :], rest[:], ALU.add).then_inc(S["summed"], 1)
                        dve.wait_ge(S["exped"], QT * head(who) + QB * (who[2] + 1))
                        wait_past(dve, S["inv_turned"], m)
                        dve.reciprocal(inv[:], total[:, s, :]).then_inc(S["inv_chain"], 1)
                        dve.wait_ge(S["inv_chain"], 2 * m + 1)
                        dve.tensor_copy(inv2[:, 0:QB], inv[:]).then_inc(S["inv_chain"], 1)
                        dve.wait_ge(S["inv_chain"], 2 * m + 2)
                        dve.tensor_tensor(inv2[:, QB:], inv[:], inv2[:, 0:QB].bitcast(F32), ALU.subtract
                                          ).then_inc(S["inv2_ready"], 1)
                    elif what == "divide":
                        m, s = block_no(who), who[2] % 2
                        dve.wait_ge(S["divisors"], m + 1)
                        dve.wait_ge(S["summed"], m + 1)
                        wait_past(dve, stored[s], 16 * ((NB // 2) * head(who) + who[2] // 2))
                        dve.tensor_tensor(out[:, s, :], ps_x[0:HD, :], both[:], ALU.mult).then_inc(S["divided"], 1)
            dve.wait_ge(S["made"], 4)
            dve.tensor_copy(ones[:], onesf[:]).then_inc(S["ones_ready"], 1)
            for i in range(QB):
                scores((0, 0, 0), i)
            pairs(dve, body)

        @block.tensor
        def _(pe):
            def prepare(who, g):
                h, e = 2 * who[0] + who[1], who[1]
                if g == 0:
                    pe.wait_ge(S["rows_in"], 32 * (h + 1))
                    wait_past(pe, S["divided"], NB * (h - 1) + 2)
                wait_past(pe, S["prepared"], 8 * h + g)
                rows = (rows_q if g < 4 else rows_k)
                for i in range(4):
                    last = pe.transpose(ps_x[:, P * i:P * i + P], rows[:, 4 * (g % 4) + i, :], ident[:])
                last.then_inc(S["rows_turned"], 1)

            def scores(who, i):
                e = who[1]
                if i == 0:
                    pe.wait_ge(S["prepared"], 8 * head(who) + 8)
                    pe.wait_ge(swapped[e], 32 * (who[0] + 1))
                for c, (a, b) in enumerate(chunks_of(i)):
                    n = chunk_no(who, i, c)
                    bank = ps_s[(chunks_before(i) + c) % 2]
                    wait_past(pe, S["chunk_out"], n - 1)
                    for x0 in range(a, b, 512):
                        x1 = min(x0 + 512, b)
                        o = bank[:, x0 - a:x1 - a]
                        pe.matmul(o, qT[e][:, P * i:P * i + P], kT[e][:, x0:x1], start=True, stop=False)
                        last = pe.matmul(o, qT[e][:, P * i:P * i + P], kX[e][:, x0:x1], start=False, stop=True)
                    last.then_inc(S["scored"], 1)

            def turn(who, kt):
                n = turn_no(who, kt)
                slot = (turns_before(who[2]) + kt) % 4
                s, d = who[2] % 2, diag_of(who, kt)
                if kt == 0:
                    pe.wait_ge(S["exped"], QT * head(who) + QB * (who[2] + 1))
                wait_past(pe, S["lo_ready"], n - 1)
                for q in range(d, QB):
                    last = pe.transpose(ps_t[slot % 2][:, P * q:P * q + P], probs[s][:, q, P * kt:P * kt + P], ident[:])
                last.then_inc(S["turned"], 1)

            def values(who, kt):
                e, n = who[1], turn_no(who, kt)
                slot = (turns_before(who[2]) + kt) % 4
                if kt == 0:
                    wait_past(pe, S["summed"], block_no(who))
                    if who[2] == 0:
                        pe.wait_ge(v_in[e], 16 * (who[0] + 1))
                pe.wait_ge(S["lo_ready"], n + 1)
                a = P * diag_of(who, kt)
                final = kt == QB * (who[2] + 1) - 1
                pe.matmul(ps_o[:, a:], v[e][:, kt, :], pT_hi[slot][:, a:], start=(kt == 0), stop=False)
                pe.matmul(ps_o[:, a:], v[e][:, kt, :], pT_lo[slot][:, a:], start=False, stop=final).then_inc(S["valued"], 1)

            def body(j, following):
                for what, who, n in attention_steps(j, following):
                    if what == "prepare":
                        prepare(who, n)
                    elif what == "scores":
                        scores(who, n)
                    elif what == "turn":
                        turn(who, n)
                    elif what == "values":
                        values(who, n)
                    elif what == "divisor":
                        m = block_no(who)
                        pe.wait_ge(S["inv2_ready"], m + 1)
                        wait_past(pe, S["divided"], m)
                        if who[2] == 2:
                            h = head(who) + 1
                            if following is not None or who[1] == 0:
                                pe.wait_ge(S["prepared"], 8 * h + 8)
                        pe.transpose(ps_x[0:2 * QB, 0:P], inv2[:].bitcast(F32), ident[:]).then_inc(S["inv_turned"], 1)
                    elif what == "divide":
                        m = block_no(who)
                        pe.wait_ge(S["spread_ready"], m + 1)
                        pe.matmul(ps_x[:], ones[:], spread[:].rearrange("r q p -> r (q p)"), start=True, stop=True
                                  ).then_inc(S["divisors"], 1)
            pe.wait_ge(S["consts"], 2 * QB + 1)
            pe.wait_ge(S["ones_ready"], 1)
            for g in range(8):
                prepare((0, 0), g)
            for i in range(QB):
                scores((0, 0, 0), i)
            pairs(pe, body)


def stream_attention(nc, t, sems):
    PAIRS = HG // 2
    CT = PAST // P
    KEYS = PAST + NEW
    R = HG * NEW
    PR = 2 * NEW
    GROUPS = 2 * STREAMS
    with ExitStack() as ctx:
        sb = lambda name, shape, dt=F32: ctx.enter_context(nc.sbuf_tensor(name, shape, dt))
        qs = sb("s_q", [P, ATT])
        ks = sb("s_k", [P, ATT])
        qd = sb("s_qd", [P, HEADS // 2, STREAMS, PR])
        kn = sb("s_kn", [P, HEADS // 2, STREAMS * NEW])
        q_now = [sb(f"s_qn{i}", [P, PAIRS, PR]) for i in range(2)]
        k_now = [sb(f"s_kn{i}", [P, PAIRS, NEW]) for i in range(2)]
        k_rows = sb("s_krows", [P, 2, CT, QKV_W])
        v_rows = sb("s_vrows", [P, 2, CT, QKV_W])
        v_new = sb("s_vnew", [NEW, 2, QKV_W])
        kT = [sb(f"s_kT{i}", [P, PAIRS, PAST]) for i in range(2)]
        bias = sb("s_bias", [R, 2, KEYS])
        probs = sb("s_probs", [R, 2, KEYS])
        pT = sb("s_pT", [P, CT + 1, R])
        mask = sb("s_mask", [R, NEW])
        ident = sb("s_ident", [P, P])
        nmax = sb("s_nmax", [R, 2])
        total = sb("s_total", [R, 2])
        inv = sb("s_inv", [R, 2])
        o_sb = sb("s_o", [R, P])
        mix = sb("s_mix", [P, HEADS // 2, STREAMS, NEW])
        ps_k = [ctx.enter_context(nc.psum_tensor(f"s_psk{i}", [P, 4 * P], F32)) for i in range(2)]
        ps_s = ctx.enter_context(nc.psum_tensor("s_pss", [P, 3 * 512], F32))
        ps_p = [ctx.enter_context(nc.psum_tensor(f"s_psp{i}", [P, 4, P], F32)) for i in range(2)]
        ps_o = ctx.enter_context(nc.psum_tensor("s_pso", [P, 512], F32))

        names = ("waited new_in mask_in k_in0 k_in1 v_in0 v_in1 bias_in0 bias_in1 made consts qd_zero turned0 out0 "
                 "k_turned kT_act kT_dve now_ready scored bias_ready least exped inv_ready p_turned p_act p_dve "
                 "valued o_ready o_turned spread stored").split()
        S = {n: sems("s_" + n) for n in names}
        k_in, v_in, bias_in = ([S[f"{n}_in{i}"] for i in range(2)] for n in ("k", "v", "bias"))

        def groups(eng, body):
            body(0)
            with eng.Fori(1, STREAMS) as b:
                body(b)

        block = ctx.enter_context(nc.Block())

        @block.sync
        def _(sp):
            sp.dma_start(qs[:], t["q_nat"][SEQ:ROWS, :]).then_inc(S["new_in"], 16)
            sp.dma_start(ks[:], t["k_s"]).then_inc(S["new_in"], 16)
            sp.wait_ge(S["consts"], 2)
            for m in range(1, HG):
                sp.dma_start(mask[NEW * m:NEW * (m + 1), :], mask[0:NEW, :]).then_inc(S["mask_in"], 16)

            def body(b):
                for s in range(2):
                    g = 2 * b + s
                    cols = slice(s * QKV_W, (s + 1) * QKV_W)
                    wait_past(sp, S["k_turned"], 6 * (g - 1))
                    src = t["cache_k"][0, bass.ds(b, 1), :, s * HG:(s + 1) * HG, :]
                    sp.dma_start(k_rows[:, s], src.rearrange("o (n p) h d -> p (o n) (h d)", p=P)).then_inc(k_in[s], 16)
                    wait_past(sp, S["least"], g - 1)
                    for m in range(HG):
                        sp.dma_start(bias[NEW * m:NEW * (m + 1), s, :],
                                     t["nF_s"][bass.ds(b * HEADS + s * HG + m, 1), :].broadcast_to([NEW, KEYS])
                                     ).then_inc(bias_in[s], 16)
                    wait_past(sp, S["valued"], g - 1)
                    src = t["cache_v"][0, bass.ds(b, 1), :, s * HG:(s + 1) * HG, :]
                    sp.dma_start(v_rows[:, s], src.rearrange("o (n p) h d -> p (o n) (h d)", p=P)).then_inc(v_in[s], 16)
                    sp.dma_start(v_new[:, s], t["v_s"][bass.ds(b * NEW, NEW), cols]).then_inc(v_in[s], 16)
            groups(sp, body)
            sp.wait_ge(S["spread"], GROUPS)
            sp.dma_start(t["mixT"][POOL:D, SEQ:ROWS].rearrange("(a p) n -> p a n", p=P),
                         mix[:].rearrange("p a b n -> p a (b n)")).then_inc(S["stored"], 16)
            sp.wait_ge(S["stored"], 16)

        @block.gpsimd
        def _(pool):
            pool.memset(mask[:], 0.0).then_inc(S["made"], 1)
            pool.memset(ident[:], 0.0).then_inc(S["made"], 1)
            pool.memset(qd[:], 0.0).then_inc(S["qd_zero"], 1)
            pool.wait_ge(S["made"], 2)
            pool.affine_select(out=mask[0:NEW, :], in_=mask[0:NEW, :], compare_op=ALU.is_ge, fill=-1e30, base=0,
                               pattern=[[-1, NEW]], channel_multiplier=1).then_inc(S["consts"], 1)
            pool.affine_select(out=ident[:], in_=ident[:], compare_op=ALU.not_equal, fill=1.0, base=0,
                               pattern=[[-1, P]], channel_multiplier=1).then_inc(S["consts"], 1)
            pool.wait_ge(S["mask_in"], 16 * (HG - 1))

            def body(b):
                for s in range(2):
                    pool.wait_ge(bias_in[s], 16 * HG * (b + 1))
                    pool.tensor_tensor(bias[:, s, PAST:KEYS], bias[:, s, PAST:KEYS], mask[:], ALU.add
                                       ).then_inc(S["bias_ready"], 1)
            groups(pool, body)

        @block.scalar
        def _(act):
            def soft(g, s):
                act.wait_ge(S["least"], g + 1)
                act.activation(probs[:, s, :], probs[:, s, :], ACT.Exp, scale=-1.0, bias=nmax[:, s:s + 1],
                               accum_out=total[:, s:s + 1]).then_inc(S["exped"], 1)

            def keys(g, s):
                wait_past(act, S["scored"], g - 1)
                for u in range(0, 6, 2):
                    act.wait_ge(S["k_turned"], 6 * g + u + 1)
                    act.activation(kT[s][:, u // 2, 0:512], ps_k[0][:], ACT.Copy).then_inc(S["kT_act"], 1)

            def values(g, s):
                wait_past(act, S["valued"], g)
                act.wait_ge(S["p_turned"], 3 * g + 1)
                act.activation(pT[:, 0:4, :], ps_p[0][:, :, 0:R], ACT.Copy).then_inc(S["p_act"], 1)
                act.wait_ge(S["p_turned"], 3 * g + 3)
                act.activation(pT[0:NEW, CT, :], ps_p[0][0:NEW, 0, 0:R], ACT.Copy).then_inc(S["p_act"], 1)
                act.wait_ge(S["valued"], g + 1)
                act.wait_ge(S["inv_ready"], g + 1)
                wait_past(act, S["o_turned"], g)
                act.activation(o_sb[:], ps_o[0:R, 0:P], ACT.Copy, scale=inv[:, s:s + 1]).then_inc(S["o_ready"], 1)

            def body(b):
                for s in range(2):
                    g = 2 * b + s
                    keys(g, s)
                    soft(g, s)
                    if not (isinstance(b, int) and b == 0 and s == 0):
                        values(g - 1, 1 - s)
            groups(act, body)
            values(GROUPS - 1, 1)

        @block.vector
        def _(dve):
            def keys(g, b, s):
                wait_past(dve, S["scored"], g - 1)
                a = slice(PAIRS * s, PAIRS * (s + 1))
                dve.tensor_copy(q_now[s][:], qd[:, a, bass.ds(b, 1), :].rearrange("p a o r -> p a (o r)"))
                dve.tensor_copy(k_now[s][:], kn[:, a, bass.ds(b * NEW, NEW)]).then_inc(S["now_ready"], 1)
                for u in range(1, 6, 2):
                    dve.wait_ge(S["k_turned"], 6 * g + u + 1)
                    dve.tensor_copy(kT[s][:, u // 2, 512:1024], ps_k[1][:]).then_inc(S["kT_dve"], 1)

            def soft(g, s):
                dve.wait_ge(S["scored"], g + 1)
                dve.wait_ge(S["bias_ready"], g + 1)
                wait_past(dve, S["p_turned"], 3 * (g - 1))
                dve.sem_inc(S["waited"], 1)
                dve.tensor_tensor_reduce(out=probs[:, s, :], in0=ps_s[0:R, 0:KEYS], in1=bias[:, s, :], scale=-1.0,
                                         scalar=3e38, op0=ALU.add, op1=ALU.min, accum_out=nmax[:, s:s + 1]
                                         ).then_inc(S["least"], 1)

            def values(g, s):
                dve.wait_ge(S["exped"], g + 1)
                dve.reciprocal(inv[:, s:s + 1], total[:, s:s + 1]).then_inc(S["inv_ready"], 1)
                wait_past(dve, S["valued"], g)
                dve.wait_ge(S["p_turned"], 3 * g + 2)
                dve.tensor_copy(pT[:, 4:8, :], ps_p[1][:, :, 0:R]).then_inc(S["p_dve"], 1)

            def spread(g, b, s):
                dve.wait_ge(S["o_turned"], g + 1)
                src = ps_o[:, P:P + R].rearrange("p (a h q) -> p a h q", a=PAIRS, h=2)
                a = slice(PAIRS * s, PAIRS * (s + 1))
                for h in range(2):
                    part = slice(HD * h, HD * h + HD)
                    last = dve.tensor_copy(mix[part, a, bass.ds(b, 1), :].rearrange("p a o q -> p a (o q)"),
                                           src[part, :, h, :])
                last.then_inc(S["spread"], 1)

            for n in range(2):
                for half in range(2):
                    m = 2 * n + half
                    dve.wait_ge(S["turned0"], m + 1)
                    a = slice(PAIRS * half, PAIRS * (half + 1))
                    bank = ps_k[m % 2][:, 0:PAIRS * P].rearrange("p (a b r) -> p a b r", a=PAIRS, b=STREAMS)
                    if n == 0:
                        if half == 0:
                            dve.wait_ge(S["qd_zero"], 1)
                        for h in range(2):
                            part = slice(HD * h, HD * h + HD)
                            last = dve.tensor_copy(qd[part, a, :, NEW * h:NEW * (h + 1)], bank[part])
                    else:
                        last = dve.tensor_copy(kn[:, a, :].rearrange("p a (b r) -> p a b r", b=STREAMS), bank)
                    last.then_inc(S["out0"], 1)
            dve.wait_ge(S["out0"], 4)

            def body(b):
                for s in range(2):
                    g = 2 * b + s
                    keys(g, b, s)
                    if not (isinstance(b, int) and b == 0):
                        spread(g - 2, b - 1, s)
                    soft(g, s)
                    if not (isinstance(b, int) and b == 0 and s == 0):
                        values(g - 1, 1 - s)
            groups(dve, body)
            spread(GROUPS - 2, STREAMS - 1, 0)
            values(GROUPS - 1, 1)
            spread(GROUPS - 1, STREAMS - 1, 1)

        @block.tensor
        def _(pe):
            def keys(g, b, s):
                pe.wait_ge(k_in[s], 16 * (b + 1))
                for u in range(6):
                    a, part = u // 2, u % 2
                    wait_past(pe, S["kT_dve" if part else "kT_act"], 3 * g + a)
                    for i in range(4):
                        last = pe.transpose(ps_k[part][:, P * i:P * i + P],
                                            k_rows[:, s, 4 * part + i, P * a:P * a + P], ident[:])
                    last.then_inc(S["k_turned"], 1)

            def scores(g, s):
                pe.wait_ge(S["kT_act"], 3 * g + 3)
                pe.wait_ge(S["kT_dve"], 3 * g + 3)
                pe.wait_ge(S["now_ready"], g + 1)
                wait_past(pe, S["least"], g)
                for x0, x1 in ((0, 512), (512, 1024), (1024, KEYS)):
                    for a in range(PAIRS):
                        rhs = kT[s][:, a, x0:x1] if x1 <= PAST else k_now[s][:, a, :]
                        last = pe.matmul(ps_s[PR * a:PR * a + PR, x0:x1], q_now[s][:, a, :], rhs, start=True, stop=True,
                                         tile_position=(0, PR * a))
                last.then_inc(S["scored"], 1)

            def turn(g, s):
                pe.wait_ge(S["exped"], g + 1)
                wait_past(pe, S["p_act"], 2 * g)
                for i in range(4):
                    last = pe.transpose(ps_p[0][:, i, 0:R], probs[:, s, P * i:P * i + P], ident[0:R, 0:R])
                last.then_inc(S["p_turned"], 1)
                wait_past(pe, S["p_dve"], g)
                for i in range(4):
                    last = pe.transpose(ps_p[1][:, i, 0:R], probs[:, s, P * (4 + i):P * (5 + i)], ident[0:R, 0:R])
                last.then_inc(S["p_turned"], 1)
                pe.wait_ge(S["p_act"], 2 * g + 1)
                pe.transpose(ps_p[0][0:NEW, 0, 0:R], probs[:, s, PAST:KEYS], ident[0:R, 0:R]).then_inc(S["p_turned"], 1)

            def values(g, b, s):
                pe.wait_ge(v_in[s], 32 * (b + 1))
                pe.wait_ge(S["p_dve"], g + 1)
                pe.wait_ge(S["p_act"], 2 * g + 2)
                wait_past(pe, S["spread"], g)
                for i in range(CT + 1):
                    for a in range(PAIRS):
                        m = P if i < CT else NEW
                        rhs = v_rows[:, s, i, P * a:P * a + P] if i < CT else v_new[:, s, P * a:P * a + P]
                        last = pe.matmul(ps_o[PR * a:PR * a + PR, 0:P], pT[0:m, i, PR * a:PR * a + PR], rhs,
                                         start=(i == 0), stop=(i == CT), tile_position=(0, PR * a))
                last.then_inc(S["valued"], 1)

            def turn_out(g):
                pe.wait_ge(S["o_ready"], g + 1)
                pe.transpose(ps_o[:, P:P + R], o_sb[:], ident[0:R, 0:R]).then_inc(S["o_turned"], 1)

            pe.wait_ge(S["consts"], 2)
            pe.wait_ge(S["new_in"], 32)
            for n, rows in enumerate((qs, ks)):
                for half in range(2):
                    m = 2 * n + half
                    wait_past(pe, S["out0"], m - 1)
                    for a in range(PAIRS):
                        pair = PAIRS * half + a
                        last = pe.transpose(ps_k[m % 2][:, P * a:P * a + P], rows[:, P * pair:P * pair + P], ident[:])
                    last.then_inc(S["turned0"], 1)
            pe.wait_ge(S["out0"], 4)

            def body(b):
                for s in range(2):
                    g = 2 * b + s
                    keys(g, b, s)
                    if not (isinstance(b, int) and b == 0):
                        turn_out(g - 2)
                    scores(g, s)
                    if not (isinstance(b, int) and b == 0 and s == 0):
                        turn(g - 1, 1 - s)
                        values(g - 1, b if s == 1 else b - 1, 1 - s)
            groups(pe, body)
            turn_out(GROUPS - 2)
            turn(GROUPS - 1, 1)
            values(GROUPS - 1, STREAMS - 1, 1)
            turn_out(GROUPS - 1)


def out_projection(nc, t, sems):
    N = QT + 1
    HALVES, W = 2, 512
    with ExitStack() as ctx:
        sb = lambda name, shape, dt=F32: ctx.enter_context(nc.sbuf_tensor(name, shape, dt))
        w_raw = sb("out_wraw", [P, 2, D])
        w_hi = sb("out_whi", [P, KT, D], F32R)
        w_lo = sb("out_wlo", [P, KT, D], F32R)
        m = [sb(f"out_m{i}", [P, KT, P]) for i in range(2)]
        m_hi = [sb(f"out_mhi{i}", [P, KT, P], F32R) for i in range(2)]
        m_lo = [sb(f"out_mlo{i}", [P, KT, P], F32R) for i in range(2)]
        x = sb("out_x", [P, 2, D])
        x2 = sb("out_x2", [P, 2, D])
        h = sb("out_h", [P, 2, D])
        hT_hi = [sb(f"out_hThi{i}", [P, KT, P], F32R) for i in range(2)]
        hT_lo = [sb(f"out_hTlo{i}", [P, KT, P], F32R) for i in range(2)]
        gate = sb("out_gate", [P, 2, D])
        scale = sb("out_scale", [P, 2, D])
        shift = sb("out_shift", [P, 2, D])
        ssq = sb("out_ssq", [P, 2])
        rstd = sb("out_rstd", [P, 2])
        eps = sb("out_eps", [P, 1])
        ident = sb("out_ident", [P, P])
        ps_o = [ctx.enter_context(nc.psum_tensor(f"out_pso{i}", [P, D], F32)) for i in range(2)]
        ps_t = [ctx.enter_context(nc.psum_tensor(f"out_pst{i}", [P, KT, P], F32)) for i in range(2)]

        waited = sems("out_waited")
        consts_in, eps_ready = sems("out_consts_in"), sems("out_eps_ready")
        ident0, ident_ready = sems("out_ident0"), sems("out_ident_ready")
        w_in = [sems(f"out_w_in{i}") for i in range(2)]
        w_hi_ready, w_ready = sems("out_w_hi_ready"), sems("out_w_ready")
        m_in = [sems(f"out_m_in{i}") for i in range(2)]
        x_in = [sems(f"out_x_in{i}") for i in range(2)]
        m_hi_ready, m_ready, projected = sems("out_m_hi_ready"), sems("out_m_ready"), sems("out_projected")
        gated, x2_ready, squared, rms_ready = sems("out_gated"), sems("out_x2_ready"), sems("out_squared"), sems("out_rms_ready")
        rstd_ready, h_scaled, h_ready = sems("out_rstd_ready"), sems("out_h_scaled"), sems("out_h_ready")
        hT_psum, hT_hi_ready, hT_ready = sems("out_hT_psum"), sems("out_hT_hi_ready"), sems("out_hT_ready")
        x2_stored = [sems(f"out_x2_stored{i}") for i in range(2)]
        hT_stored = [sems(f"out_hT_stored{i}") for i in range(2)]

        def number(i, k):
            return 2 * i + k

        def uses(i, k):
            return i + k // 2

        def rows(i, k):
            n = number(i, k)
            return slice(n * P, (n + 1) * P) if isinstance(n, int) else bass.ds(n * P, P)

        def exists(i, k):
            return not isinstance(i, int) or number(i, k) < N

        def which(i, k):
            return 1 if isinstance(i, int) and number(i, k) == N - 1 else 0

        def over_tiles(eng, step):
            for k in range(2):
                step(0, k)
            with eng.Fori(1, N // 2 - 1) as i:
                for k in range(2):
                    step(i, k)
            for k in range(3):
                step(N // 2 - 1, k)

        block = ctx.enter_context(nc.Block())

        @block.sync
        def _(sp):
            def load_mix(i, k):
                wait_past(sp, m_ready, number(i, k) - 1)
                src = t["mixT"].rearrange("(k p) r -> p k r", p=P)
                sp.dma_start(m[k % 2][:], src[:, :, rows(i, k)]).then_inc(m_in[k % 2], 16)

            def load_x(i, k):
                wait_past(sp, x2_ready, number(i, k) - 1)
                if which(i, k):
                    src = t["x_sample"].rearrange("b n d -> (b n) d")
                else:
                    src = t["x_prompt"][0, rows(i, k), :]
                sp.dma_start(x[:, k % 2, :], src).then_inc(x_in[k % 2], 16)

            def store_x2(i, k):
                sp.wait_ge(x2_ready, number(i, k) + 1)
                sp.dma_start(t["x2"][rows(i, k), :], x2[:, k % 2, :]).then_inc(x2_stored[k % 2], 16)

            def store_hT(i, k):
                sp.wait_ge(hT_ready, number(i, k) + 1)
                sp.sem_inc(waited, 1)
                for name, part in (("h2T_hi", hT_hi), ("h2T_lo", hT_lo)):
                    dst = t[name].rearrange("(k p) r -> p k r", p=P).bitcast(F32)
                    sp.dma_start(dst[:, :, rows(i, k)], part[k % 2][:].bitcast(F32)).then_inc(hT_stored[k % 2], 16)

            load_mix(0, 0)
            for k in range(2):
                sp.dma_start(w_raw[:, k, :], t["w_out"][0, k * P:(k + 1) * P, :]).then_inc(w_in[k], 16)
            load_x(0, 0)
            load_mix(0, 1)
            for k in range(2, KT):
                sp.wait_ge(w_ready, k - 1)
                sp.dma_start(w_raw[:, k % 2, :], t["w_out"][0, k * P:(k + 1) * P, :]).then_inc(w_in[k % 2], 16)
            for to, col in ((gate, 2 * D), (scale, 4 * D), (shift, 3 * D)):
                sp.dma_start(to[:, 0, :], t["mod"][0:1, col:col + D].broadcast_to([P, D])).then_inc(consts_in, 16)
                for s in range(STREAMS):
                    sp.dma_start(to[NEW * s:NEW * (s + 1), 1, :],
                                 t["mod"][1 + s:2 + s, col:col + D].broadcast_to([NEW, D])).then_inc(consts_in, 16)
            load_x(0, 1)
            store_x2(0, 0)

            def step(i, k):
                if exists(i, k + 2):
                    load_mix(i, k + 2)
                    load_x(i, k + 2)
                if exists(i, k + 1):
                    store_x2(i, k + 1)
                store_hT(i, k)
            over_tiles(sp, step)
            for s in range(2):
                tiles = (N + 1 - s) // 2
                sp.wait_ge(x2_stored[s], 16 * tiles)
                sp.wait_ge(hT_stored[s], 32 * tiles)

        @block.gpsimd
        def _(pool):
            pool.memset(ident[:], 0.0).then_inc(ident0, 1)
            pool.wait_ge(ident0, 1)
            pool.affine_select(out=ident[:], in_=ident[:], compare_op=ALU.not_equal, fill=1.0, base=0,
                               pattern=[[-1, P]], channel_multiplier=1).then_inc(ident_ready, 1)

        @block.scalar
        def _(act):
            def split_mix(i, k):
                act.wait_ge(m_in[k % 2], 16 * (uses(i, k) + 1))
                wait_past(act, projected, number(i, k) - 1)
                act.activation(m_hi[k % 2][:], m[k % 2][:], ACT.Copy).then_inc(m_hi_ready, 1)

            def norm(i, k):
                n, s = number(i, k), k % 2
                act.wait_ge(x2_ready, n + 1)
                wait_past(act, hT_psum, n - 1)
                act.activation(h[:, s, :], x2[:, s, :], ACT.Square, accum_out=ssq[:, s:s + 1]).then_inc(squared, 1)
                act.wait_ge(squared, n + 1)
                act.activation(rstd[:, s:s + 1], ssq[:, s:s + 1], ACT.Sqrt, scale=1.0 / D, bias=eps[:]).then_inc(rms_ready, 1)

            def transposed(i, k):
                n, s = number(i, k), k % 2
                act.wait_ge(hT_psum, n + 1)
                if not (isinstance(i, int) and n < 2):
                    act.wait_ge(hT_stored[s], 32 * uses(i, k))
                act.activation(hT_hi[s][:], ps_t[s][:], ACT.Copy).then_inc(hT_hi_ready, 1)

            split_mix(0, 0)
            for k in range(KT):
                act.wait_ge(w_in[k % 2], 16 * (k // 2 + 1))
                act.activation(w_hi[:, k, :], w_raw[:, k % 2, :], ACT.Copy).then_inc(w_hi_ready, 1)
            split_mix(0, 1)
            act.wait_ge(eps_ready, 1)
            norm(0, 0)

            def step(i, k):
                if exists(i, k + 2):
                    split_mix(i, k + 2)
                if exists(i, k + 1):
                    norm(i, k + 1)
                transposed(i, k)
            over_tiles(act, step)

        @block.vector
        def _(dve):
            def split_mix(i, k):
                s = k % 2
                dve.wait_ge(m_hi_ready, number(i, k) + 1)
                dve.tensor_tensor(m_lo[s][:], m[s][:], m_hi[s][:].bitcast(F32), ALU.subtract).then_inc(m_ready, 1)

            def residual(i, k):
                n, s = number(i, k), k % 2
                dve.wait_ge(projected, n + 1)
                if not (isinstance(i, int) and n < 2):
                    dve.wait_ge(x2_stored[s], 16 * uses(i, k))
                    dve.wait_ge(squared, n - 1)
                dve.tensor_tensor(x2[:, s, :], ps_o[s][:], gate[:, which(i, k), :], ALU.mult).then_inc(gated, 1)
                dve.wait_ge(gated, n + 1)
                dve.wait_ge(x_in[s], 16 * (uses(i, k) + 1))
                dve.tensor_tensor(x2[:, s, :], x2[:, s, :], x[:, s, :], ALU.add).then_inc(x2_ready, 1)

            def norm(i, k):
                n, s = number(i, k), k % 2
                dve.wait_ge(rms_ready, n + 1)
                dve.reciprocal(rstd[:, s:s + 1], rstd[:, s:s + 1]).then_inc(rstd_ready, 1)
                dve.wait_ge(rstd_ready, n + 1)
                dve.scalar_tensor_tensor(h[:, s, :], x2[:, s, :], rstd[:, s:s + 1], scale[:, which(i, k), :],
                                         ALU.mult, ALU.mult).then_inc(h_scaled, 1)
                dve.wait_ge(h_scaled, n + 1)
                dve.tensor_tensor(h[:, s, :], h[:, s, :], shift[:, which(i, k), :], ALU.add).then_inc(h_ready, 1)

            def transposed(i, k):
                s = k % 2
                dve.wait_ge(hT_hi_ready, number(i, k) + 1)
                dve.tensor_tensor(hT_lo[s][:], ps_t[s][:], hT_hi[s][:].bitcast(F32), ALU.subtract).then_inc(hT_ready, 1)

            dve.memset(eps[:], EPS).then_inc(eps_ready, 1)
            split_mix(0, 0)
            for k in range(KT):
                dve.wait_ge(w_hi_ready, k + 1)
                dve.tensor_tensor(w_lo[:, k, :], w_raw[:, k % 2, :], w_hi[:, k, :].bitcast(F32),
                                  ALU.subtract).then_inc(w_ready, 1)
            split_mix(0, 1)
            dve.wait_ge(consts_in, 16 * 3 * (1 + STREAMS))
            residual(0, 0)
            norm(0, 0)

            def step(i, k):
                if exists(i, k + 2):
                    split_mix(i, k + 2)
                if exists(i, k + 1):
                    residual(i, k + 1)
                    norm(i, k + 1)
                transposed(i, k)
            over_tiles(dve, step)

        @block.tensor
        def _(pe):
            def project(i, k):
                n, s = number(i, k), k % 2
                pe.wait_ge(m_ready, n + 1)
                wait_past(pe, gated, n - 1)
                for c in range(KT):
                    if isinstance(i, int) and n == 0:
                        pe.wait_ge(w_ready, c + 1)
                    for j, (a, w) in enumerate(((m_hi, w_hi), (m_hi, w_lo), (m_lo, w_hi))):
                        for half in range(HALVES):
                            cols = slice(half * W, (half + 1) * W)
                            last = pe.matmul(ps_o[s][:, cols], a[s][:, c, :], w[:, c, cols],
                                             start=(c == 0 and j == 0), stop=(c == KT - 1 and j == 2))
                last.then_inc(projected, 1)

            def transpose(i, k):
                n, s = number(i, k), k % 2
                pe.wait_ge(h_ready, n + 1)
                wait_past(pe, hT_ready, n - 1)
                for c in range(KT):
                    last = pe.transpose(ps_t[s][:, c, :], h[:, s, c * P:(c + 1) * P], ident[:])
                last.then_inc(hT_psum, 1)

            pe.wait_ge(ident_ready, 1)
            project(0, 0)

            def step(i, k):
                if exists(i, k + 1):
                    project(i, k + 1)
                transpose(i, k)
            over_tiles(pe, step)


def channel_mixing(nc, t, sems):
    NB, RB = 4, ROWS // 4
    HW = RB // 2
    G = 2
    STEPS = FF // P // G
    PIECES = [(0, P), (P, P), (2 * P, P), (3 * P, RB - 4 * P), (RB - P, P)]
    NPC = len(PIECES)
    USES = STEPS * KT + NPC
    CREDIT = KT + 1
    with ExitStack() as ctx:
        sb = lambda name, shape, dt=F32: ctx.enter_context(nc.sbuf_tensor(name, shape, dt))
        hT = [sb(f"c_hT{i}", [P, KT, RB], F32R) for i in range(2)]
        up_raw = sb("c_up_raw", [P, KT, G * P])
        up_hi = [sb(f"c_up_hi{i}", [P, KT, G * P], F32R) for i in range(2)]
        up_lo = [sb(f"c_up_lo{i}", [P, KT, G * P], F32R) for i in range(2)]
        dn_raw = sb("c_dn_raw", [P, G, D])
        dn_hi = [sb(f"c_dn_hi{i}", [P, G, D], F32R) for i in range(2)]
        dn_lo = [sb(f"c_dn_lo{i}", [P, G, D], F32R) for i in range(2)]
        r = sb("c_relu", [P, G, RB])
        a_hi = [sb(f"c_a_hi{i}", [P, G, RB], F32R) for i in range(2)]
        a_lo = [sb(f"c_a_lo{i}", [P, G, RB], F32R) for i in range(2)]
        ffT = sb("c_ffT", [P, KT, RB])
        x2 = sb("c_x2", [P, NPC, D])
        gated = sb("c_gated", [P, 2, D])
        gate = sb("c_gate", [P, 2, D])
        ident = sb("c_ident", [P, P])
        ps_u = [ctx.enter_context(nc.psum_tensor(f"c_psu{i}", [P, 2, 512], F32)) for i in range(G)]
        ps_d = [ctx.enter_context(nc.psum_tensor(f"c_psd{i}", [P, 2, 512], F32)) for i in range(2)]

        gates_in, ident0, ident_ready = sems("c_gates_in"), sems("c_ident0"), sems("c_ident_ready")
        hT_in, waited = sems("c_hT_in"), sems("c_waited")
        up_in, dn_in = sems("c_up_in"), sems("c_dn_in")
        up_hi_ready, up_ready = sems("c_up_hi_ready"), sems("c_up_ready")
        dn_hi_ready, dn_ready = sems("c_dn_hi_ready"), sems("c_dn_ready")
        up_done = sems("c_up_done")
        relu_done, squared, a_hi_ready = sems("c_relu_done"), sems("c_squared"), sems("c_a_hi_ready")
        a_ready = sems("c_a_ready")
        down_done = sems("c_down_done")
        dn_free = sems("c_dn_free")
        zeroed = sems("c_zeroed")
        ff_transposed, y_ready = sems("c_ff_transposed"), sems("c_y_ready")
        x2_in, y_stored = sems("c_x2_in"), sems("c_y_stored")

        def over_blocks(eng, body):
            with eng.Fori(0, NB - 1) as b:
                body(b, False)
            body(NB - 1, True)

        def over_steps(eng, b, unit):
            with eng.Fori(0, STEPS // 2 - 1) as i:
                for p in range(2):
                    unit(b * STEPS + 2 * i + p, p)

        block = ctx.enter_context(nc.Block())

        @block.sync
        def _(sp):
            def load_hT(b):
                for part, name in ((0, "h2T_hi"), (1, "h2T_lo")):
                    src = t[name].rearrange("(k p) r -> p k r", p=P).bitcast(F32)
                    for k in (slice(0, KT // 2), slice(KT // 2, KT)):
                        cols = slice(b * RB, (b + 1) * RB) if isinstance(b, int) else bass.ds(b * RB, RB)
                        sp.dma_start(hT[part][:, k, :].bitcast(F32), src[:, k, cols]).then_inc(hT_in, 16)

            def load_up(S, s):
                wait_past(sp, up_ready, S)
                cols = slice(s * G * P, (s + 1) * G * P) if isinstance(s, int) else bass.ds(s * G * P, G * P)
                sp.dma_start(up_raw[:], t["w_up"][0].rearrange("(k p) f -> p k f", p=P)[:, :, cols]
                             ).then_inc(up_in, 16)

            def load_down(S, s):
                wait_past(sp, dn_ready, S)
                rws = slice(s * G * P, (s + 1) * G * P) if isinstance(s, int) else bass.ds(s * G * P, G * P)
                sp.dma_start(dn_raw[:], t["w_down"][0][rws, :].rearrange("(g p) d -> p g d", p=P)
                             ).then_inc(dn_in, 16)

            load_up(0, 0)
            load_hT(0)
            sp.dma_start(gate[:, 0, :], t["mod"][0:1, 5 * D:].broadcast_to([P, D])).then_inc(gates_in, 16)
            for s in range(STREAMS):
                sp.dma_start(gate[NEW * s:NEW * (s + 1), 1, :],
                             t["mod"][1 + s:2 + s, 5 * D:].broadcast_to([NEW, D])).then_inc(gates_in, 16)
            load_up(1, 1)
            load_down(0, 0)

            def body(b, last):
                with sp.Fori(0, STEPS // 2 - 1) as i:
                    for p in range(2):
                        s = 2 * i + p
                        load_up(b * STEPS + s + 2, s + 2)
                        load_down(b * STEPS + s + 1, s + 1)
                first = (b + 1) * STEPS
                if not last:
                    load_up(first, 0)
                load_down(first - 1, STEPS - 1)
                if not last:
                    sp.wait_ge(up_done, G * first)
                    load_hT(b + 1)
                    load_up(first + 1, 1)
                    load_down(first, 0)
            over_blocks(sp, body)

        @block.gpsimd
        def _(pool):
            def load_x2(b):
                for q, (off, w) in enumerate(PIECES):
                    pool.dma_start(x2[0:w, q, :], t["x2"][bass.ds(b * RB + off, w), :]).then_inc(x2_in, 16)

            pool.memset(ident[:], 0.0).then_inc(ident0, 1)
            pool.wait_ge(ident0, 1)
            pool.affine_select(out=ident[:], in_=ident[:], compare_op=ALU.not_equal, fill=1.0, base=0,
                               pattern=[[-1, P]], channel_multiplier=1).then_inc(ident_ready, 1)
            pool.memset(ffT[:], 0.0).then_inc(zeroed, 1)
            load_x2(0)

            def body(b, last):
                pool.wait_ge(x2_in, 16 * NPC * (b + 1))
                for q, (off, w) in enumerate(PIECES):
                    pool.wait_ge(dn_free, USES * b + STEPS * KT + q + 1 + CREDIT)
                    pool.tensor_tensor(x2[0:w, q, :], x2[0:w, q, :], gated[0:w, q % 2, :], ALU.add).then_inc(y_ready, 1)
                    pool.wait_ge(y_ready, NPC * b + q + 1)
                    if last and q == NPC - 1:
                        dst = t["y_sample"].rearrange("b n d -> (b n) d")
                    else:
                        dst = t["y_prompt"][0, bass.ds(b * RB + off, w), :]
                    pool.dma_start(dst, x2[0:w, q, :]).then_inc(y_stored, 16)
                if not last:
                    pool.wait_ge(ff_transposed, NPC * (b + 1))
                    pool.sem_inc(waited, 1)
                    pool.memset(ffT[:], 0.0).then_inc(zeroed, 1)
                pool.wait_ge(y_stored, 16 * NPC * (b + 1))
                if not last:
                    load_x2(b + 1)
            over_blocks(pool, body)

        @block.scalar
        def _(act):
            def split_up(S, p):
                act.wait_ge(up_in, 16 * (S + 1))
                wait_past(act, up_done, G * (S - 1))
                act.activation(up_hi[p][:], up_raw[:], ACT.Copy).then_inc(up_hi_ready, 1)

            def split_down(S, p):
                act.wait_ge(dn_in, 16 * (S + 1))
                wait_past(act, down_done, KT * (S - 1))
                act.activation(dn_hi[p][:], dn_raw[:], ACT.Copy).then_inc(dn_hi_ready, 1)

            def relu_squared(S, p, g):
                n = G * S + g
                act.wait_ge(up_done, n + 1)
                if not isinstance(S, int) or S > 0:
                    act.wait_ge(a_ready, n - G + 1)
                act.activation(r[:, g, :].rearrange("p (h n) -> p h n", h=2), ps_u[g][:, :, 0:HW],
                               ACT.Relu).then_inc(relu_done, 1)
                act.wait_ge(relu_done, n + 1)
                act.activation(r[:, g, :], r[:, g, :], ACT.Square).then_inc(squared, 1)
                act.wait_ge(squared, n + 1)
                wait_past(act, down_done, KT * (S - 1))
                act.activation(a_hi[p][:, g, :], r[:, g, :], ACT.Copy).then_inc(a_hi_ready, 1)

            split_up(0, 0)
            split_up(1, 1)
            split_down(0, 0)
            for g in range(G):
                relu_squared(0, 0, g)

            def unit(S, p):
                split_up(S + 2, p)
                relu_squared(S + 1, 1 - p, 0)
                split_down(S + 1, 1 - p)
                relu_squared(S + 1, 1 - p, 1)

            def body(b, last):
                over_steps(act, b, unit)
                S = (b + 1) * STEPS - 2
                if not last:
                    split_up(S + 2, 0)
                relu_squared(S + 1, 1, 0)
                split_down(S + 1, 1)
                relu_squared(S + 1, 1, 1)
                if not last:
                    split_up(S + 3, 1)
                    split_down(S + 2, 0)
                    for g in range(G):
                        relu_squared(S + 2, 0, g)
            over_blocks(act, body)

        @block.vector
        def _(dve):
            def split_up(S, p):
                dve.wait_ge(up_hi_ready, S + 1)
                dve.tensor_tensor(up_lo[p][:], up_raw[:], up_hi[p][:].bitcast(F32), ALU.subtract).then_inc(up_ready, 1)

            def split_down(S, p):
                dve.wait_ge(dn_hi_ready, S + 1)
                dve.tensor_tensor(dn_lo[p][:], dn_raw[:], dn_hi[p][:].bitcast(F32), ALU.subtract).then_inc(dn_ready, 1)

            def rest(S, p, g):
                dve.wait_ge(a_hi_ready, G * S + g + 1)
                dve.tensor_tensor(a_lo[p][:, g, :], r[:, g, :], a_hi[p][:, g, :].bitcast(F32),
                                  ALU.subtract).then_inc(a_ready, 1)

            def accumulate(b, S):
                for d in range(KT):
                    use = S * KT + b * NPC + d
                    dve.wait_ge(down_done, S * KT + d + 1)
                    if d == 0:
                        dve.wait_ge(zeroed, b + 1)
                    dve.wait_ge(dn_free, use - KT + 1 + CREDIT)
                    out = ffT[:, d, :].rearrange("p (h n) -> p h n", h=2)
                    dve.tensor_tensor(out, out, ps_d[d % 2][:, :, 0:HW], ALU.add).then_inc(dn_free, 1)

            dve.memset(gated[:], 0.0).then_inc(dn_free, CREDIT)
            split_up(0, 0)
            split_up(1, 1)
            split_down(0, 0)
            for g in range(G):
                rest(0, 0, g)
            dve.wait_ge(gates_in, 16 * (1 + STREAMS))

            def body(b, last):
                def unit(S, p):
                    split_up(S + 2, p)
                    rest(S + 1, 1 - p, 0)
                    split_down(S + 1, 1 - p)
                    rest(S + 1, 1 - p, 1)
                    accumulate(b, S)
                over_steps(dve, b, unit)
                S = (b + 1) * STEPS - 2
                if not last:
                    split_up(S + 2, 0)
                rest(S + 1, 1, 0)
                split_down(S + 1, 1)
                rest(S + 1, 1, 1)
                accumulate(b, S)
                if not last:
                    split_up(S + 3, 1)
                accumulate(b, S + 1)
                if not last:
                    split_down(S + 2, 0)
                for q, (off, w) in enumerate(PIECES):
                    dve.wait_ge(ff_transposed, NPC * b + q + 1)
                    if q == 0:
                        dve.wait_ge(x2_in, 16 * NPC * (b + 1))
                    elif q >= 2:
                        dve.wait_ge(y_ready, NPC * b + q - 1)
                    whose = 1 if last and q == NPC - 1 else 0
                    dve.tensor_tensor(gated[0:w, q % 2, :], ps_d[q % 2][0:w].rearrange("p a n -> p (a n)"),
                                      gate[0:w, whose, :], ALU.mult).then_inc(dn_free, 1)
                if not last:
                    for g in range(G):
                        rest(S + 2, 0, g)
            over_blocks(dve, body)

        @block.tensor
        def _(pe):
            def up(S, p, block_start=None):
                pe.wait_ge(up_ready, S + 1)
                if block_start is not None:
                    pe.wait_ge(hT_in, 16 * 4 * (block_start + 1))
                for g in range(G):
                    if not isinstance(S, int) or S > 0:
                        pe.wait_ge(relu_done, G * (S - 1) + g + 1)
                    f = slice(g * P, (g + 1) * P)
                    for k in range(KT):
                        for j, (w, x) in enumerate(((up_hi, hT[0]), (up_hi, hT[1]), (up_lo, hT[0]))):
                            for half in range(2):
                                last = pe.matmul(ps_u[g][:, half, 0:HW], w[p][:, k, f],
                                                 x[:, k, half * HW:(half + 1) * HW],
                                                 start=(k == 0 and j == 0), stop=(k == KT - 1 and j == 2))
                    last.then_inc(up_done, 1)

            def down(b, S, p):
                pe.wait_ge(dn_ready, S + 1)
                pe.wait_ge(a_ready, G * (S + 1))
                for d in range(KT):
                    use = S * KT + b * NPC + d
                    pe.wait_ge(dn_free, use - (0 if d == 0 else 1) + CREDIT)
                    cols = slice(d * P, (d + 1) * P)
                    for g in range(G):
                        for j, (w, a) in enumerate(((dn_hi, a_hi), (dn_hi, a_lo), (dn_lo, a_hi))):
                            for half in range(2):
                                last = pe.matmul(ps_d[d % 2][:, half, 0:HW], w[p][:, g, cols],
                                                 a[p][:, g, half * HW:(half + 1) * HW],
                                                 start=(g == 0 and j == 0), stop=(g == G - 1 and j == 2))
                    last.then_inc(down_done, 1)

            def transpose_back(b):
                for q, (off, w) in enumerate(PIECES):
                    use = (b + 1) * STEPS * KT + b * NPC + q
                    pe.wait_ge(dn_free, use - (0 if q == 0 else 1) + CREDIT)
                    for d in range(KT):
                        last = pe.transpose(ps_d[q % 2][0:w, d // 4, d % 4 * P:(d % 4 + 1) * P],
                                            ffT[:, d, off:off + w], ident[:])
                    last.then_inc(ff_transposed, 1)

            pe.wait_ge(ident_ready, 1)
            up(0, 0, 0)

            def body(b, last):
                def unit(S, p):
                    up(S + 1, 1 - p)
                    down(b, S, p)
                over_steps(pe, b, unit)
                S = (b + 1) * STEPS - 2
                up(S + 1, 1)
                down(b, S, 0)
                down(b, S + 1, 1)
                transpose_back(b)
                if not last:
                    up(S + 2, 0, b + 1)
            over_blocks(pe, body)


def build(nc, ins, outs):
    t = dict(ins)
    t.update(outs)
    inner = lambda name, shape, dt=F32: nc.dram_tensor(name, shape, dt).ap()
    t["mod"] = inner("mod", [1 + STREAMS, 6 * D])
    for name in ("q_split", "k_split", "v_split"):
        t[name] = inner(name, [ROWS, HEADS, 2 * HD], F32R)
    t["q_nat"] = inner("q_nat", [ROWS, ATT])
    t["u"] = inner("u", [ROWS, POOL])
    t["nF_p"] = inner("nF_p", [HEADS, SEQ])
    t["nF_s"] = inner("nF_s", [STREAMS * HEADS, PAST + NEW])
    t["mixT"] = inner("mixT", [D, ROWS])
    t["x2"] = inner("x2", [ROWS, D])
    t["h2T_hi"] = inner("h2T_hi", [D, ROWS], F32R)
    t["h2T_lo"] = inner("h2T_lo", [D, ROWS], F32R)
    for stage in (modulation, projection, pooling, prompt_attention, stream_attention,
                  out_projection, channel_mixing):
        taken = []

        def sems(name):
            taken.append(nc.alloc_semaphore(name=name))
            return taken[-1]
        stage(nc, t, sems)
        nc.clear_and_free_semaphores(taken)
        nc.all_engine_barrier()


_INS = ["x_prompt", "x_sample", "c_prompt", "c_sample", "cache_k", "cache_v", "cache_logf", "cache_pool",
        "w_mod", "b_mod", "w_in", "b_f", "q_gain", "k_gain", "w_pool", "pool_scale", "w_out", "w_up", "w_down"]
_OUTS = [("y_prompt", (1, 2048, 1024), (1, 2048, 1024)), ("y_sample", (8, 16, 1024), (8, 16, 1024)),
         ("k_p", (2048, 768), (1, 1, 2048, 12, 64)), ("v_p", (2048, 768), (1, 1, 2048, 12, 64)),
         ("logf_p", (2048, 12), (1, 1, 2048, 12)), ("pool_p", (15, 256), (1, 1, 15, 256)),
         ("k_s", (128, 768), (1, 8, 16, 12, 64)), ("v_s", (128, 768), (1, 8, 16, 12, 64)),
         ("logf_s", (128, 12), (1, 8, 16, 12)), ("pool_s", (8, 15, 256), (1, 8, 15, 256))]


def kernel(**inputs):
    import numpy as _np
    import concourse.bacc as _bacc
    from concourse.bass_utils import run_bass_kernel_spmd as _run

    nc = _bacc.Bacc("TRN2", target_bir_lowering=False, num_devices=1)
    arrays, ins, outs = {}, {}, {}
    for name in _INS:
        a = _np.ascontiguousarray(inputs[name])
        arrays[f"in_{name}_dram"] = a
        ins[name] = nc.dram_tensor(f"in_{name}_dram", a.shape, F32, kind="ExternalInput").ap()
    for i, (name, shape, _) in enumerate(_OUTS):
        outs[name] = nc.dram_tensor(f"out_{i}_dram", shape, F32, kind="ExternalOutput").ap()
    build(nc, ins, outs)
    r = _run(nc, [arrays], core_ids=[0])
    return tuple(r.results[0][f"out_{i}_dram"].reshape(shape) for i, (_, _, shape) in enumerate(_OUTS))
```

```python
import concourse.bass as bass
from concourse import mybir
from contextlib import ExitStack

F32 = mybir.dt.float32
F32R = mybir.dt.float32r
ALU = mybir.AluOpType
ACT = mybir.ActivationFunctionType
AX_X = mybir.AxisListType.X

P = 128
D = 1024
KT = D // P
SEQ = 2048
STREAMS = 8
NEW = 16
PAST = 1024
ROWS = SEQ + STREAMS * NEW
QT = SEQ // P
HEADS = 12
HD = 64
ATT = HEADS * HD
POOL = 256
HIST = 15
IN_COLS = POOL + 3 * ATT + HEADS
FF = 4096
EPS = 1e-6

BLOCKS = 4
TILES0, TILES = 5, 4


def n_tiles(b):
    return TILES0 if isinstance(b, int) and b == 0 else TILES


def tiles_before(b):
    return 0 if isinstance(b, int) and b == 0 else b * TILES + 1


def blocks(eng, body):
    body(0, 1)
    with eng.Fori(1, BLOCKS - 1) as b:
        body(b, b + 1)
    body(BLOCKS - 1, None)


def prompt_row(b, r):
    return (b * TILES + r) * P


def is_streams(b, r):
    return isinstance(b, int) and b == 0 and r == TILES0 - 1


C = 1 + STREAMS
MOD_W = 512
MOD_TILES = 4
MOD_GROUPS = 6 * D // (MOD_W * MOD_TILES)


def load_mod_bias(eng, t, bm, groups, sem):
    bias = t["b_mod"].rearrange("o (g j n) -> (o j) g n", g=MOD_GROUPS, j=MOD_TILES)[:, groups.start:groups.stop, :]
    for j in range(MOD_TILES):
        eng.dma_start(bm[32 * j:32 * j + C, :, :],
                      bias[j:j + 1].broadcast_to([C, len(groups), MOD_W])).then_inc(sem, 16)


def load_mod_weights(eng, t, to, g, k, sem):
    cols = slice(g * MOD_TILES * MOD_W, (g + 1) * MOD_TILES * MOD_W)
    eng.dma_start(to, t["w_mod"][0, k * P:(k + 1) * P, cols]).then_inc(sem, 16)


def modulate_tile(pe, bank, cT, wm, k):
    for j in range(MOD_TILES):
        last = pe.matmul(bank[32 * j:32 * j + C, :], cT[:, k, :], wm[:, j * MOD_W:(j + 1) * MOD_W],
                         start=(k == 0), stop=(k == KT - 1), tile_position=(0, 32 * j))
    return last


def modulation(nc, t, sems):
    NG, W, CT = 1, MOD_W, MOD_TILES
    DEPTH = 3
    with ExitStack() as ctx:
        sb = lambda name, shape, dt=F32: ctx.enter_context(nc.sbuf_tensor(name, shape, dt))
        c = sb("m_c", [C, D])
        e = sb("m_e", [C, D])
        cT = sb("m_cT", [P, KT, C])
        wm = sb("m_w", [P, DEPTH, CT * W])
        bm = sb("m_b", [P, NG, W])
        mo = sb("m_out", [P, NG, W])
        ident = sb("m_ident", [P, P])
        ps_c = ctx.enter_context(nc.psum_tensor("m_psc", [P, KT, C], F32))
        ps = [ctx.enter_context(nc.psum_tensor(f"m_ps{i}", [P, W], F32)) for i in range(NG)]
        c_in = sems("m_c_in")
        b_in = sems("m_b_in")
        w_in = [sems(f"m_w_in{i}") for i in range(DEPTH)]
        ident0 = sems("m_ident0")
        ident_ready = sems("m_ident_ready")
        e_ready = sems("m_e_ready")
        silu_ready = sems("m_silu_ready")
        chained = sems("m_chained")
        cT_psum = sems("m_cT_psum")
        cT_ready = sems("m_cT_ready")
        w_used = sems("m_w_used")
        mod_ready = sems("m_mod_ready")
        stored = sems("m_stored")

        block = ctx.enter_context(nc.Block())

        @block.sync
        def _(sp):
            sp.dma_start(c[0:1, :], t["c_prompt"]).then_inc(c_in, 16)
            sp.dma_start(c[1:C, :], t["c_sample"]).then_inc(c_in, 16)
            load_mod_bias(sp, t, bm, range(NG), b_in)
            for n in range(NG * KT):
                g, k = divmod(n, KT)
                if n >= DEPTH:
                    sp.wait_ge(w_used, n - DEPTH + 1)
                load_mod_weights(sp, t, wm[:, n % DEPTH, :], g, k, w_in[n % DEPTH])
            sp.wait_ge(cT_ready, 1)
            sp.dma_start(t["cT"], cT[:]).then_inc(stored, 16)
            for g in range(NG):
                sp.wait_ge(mod_ready, CT * (g + 1))
                for j in range(CT):
                    col = (g * CT + j) * W
                    sp.dma_start(t["mod"][:, col:col + W], mo[32 * j:32 * j + C, g, :]).then_inc(stored, 16)
            sp.wait_ge(stored, 16 * (NG * CT + 1))

        @block.gpsimd
        def _(pool):
            pool.memset(ident[:], 0.0).then_inc(ident0, 1)
            pool.wait_ge(ident0, 1)
            pool.affine_select(out=ident[:], in_=ident[:], compare_op=ALU.not_equal, fill=1.0, base=0,
                               pattern=[[-1, P]], channel_multiplier=1).then_inc(ident_ready, 1)

        @block.scalar
        def _(act):
            act.wait_ge(c_in, 32)
            act.activation(e[:], c[:], ACT.Exp, scale=-1.0).then_inc(e_ready, 1)

        @block.vector
        def _(dve):
            dve.wait_ge(e_ready, 1)
            dve.tensor_scalar(e[:], e[:], 1.0, None, ALU.add).then_inc(chained, 1)
            dve.wait_ge(chained, 1)
            dve.reciprocal(e[:], e[:]).then_inc(chained, 1)
            dve.wait_ge(chained, 2)
            dve.tensor_tensor(c[:], c[:], e[:], ALU.mult).then_inc(silu_ready, 1)
            dve.wait_ge(cT_psum, 1)
            dve.tensor_copy(cT[:], ps_c[:]).then_inc(cT_ready, 1)
            dve.wait_ge(b_in, 16 * CT)
            for g in range(NG):
                dve.wait_ge(w_used, KT * (g + 1))
                for j in range(CT):
                    one = 1.0 if (g * CT + j) // 2 in (1, 4) else 0.0
                    rows = slice(32 * j, 32 * j + C)
                    dve.scalar_tensor_tensor(mo[rows, g, :], ps[g][rows, :], one, bm[rows, g, :],
                                             ALU.add, ALU.add).then_inc(mod_ready, 1)

        @block.tensor
        def _(pe):
            pe.wait_ge(ident_ready, 1)
            pe.wait_ge(silu_ready, 1)
            for k in range(KT):
                last = pe.transpose(ps_c[:, k, :], c[:, k * P:(k + 1) * P], ident[0:C, 0:C])
            last.then_inc(cT_psum, 1)
            pe.wait_ge(cT_ready, 1)
            for n in range(NG * KT):
                g, k = divmod(n, KT)
                pe.wait_ge(w_in[n % DEPTH], 16 * (n // DEPTH + 1))
                modulate_tile(pe, ps[g], cT, wm[:, n % DEPTH, :], k).then_inc(w_used, 1)


HG = 6
QKV_W = HG * HD
UF_W = POOL + HEADS
CHUNKS = [("q", 0), ("q", 1), ("k", 0), ("k", 1), ("v", 0), ("v", 1), ("uf", 0)]
NCH = len(CHUNKS)
UF = NCH - 1


def tile_no(b, r):
    return tiles_before(b) + r


def tile_slot(b, r):
    return (r if isinstance(b, int) and b == 0 else TILES0 - TILES + r) % 2


def tile_half(b, r):
    return r // 2 if isinstance(b, int) and b == 0 else 2 * b + (1 + r) // 2


def step_taken(b, c, r):
    return not (isinstance(b, int) and b == 0 and c == 0 and r < 2)


def step_no(b, c, r):
    return NCH * tiles_before(b) + c * n_tiles(b) + r


def step_mod(b, c, r, n):
    first = 0 if isinstance(b, int) and b == 0 else NCH * (TILES0 - TILES)
    return (first + c * n_tiles(b) + r) % n


def step_half(b, c, r):
    if isinstance(b, int) and b == 0:
        return (c * TILES0 + r) // 2
    return b * (NCH * TILES // 2) + (NCH + c * TILES + r) // 2


def block_steps(b, following):
    R = n_tiles(b)
    for c in range(NCH):
        for r in range(R):
            yield "project", b, c, r
            if c == 0 and r == 0 and not (isinstance(b, int) and b == 0):
                yield "transpose", b, 0, TILES - 1
                yield "transposed", b, 0, TILES - 1
            if r == 0 and c + 1 < NCH:
                yield "weights", b, c + 1, 0
            if c == UF - 1 and following is not None:
                if r < 2:
                    yield "normalize", following, 0, r
                if r == 3:
                    yield "transpose", following, 0, 0
                    yield "transpose", following, 0, 1
                    yield "weights", following, 0, 0
            if c == UF and following is not None:
                if r < 2:
                    yield "transposed", following, 0, r
                    yield "normalize", following, 0, r + 2
                elif r == 3:
                    yield "transpose", following, 0, 2
                    yield "transposed", following, 0, 2


def projection(nc, t, sems):
    with ExitStack() as ctx:
        sb = lambda name, shape, dt=F32: ctx.enter_context(nc.sbuf_tensor(name, shape, dt))
        x = sb("p_x", [P, 2, D])
        h = sb("p_h", [P, 2, D])
        hT_hi = sb("p_hT_hi", [P, KT, TILES0 * P], F32R)
        hT_lo = sb("p_hT_lo", [P, KT, TILES0 * P], F32R)
        widths = [QKV_W, QKV_W, UF_W]
        raw = [sb(f"p_raw{i}", [P, KT, w]) for i, w in enumerate(widths)]
        w_hi = [sb(f"p_whi{i}", [P, KT, w], F32R) for i, w in enumerate(widths)]
        w_lo = [sb(f"p_wlo{i}", [P, KT, w], F32R) for i, w in enumerate(widths)]
        mod1 = sb("p_mod", [P, 2, 2 * D])
        shift1, scale1 = mod1[:, :, 0:D], mod1[:, :, D:2 * D]
        gain = {"q": sb("p_qgain", [P, HD]), "k": sb("p_kgain", [P, HD])}
        bf = sb("p_bf", [P, HEADS])
        ident = sb("p_ident", [P, P])
        ssq = sb("p_ssq", [P, 2])
        rstd = sb("p_rstd", [P, 2])
        eps = sb("p_eps", [P, 1])
        CONSTS = 1 + STREAMS + 3
        square = sb("p_square", [P, QKV_W])
        ssh = sb("p_ssh", [P, HG])
        rh = sb("p_rh", [P, HG])
        fz = sb("p_fz", [P, QT + 1, HEADS])
        fa = sb("p_fa", [P, QT + 1, HEADS])
        nat = sb("p_nat", [P, 2, QKV_W])
        split = [sb(f"p_split{i}", [P, HG, 2, HD], F32R) for i in range(2)]
        ps_x = [ctx.enter_context(nc.psum_tensor(f"p_psx{i}", [P, KT, P], F32)) for i in range(2)]
        ps_m = [ctx.enter_context(nc.psum_tensor(f"p_psm{i}", [P, 512], F32)) for i in range(4)]

        consts_in, ident0, ident_ready = sems("p_consts_in"), sems("p_ident0"), sems("p_ident_ready")
        consts_ready = sems("p_consts_ready")
        x_in = [sems(f"p_x_in{i}") for i in range(2)]
        squared, rms_ready, rstd_ready = sems("p_squared"), sems("p_rms_ready"), sems("p_rstd_ready")
        scaled, h_ready, hT_psum = sems("p_scaled"), sems("p_h_ready"), sems("p_hT_psum")
        hT_hi_ready, hT_ready = sems("p_hT_hi_ready"), sems("p_hT_ready")
        raw_in = [sems(f"p_raw_in{i}") for i in range(3)]
        w_hi_ready, w_ready, projected = sems("p_w_hi_ready"), sems("p_w_ready"), sems("p_projected")
        sq_ready, ss_ready, rmsh_ready, rh_ready = sems("p_sq_ready"), sems("p_ss_ready"), sems("p_rmsh_ready"), sems("p_rh_ready")
        normed, gained, hi_ready = sems("p_normed"), sems("p_gained"), sems("p_hi_ready")
        u_copied, f_chain, log1p_f = sems("p_u_copied"), sems("p_f_chain"), sems("p_log1p_f")
        staged = sems("p_staged")
        stored = [sems(f"p_stored{i}") for i in range(2)]

        def w_slot(c):
            return 2 if c == UF else c % 2

        def w_uses(b, c):
            return b if c == UF else 3 * b + c // 2

        def slot_taken(b, c):
            return not (isinstance(b, int) and b == 0 and (c < 2 or c == UF))

        def chunk_before(b, c):
            if 2 <= c < UF:
                return b * NCH + c - 2
            return b * NCH - (NCH - UF if c == UF else NCH - 4 - c)

        def steps_before(b, c):
            if 2 <= c < UF:
                return NCH * tiles_before(b) + (c - 1) * n_tiles(b)
            return NCH * tiles_before(b) - (0 if c == UF else NCH - 5 - c) * TILES

        def x_tile_taken(b, r):
            return not (isinstance(b, int) and b == 0 and r < 2)

        block = ctx.enter_context(nc.Block())

        @block.sync
        def _(sp):
            def load_x(b, r):
                s = tile_slot(b, r)
                if x_tile_taken(b, r):
                    sp.wait_ge(scaled, tile_no(b, r) - 1)
                if is_streams(b, r):
                    src = t["x_sample"].rearrange("b n d -> (b n) d")
                else:
                    src = t["x_prompt"][0, bass.ds(prompt_row(b, r), P), :]
                sp.dma_start(x[:, s, :], src).then_inc(x_in[s], 16)

            def load_weights(b, c):
                s = w_slot(c)
                if slot_taken(b, c):
                    sp.wait_ge(w_ready, chunk_before(b, c) + 1)
                kind, half = CHUNKS[c]
                w = t["w_in"][0].rearrange("(k p) n -> p k n", p=P)
                if kind == "uf":
                    sp.dma_start(raw[s][:, :, 0:POOL], w[:, :, 0:POOL]).then_inc(raw_in[s], 16)
                    sp.dma_start(raw[s][:, :, POOL:UF_W], w[:, :, IN_COLS - HEADS:IN_COLS]).then_inc(raw_in[s], 16)
                else:
                    col = POOL + "qkv".index(kind) * ATT + half * QKV_W
                    sp.dma_start(raw[s][:], w[:, :, col:col + QKV_W]).then_inc(raw_in[s], 16)

            def store(b, c, r):
                s = step_mod(b, c, r, 2)
                kind, half = CHUNKS[c]
                streams = is_streams(b, r)
                rows = slice(SEQ, ROWS) if streams else bass.ds(prompt_row(b, r), P)
                sp.wait_ge(staged, step_no(b, c, r) + 1)
                if kind == "uf":
                    for part in (slice(0, POOL // 2), slice(POOL // 2, POOL)):
                        sp.dma_start(t["u"][rows, part], nat[:, s, part]).then_inc(stored[s], 16)
                    return
                heads, cols = slice(half * HG, (half + 1) * HG), slice(half * QKV_W, (half + 1) * QKV_W)
                dst = t[kind + "_split"][rows, heads, :].bitcast(F32)
                sp.dma_start(dst, split[s][:].rearrange("p h a d -> p h (a d)").bitcast(F32)).then_inc(stored[s], 16)
                if kind == "q":
                    dst = t["q_nat"][rows, cols]
                else:
                    dst = t[kind + "_s"][:, cols] if streams else t[kind + "_p"][rows, cols]
                sp.dma_start(dst, nat[:, s, :]).then_inc(stored[s], 16)

            load_x(0, 0)
            load_weights(0, 0)
            sp.dma_start(mod1[:, 0, :], t["mod"][0:1, 0:2 * D].broadcast_to([P, 2 * D])).then_inc(consts_in, 16)
            for s in range(STREAMS):
                sp.dma_start(mod1[NEW * s:NEW * (s + 1), 1, :],
                             t["mod"][1 + s:2 + s, 0:2 * D].broadcast_to([NEW, 2 * D])).then_inc(consts_in, 16)
            sp.dma_start(gain["q"][:], t["q_gain"].broadcast_to([P, HD])).then_inc(consts_in, 16)
            sp.dma_start(gain["k"][:], t["k_gain"].broadcast_to([P, HD])).then_inc(consts_in, 16)
            sp.dma_start(bf[:], t["b_f"].broadcast_to([P, HEADS])).then_inc(consts_in, 16)

            load_x(0, 1)
            load_weights(0, 1)
            for r in range(2, TILES0):
                load_x(0, r)

            def body(b, following):
                for what, blk, c, r in block_steps(b, following):
                    if what == "weights":
                        if c + 1 < NCH:
                            load_weights(blk, c + 1)
                        if c == UF - 1 and following is not None:
                            load_x(following, 0)
                            load_x(following, 1)
                        if c == UF and following is not None:
                            load_weights(following, 0)
                    elif what == "normalize":
                        if 2 <= r + 2 < TILES:
                            load_x(blk, r + 2)
                    elif what == "project":
                        store(blk, c, r)
            blocks(sp, body)
            sp.wait_ge(f_chain, 3)
            logf = t["logf_p"].rearrange("(n p) h -> p n h", p=P)
            sp.dma_start(logf[:, 0:TILES, :], fz[:, 0:TILES, :]).then_inc(consts_in, 16)
            sp.dma_start(logf[:, TILES:, :], fz[:, TILES0:, :]).then_inc(consts_in, 16)
            sp.dma_start(t["logf_s"], fz[:, TILES0 - 1, :]).then_inc(consts_in, 16)
            sp.wait_ge(consts_in, 16 * (CONSTS + 3))
            last = BLOCKS - 1, UF, TILES - 1
            for s in range(2):
                uses = step_half(*last) + (1 if s <= step_mod(*last, 2) else 0)
                sp.wait_ge(stored[s], 32 * uses)

        @block.gpsimd
        def _(pool):
            pool.memset(ident[:], 0.0).then_inc(ident0, 1)
            pool.wait_ge(ident0, 1)
            pool.affine_select(out=ident[:], in_=ident[:], compare_op=ALU.not_equal, fill=1.0, base=0,
                               pattern=[[-1, P]], channel_multiplier=1).then_inc(ident_ready, 1)


        @block.scalar
        def _(act):
            def split_weights(b, c):
                s = w_slot(c)
                act.wait_ge(raw_in[s], (32 if c == UF else 16) * (w_uses(b, c) + 1))
                if slot_taken(b, c):
                    act.wait_ge(projected, steps_before(b, c))
                act.activation(w_hi[s][:], raw[s][:], ACT.Copy).then_inc(w_hi_ready, 1)

            def normalize(b, r):
                n, s = tile_no(b, r), tile_slot(b, r)
                act.wait_ge(x_in[s], 16 * (tile_half(b, r) + 1))
                if x_tile_taken(b, r):
                    act.wait_ge(hT_psum, n - 1)
                act.activation(h[:, s, :], x[:, s, :], ACT.Square, accum_out=ssq[:, s:s + 1]).then_inc(squared, 1)
                act.wait_ge(squared, n + 1)
                act.activation(rstd[:, s:s + 1], ssq[:, s:s + 1], ACT.Sqrt, scale=1.0 / D, bias=eps[:]).then_inc(rms_ready, 1)

            def transposed(b, r):
                s = tile_slot(b, r)
                act.wait_ge(hT_psum, tile_no(b, r) + 1)
                if not (isinstance(b, int) and b == 0):
                    act.wait_ge(projected, NCH * tiles_before(b) - TILES + r + 1)
                act.activation(hT_hi[:, :, r * P:(r + 1) * P], ps_x[s][:], ACT.Copy).then_inc(hT_hi_ready, 1)

            def project(b, c, r):
                kind, half = CHUNKS[c]
                s = step_mod(b, c, r, 2)
                bank = ps_m[step_mod(b, c, r, 4)]
                act.wait_ge(projected, step_no(b, c, r) + 1)
                if kind in "qk":
                    n = 4 * tiles_before(b) + c * n_tiles(b) + r
                    act.activation(square[:], bank[:, 0:QKV_W], ACT.Square).then_inc(sq_ready, 1)
                    act.wait_ge(ss_ready, n + 1)
                    act.activation(rh[:], ssh[:], ACT.Sqrt, scale=1.0 / HD, bias=eps[:]).then_inc(rmsh_ready, 1)
                    act.wait_ge(gained, n + 1)
                    act.activation(split[s][:, :, 0, :], nat[:, s, :].rearrange("p (h d) -> p h d", d=HD),
                                   ACT.Copy).then_inc(hi_ready, 1)
                    return
                if step_taken(b, c, r):
                    act.wait_ge(stored[s], 32 * step_half(b, c, r))
                if kind == "v":
                    act.activation(nat[:, s, :], bank[:, 0:QKV_W], ACT.Copy)
                    act.activation(split[s][:, :, 0, :], bank[:, 0:QKV_W].rearrange("p (h d) -> p h d", d=HD),
                                   ACT.Copy).then_inc(hi_ready, 1)
                else:
                    act.activation(nat[:, s, 0:POOL], bank[:, 0:POOL], ACT.Copy).then_inc(u_copied, 1)

            act.wait_ge(consts_ready, 1)
            normalize(0, 0)
            split_weights(0, 0)
            for r in range(TILES0):
                if r + 1 < TILES0:
                    normalize(0, r + 1)
                transposed(0, r)

            def body(b, following):
                for what, blk, c, r in block_steps(b, following):
                    if what == "weights":
                        split_weights(blk, c)
                    elif what == "normalize":
                        normalize(blk, r)
                    elif what == "transposed":
                        transposed(blk, r)
                    elif what == "project":
                        project(blk, c, r)
            blocks(act, body)
            act.wait_ge(f_chain, 2)
            act.activation(fa[:], fa[:], ACT.Exp, scale=-1.0).then_inc(log1p_f, 1)
            act.wait_ge(log1p_f, 1)
            act.activation(fa[:], fa[:], ACT.Ln, bias=1.0).then_inc(log1p_f, 1)

        @block.vector
        def _(dve):
            def split_weights(b, c):
                s = w_slot(c)
                dve.wait_ge(w_hi_ready, b * NCH + c + 1)
                dve.tensor_tensor(w_lo[s][:], raw[s][:], w_hi[s][:].bitcast(F32), ALU.subtract).then_inc(w_ready, 1)

            def normalize(b, r):
                n, s = tile_no(b, r), tile_slot(b, r)
                which = 1 if is_streams(b, r) else 0
                dve.wait_ge(rms_ready, n + 1)
                dve.reciprocal(rstd[:, s:s + 1], rstd[:, s:s + 1]).then_inc(rstd_ready, 1)
                dve.wait_ge(rstd_ready, n + 1)
                dve.scalar_tensor_tensor(h[:, s, :], x[:, s, :], rstd[:, s:s + 1], scale1[:, which, :],
                                         ALU.mult, ALU.mult).then_inc(scaled, 1)
                dve.wait_ge(scaled, n + 1)
                dve.tensor_tensor(h[:, s, :], h[:, s, :], shift1[:, which, :], ALU.add).then_inc(h_ready, 1)

            def transposed(b, r):
                s = tile_slot(b, r)
                dve.wait_ge(hT_hi_ready, tile_no(b, r) + 1)
                cols = slice(r * P, (r + 1) * P)
                dve.tensor_tensor(hT_lo[:, :, cols], ps_x[s][:], hT_hi[:, :, cols].bitcast(F32),
                                  ALU.subtract).then_inc(hT_ready, 1)

            def project(b, c, r):
                kind, half = CHUNKS[c]
                s = step_mod(b, c, r, 2)
                bank = ps_m[step_mod(b, c, r, 4)]
                if kind in "qk":
                    n = 4 * tiles_before(b) + c * n_tiles(b) + r
                    by_head = lambda ap: ap.rearrange("p (h d) -> p h d", d=HD)
                    dve.wait_ge(sq_ready, n + 1)
                    dve.reduce_sum(ssh[:], by_head(square[:]), AX_X).then_inc(ss_ready, 1)
                    dve.wait_ge(rmsh_ready, n + 1)
                    dve.reciprocal(rh[:], rh[:]).then_inc(rh_ready, 1)
                    dve.wait_ge(rh_ready, n + 1)
                    dve.tensor_tensor(by_head(square[:]), by_head(bank[:, 0:QKV_W]),
                                      rh[:].unsqueeze(2).broadcast_to([P, HG, HD]), ALU.mult
                                      ).then_inc(normed, 1)
                    dve.wait_ge(normed, n + 1)
                    if step_taken(b, c, r):
                        dve.wait_ge(stored[s], 32 * step_half(b, c, r))
                    g = gain[kind][:].unsqueeze(1).broadcast_to([P, HG, HD])
                    dve.tensor_tensor(by_head(nat[:, s, :]), by_head(square[:]), g, ALU.mult).then_inc(gained, 1)
                    dve.wait_ge(hi_ready, 6 * tiles_before(b) + c * n_tiles(b) + r + 1)
                    dve.tensor_tensor(split[s][:, :, 1, :], by_head(nat[:, s, :]),
                                      split[s][:, :, 0, :].bitcast(F32), ALU.subtract).then_inc(staged, 1)
                elif kind == "v":
                    dve.wait_ge(hi_ready, 6 * tiles_before(b) + c * n_tiles(b) + r + 1)
                    dve.tensor_tensor(split[s][:, :, 1, :], bank[:, 0:QKV_W].rearrange("p (h d) -> p h d", d=HD),
                                      split[s][:, :, 0, :].bitcast(F32), ALU.subtract).then_inc(staged, 1)
                else:
                    n = tile_no(b, r)
                    dve.wait_ge(u_copied, n + 1)
                    dve.tensor_tensor(fz[:, bass.ds(n, 1), :].rearrange("p o h -> p (o h)"), bank[:, POOL:UF_W], bf[:],
                                      ALU.add).then_inc(staged, 1)

            dve.memset(eps[:], EPS).then_inc(consts_ready, 1)
            split_weights(0, 0)
            dve.wait_ge(consts_in, 16 * CONSTS)
            dve.tensor_scalar(gain["q"][:], gain["q"][:], HD ** -0.5, None, ALU.mult).then_inc(consts_ready, 1)
            dve.wait_ge(consts_ready, 2)
            normalize(0, 0)
            for r in range(TILES0):
                if r + 1 < TILES0:
                    normalize(0, r + 1)
                transposed(0, r)

            def body(b, following):
                for what, blk, c, r in block_steps(b, following):
                    if what == "weights":
                        split_weights(blk, c)
                    elif what == "normalize":
                        normalize(blk, r)
                    elif what == "transposed":
                        transposed(blk, r)
                    elif what == "project":
                        project(blk, c, r)
            blocks(dve, body)
            dve.wait_ge(staged, NCH * (QT + 1))
            dve.tensor_scalar(fa[:], fz[:], -1.0, None, ALU.mult).then_inc(f_chain, 1)
            dve.wait_ge(f_chain, 1)
            dve.tensor_tensor(fa[:], fz[:], fa[:], ALU.max).then_inc(f_chain, 1)
            dve.wait_ge(log1p_f, 2)
            dve.scalar_tensor_tensor(fz[:], fz[:], 0.0, fa[:], ALU.min, ALU.subtract).then_inc(f_chain, 1)

        @block.tensor
        def _(pe):
            def transpose(b, r):
                n, s = tile_no(b, r), tile_slot(b, r)
                pe.wait_ge(h_ready, n + 1)
                if x_tile_taken(b, r):
                    pe.wait_ge(hT_ready, n - 1)
                for k in range(KT):
                    last = pe.transpose(ps_x[s][:, k, :], h[:, s, k * P:(k + 1) * P], ident[:])
                last.then_inc(hT_psum, 1)

            def project(b, c, r):
                bank = ps_m[step_mod(b, c, r, 4)]
                s, w = w_slot(c), (UF_W if c == UF else QKV_W)
                if r == 0:
                    pe.wait_ge(w_ready, b * NCH + c + 1)
                if c == 0:
                    pe.wait_ge(hT_ready, tile_no(b, r) + 1)
                if not (isinstance(b, int) and b == 0 and c == 0 and r < 4):
                    pe.wait_ge(staged, step_no(b, c, r) - 3)
                rows = slice(r * P, (r + 1) * P)
                for k in range(KT):
                    for i, (a, wt) in enumerate(((hT_hi, w_hi), (hT_hi, w_lo), (hT_lo, w_hi))):
                        last = pe.matmul(bank[:, 0:w], a[:, k, rows], wt[s][:, k, :],
                                         start=(k == 0 and i == 0), stop=(k == KT - 1 and i == 2))
                last.then_inc(projected, 1)

            pe.wait_ge(ident_ready, 1)
            for r in range(2):
                transpose(0, r)

            def body(b, following):
                for what, blk, c, r in block_steps(b, following):
                    if what == "transpose":
                        transpose(blk, r)
                    elif what == "project":
                        project(blk, c, r)
                        if isinstance(blk, int) and blk == 0 and c == 0 and r + 2 < TILES0:
                            transpose(0, r + 2)
            blocks(pe, body)


def pooling(nc, t, sems):
    L = HIST + SEQ
    SL = HIST + NEW
    WINDOWS = (2, 4, 8, 16)
    KEYS = PAST + NEW
    GD = POOL // len(WINDOWS)
    with ExitStack() as ctx:
        sb = lambda name, shape, dt=F32: ctx.enter_context(nc.sbuf_tensor(name, shape, dt))
        u = sb("o_u", [P, QT + 1, POOL])
        hist = sb("o_hist", [STREAMS * HIST, POOL])
        z = sb("o_z", [P, 2, L])
        zs = sb("o_zs", [P, 2, STREAMS, SL])
        sums = sb("o_sums", [P, 2, L])
        sumss = sb("o_sumss", [P, 2, STREAMS, SL])
        mixed = sb("o_mixed", [P, 2, ROWS])
        y = sb("o_y", [P, 2, ROWS])
        count = sb("o_count", [P, 2, HIST])
        w = sb("o_w", [P, 2, P])
        pscale = sb("o_pscale", [P, 2])
        ident = sb("o_ident", [P, P])
        lf = sb("o_lf", [P, QT, HEADS])
        lc = sb("o_lc", [P, PAST // P, STREAMS, HEADS])
        nl = sb("o_nl", [HEADS, SEQ])
        nf = sb("o_nf", [HEADS, SEQ])
        nls = sb("o_nls", [STREAMS * HEADS, KEYS])
        nfs = sb("o_nfs", [STREAMS * HEADS, KEYS])
        zero = sb("o_zero", [P, SEQ])
        ps = [ctx.enter_context(nc.psum_tensor(f"o_ps{i}", [P, 4 * P], F32)) for i in range(8)]

        GROUPS = range(1, MOD_GROUPS)
        DEPTH = 3
        EARLY = 11
        cT = sb("o_cT", [P, KT, C])
        wm = sb("o_wm", [P, DEPTH, MOD_TILES * MOD_W])
        bm = sb("o_bm", [P, len(GROUPS), MOD_W])
        mo = sb("o_mo", [P, len(GROUPS), MOD_W])
        cT_in, bm_in, wm_used, mod_ready = (sems("o_" + n) for n in ("cT_in", "bm_in", "wm_used", "mod_ready"))
        wm_in = [sems(f"o_wm_in{i}") for i in range(DEPTH)]

        u_in, hist_in, w_in, lf_in, lc_in, new_in = (sems("o_" + n) for n in (
            "u_in", "hist_in", "w_in", "lf_in", "lc_in", "new_in"))
        zeroed, ident0, ready, turned, out_of_bank = (sems("o_" + n) for n in (
            "zeroed", "ident0", "ready", "turned", "out_of_bank"))
        chain, mixed_ready, product, y_ready, nf_ready, stored = (sems("o_" + n) for n in (
            "chain", "mixed_ready", "product", "y_ready", "nf_ready", "stored"))

        turns = [("u", half, g) for g in range(QT // 4) for half in range(2)]
        turns += [("s", 0, 0), ("s", 1, 0), ("hist", 0, 0), ("hist", 1, 0)]
        turns += [("lf", 0, g) for g in range(QT // 4)] + [("lc", 0, g) for g in range(PAST // P // 4)]
        n_z = turns.index(("lf", 0, 0))
        block = ctx.enter_context(nc.Block())

        @block.sync
        def _(sp):
            sp.dma_start(u[:], t["u"].rearrange("(n p) c -> p n c", p=P)).then_inc(u_in, 16)
            sp.dma_start(hist[:], t["cache_pool"][0].rearrange("b n c -> (b n) c")).then_inc(hist_in, 16)
            sp.dma_start(lf[:], t["logf_p"].rearrange("(n p) h -> p n h", p=P)).then_inc(lf_in, 16)
            sp.wait_ge(zeroed, 1)
            for g in range(len(WINDOWS)):
                part = slice(GD * (g % 2), GD * (g % 2) + GD)
                sp.dma_start(w[part, g // 2, part], t["w_pool"][0, g]).then_inc(w_in, 16)
            sp.dma_start(pscale[:], t["pool_scale"][0].rearrange("(a p) -> p a", p=P),
                         allow_slow_non_contiguous=True).then_inc(w_in, 16)
            sp.dma_start(t["pool_p"], t["u"][SEQ - HIST:SEQ, :]).then_inc(stored, 16)
            sp.dma_start(t["pool_s"], t["u"][SEQ:ROWS, :].rearrange("(b n) c -> b n c", n=NEW)[:, 1:, :]
                         ).then_inc(stored, 16)
            sp.dma_start(cT[:], t["cT"]).then_inc(cT_in, 16)
            load_mod_bias(sp, t, bm, GROUPS, bm_in)
            for n in range(len(GROUPS) * KT):
                if n >= DEPTH:
                    sp.wait_ge(wm_used, n - DEPTH + 1)
                load_mod_weights(sp, t, wm[:, n % DEPTH, :], GROUPS[n // KT], n % KT, wm_in[n % DEPTH])
            for half in range(2):
                for a, b in ((0, 1024), (1024, ROWS)):
                    sp.wait_ge(y_ready, 5 * half + (2 if a == 0 else 5))
                    sp.dma_start(t["mixT"][P * half:P * half + P, a:b], y[:, half, a:b]).then_inc(stored, 16)
            sp.wait_ge(nf_ready, 2)
            sp.dma_start(t["nF_p"], nf[:]).then_inc(stored, 16)
            sp.dma_start(t["nF_s"], nfs[:]).then_inc(stored, 16)
            for i, g in enumerate(GROUPS):
                sp.wait_ge(mod_ready, MOD_TILES * (i + 1))
                for j in range(MOD_TILES):
                    col = (g * MOD_TILES + j) * MOD_W
                    sp.dma_start(t["mod"][:, col:col + MOD_W], mo[32 * j:32 * j + C, i, :]).then_inc(stored, 16)
            sp.wait_ge(stored, 16 * (8 + len(GROUPS) * MOD_TILES))

        @block.gpsimd
        def _(pool):
            pool.memset(w[:], 0.0).then_inc(zeroed, 1)
            pool.memset(zero[:], 0.0).then_inc(ready, 1)
            pool.memset(z[:, :, 0:HIST], 0.0).then_inc(ready, 1)
            for i in range(HIST):
                pool.memset(count[:, :, i:i + 1], float(i + 1)).then_inc(ready, 1)
            pool.memset(ident[:], 0.0).then_inc(ident0, 1)
            pool.wait_ge(ident0, 1)
            pool.affine_select(out=ident[:], in_=ident[:], compare_op=ALU.not_equal, fill=1.0, base=0,
                               pattern=[[-1, P]], channel_multiplier=1).then_inc(ident0, 1)
            for tt in range(PAST // P):
                pool.dma_start(lc[:, tt, :, :], t["cache_logf"][0, :, tt * P:(tt + 1) * P, :].rearrange("b p h -> p b h")
                               ).then_inc(lc_in, 16)
            for b in range(STREAMS):
                pool.dma_start(nls[HEADS * b:HEADS * (b + 1), PAST:KEYS],
                               t["logf_s"][NEW * b:NEW * (b + 1), :].rearrange("n h -> h n"),
                               allow_slow_non_contiguous=True).then_inc(new_in, 16)

        @block.tensor
        def _(pe):
            pe.wait_ge(ident0, 2)

            def modulate(tiles):
                pe.wait_ge(cT_in, 16)
                for m in tiles:
                    pe.wait_ge(wm_in[m % DEPTH], 16 * (m // DEPTH + 1))
                    modulate_tile(pe, ps[6 + m // KT], cT, wm[:, m % DEPTH, :], m % KT).then_inc(wm_used, 1)

            for n, (kind, half, g) in enumerate(turns):
                if n == n_z:
                    modulate(range(0, EARLY))
                bank = ps[n % 4]
                if n >= 4:
                    pe.wait_ge(out_of_bank, n - 3)
                cols = slice(P * half, P * half + P)
                if kind == "u":
                    if n == 0:
                        pe.wait_ge(u_in, 16)
                    for i in range(4):
                        tile = 4 * g + i
                        last = pe.transpose(bank[:, P * i:P * i + P], u[:, tile, cols], ident[:])
                elif kind == "s":
                    last = pe.transpose(bank[:, 0:P], u[:, QT, cols], ident[:])
                elif kind == "hist":
                    pe.wait_ge(hist_in, 16)
                    m = STREAMS * HIST
                    last = pe.transpose(bank[:, 0:m], hist[:, cols], ident[0:m, 0:m])
                elif kind == "lf":
                    pe.wait_ge(lf_in, 16)
                    for i in range(4):
                        last = pe.transpose(bank[0:HEADS, P * i:P * i + P], lf[:, 4 * g + i, :], ident[:])
                else:
                    pe.wait_ge(lc_in, 16 * (PAST // P))
                    for i in range(4):
                        last = pe.transpose(bank[0:STREAMS * HEADS, P * i:P * i + P],
                                            lc[:, 4 * g + i, :, :].rearrange("p b h -> p (b h)"), ident[:])
                last.then_inc(turned, 1)
            modulate(range(EARLY, len(GROUPS) * KT))
            pe.wait_ge(w_in, 16 * 5)
            for half in range(2):
                pe.wait_ge(mixed_ready, half + 1)
                for i in range(5):
                    n = 5 * half + i
                    bank = ps[4 + n % 2]
                    if n >= 2:
                        pe.wait_ge(y_ready, n - 1)
                    a, b = 512 * i, min(512 * i + 512, ROWS)
                    pe.matmul(bank[:, 0:b - a], w[:, half, :], mixed[:, half, a:b], start=True, stop=True
                              ).then_inc(product, 1)

        @block.scalar
        def _(act):
            for half in range(2):
                for i in range(5):
                    n = 5 * half + i
                    act.wait_ge(product, n + 1)
                    a, b = 512 * i, min(512 * i + 512, ROWS)
                    act.activation(y[:, half, a:b], ps[4 + n % 2][:, 0:b - a], ACT.Copy,
                                   scale=pscale[:, half:half + 1]).then_inc(y_ready, 1)

        @block.vector
        def _(dve):
            done = 0

            def link(ins):
                nonlocal done
                ins.then_inc(chain, 1)
                done += 1
                dve.wait_ge(chain, done)

            def take(n):
                kind, half, g = turns[n]
                bank = ps[n % 4]
                dve.wait_ge(turned, n + 1)
                if kind == "u":
                    dst, src = z[:, half, HIST + 4 * P * g:HIST + 4 * P * (g + 1)], bank[:]
                elif kind == "s":
                    dst, src = zs[:, half, :, HIST:], bank[:, 0:P].rearrange("p (b n) -> p b n", n=NEW)
                elif kind == "hist":
                    dst = zs[:, half, :, 0:HIST]
                    src = bank[:, 0:STREAMS * HIST].rearrange("p (b n) -> p b n", n=HIST)
                elif kind == "lf":
                    dst, src = nl[:, 4 * P * g:4 * P * (g + 1)], bank[0:HEADS, :]
                else:
                    dst, src = nls[:, 4 * P * g:4 * P * (g + 1)], bank[0:STREAMS * HEADS, :]
                sign = -1.0 if kind in ("lf", "lc") else 1.0
                dve.tensor_scalar(dst, src, sign, None, ALU.mult).then_inc(out_of_bank, 1)

            for n in range(n_z):
                take(n)
            dve.wait_ge(out_of_bank, n_z)
            dve.wait_ge(ready, 2 + HIST)
            for g, win in enumerate(WINDOWS):
                part = slice(GD * (g % 2), GD * (g % 2) + GD)
                link(dve.tensor_scalar(count[part, g // 2, :], count[part, g // 2, :], float(win), None, ALU.min))
            link(dve.reciprocal(count[:], count[:]))
            for half in range(2):
                src, srcs = z[:, half, :], zs[:, half, :, :]
                for level, (step, g) in enumerate(((1, 0), (2, 1), (4, 2), (8, 3))):
                    if 2 * step > WINDOWS[2 * half + 1]:
                        break
                    lo = 2 * step - 1
                    dst, dsts = sums[:, level % 2, :], sumss[:, level % 2, :, :]
                    link(dve.tensor_tensor(dst[:, lo:L], src[:, lo:L], src[:, lo - step:L - step], ALU.add))
                    link(dve.tensor_tensor(dsts[:, :, lo:SL], srcs[:, :, lo:SL], srcs[:, :, lo - step:SL - step], ALU.add))
                    src, srcs = dst, dsts
                    if g // 2 == half:
                        part = slice(GD * (g % 2), GD * (g % 2) + GD)
                        inv = 1.0 / (2 * step)
                        out = mixed[part, half, :]
                        link(dve.scalar_tensor_tensor(out[:, HIST:SEQ], dst[part, 2 * HIST:L], inv,
                                                      z[part, half, 2 * HIST:L], ALU.mult, ALU.subtract))
                        link(dve.tensor_tensor(out[:, 0:HIST], dst[part, HIST:2 * HIST], count[part, half, :], ALU.mult))
                        link(dve.tensor_tensor(out[:, 0:HIST], out[:, 0:HIST], z[part, half, HIST:2 * HIST], ALU.subtract))
                        last = dve.scalar_tensor_tensor(out[:, SEQ:ROWS].rearrange("p (b n) -> p b n", n=NEW),
                                                        dsts[part, :, HIST:], inv, zs[part, half, :, HIST:],
                                                        ALU.mult, ALU.subtract)
                        if 2 * step == WINDOWS[2 * half + 1]:
                            last.then_inc(mixed_ready, 1)
                        else:
                            link(last)
            for n in range(n_z, len(turns)):
                take(n)
            dve.wait_ge(out_of_bank, len(turns))
            dve.wait_ge(new_in, 16 * STREAMS)
            link(dve.tensor_scalar(nls[:, PAST:KEYS], nls[:, PAST:KEYS], -1.0, None, ALU.mult))
            dve.tensor_tensor_scan(nf[:], nl[:], zero[0:HEADS, :], 0.0, ALU.add, ALU.add).then_inc(nf_ready, 1)
            dve.tensor_tensor_scan(nfs[:], nls[:], zero[0:STREAMS * HEADS, 0:KEYS], 0.0, ALU.add, ALU.add
                                   ).then_inc(nf_ready, 1)
            dve.wait_ge(bm_in, 16 * MOD_TILES)
            for i, g in enumerate(GROUPS):
                dve.wait_ge(wm_used, KT * (i + 1))
                for j in range(MOD_TILES):
                    one = 1.0 if (g * MOD_TILES + j) * MOD_W // D == 4 else 0.0
                    rows = slice(32 * j, 32 * j + C)
                    dve.scalar_tensor_tensor(mo[rows, i, :], ps[6 + i][rows, :], one, bm[rows, i, :],
                                             ALU.add, ALU.add).then_inc(mod_ready, 1)


QB = 4
NB = QT // QB
WIDE = 512
PIECE = 1024


def wait_past(eng, sem, value):
    if not isinstance(value, int) or value > 0:
        eng.wait_ge(sem, value)


def pairs(eng, body):
    n = HEADS // 2
    body(0, False)
    with eng.Fori(1, n - 1) as j:
        body(j, False)
    body(n - 1, True)


SLOTS = sum(QB * (b + 1) for b in range(NB))
PAIR = 2 * SLOTS
LEAD = 23
AHEAD = 3
TURNS_OF = [(b, kt) for b in range(NB) for kt in range(QB * (b + 1))]
CHUNKS_OF = [(i, c) for i in range(QT) for c in range(i // QB + 1)]
EXPS = sum(1 if (i + 1) * P <= PIECE else 2 for i in range(QT))


def exps_before(i):
    return sum(1 if (n + 1) * P <= PIECE else 2 for n in range(i))


def turn_bank(idx):
    return idx % PAIR % 3


def bank_reuse(idx):
    return 2 if idx % PAIR < 2 else 3


def block_start(b):
    return QB * b * (b + 1) // 2


def row_ends(idx):
    i, c = CHUNKS_OF[idx % SLOTS]
    return c == i // QB


def lead_in():
    for g in range(8):
        yield "prepare", 0, g
    yield "swap", 0, 0
    yield "load_rows", 1, 0
    for c in range(LEAD):
        yield "score", c, 0
        yield from exponentials(c - 1, False)
        if c >= LEAD - 8:
            yield "prepare", 1, c - (LEAD - 8)
    yield "swap", 1, 0
    for n in range(AHEAD):
        yield "turn", n, 0
        if n:
            yield "rest", n - 1, 0
            yield "inverse", 0, n - 1


def exponentials(idx, last):
    for piece in range(2):
        at = idx - piece
        if 0 <= at < (PAIR if last else PAIR + SLOTS) and row_ends(at):
            if piece == 0 or (CHUNKS_OF[at % SLOTS][0] + 1) * P > PIECE:
                yield "exp", at, piece


def attention_steps(j, last):
    first = isinstance(j, int) and j == 0
    end = PAIR if last else PAIR + SLOTS
    for s in range(PAIR):
        b, kt = TURNS_OF[s % SLOTS]
        blk = NB * (s // SLOTS) + b
        if s + AHEAD - 1 < end:
            yield "rest", s + AHEAD - 1, 0
        if s + AHEAD < end:
            yield "turn", s + AHEAD, 0
        if s + LEAD < end:
            yield "score", s + LEAD, 0
        yield from exponentials(s + LEAD - 1, last)
        yield "values", s, 0
        if kt == 0 and not (first and s == 0):
            yield "divisors", blk - 1, 0
            yield "sum", blk - 1, 0
        if kt == 1:
            if not (first and s == 1):
                yield "divide", blk - 1, 0
            yield "inverse", blk, 3
        if kt == 0:
            yield "inverse", blk, 2
        for part, at in ((0, s + 2), (1, s + 1)):
            if at < end and TURNS_OF[at % SLOTS][1] == 0:
                yield "inverse", NB * (at // SLOTS) + TURNS_OF[at % SLOTS][0], part
        if kt == (2 if b == 0 else 4):
            yield "inverse_turn", blk, 0
        t, head = s % SLOTS, s // SLOTS
        if head + 1 < 2 or not last:
            if t == 0:
                yield "load_v", head + 1, 0
        if not last:
            if t == 0:
                yield "load_rows", head + 2, 0
            if 29 <= t < 37:
                yield "prepare", head + 2, t - 29
            if t == 37:
                yield "swap", head + 2, 0
            if t == 20:
                yield "load_bias", head + 2, 0
    if last:
        for what in ("divisors", "sum", "divide"):
            yield what, 2 * NB - 1, 0


def prompt_attention(nc, t, sems):
    with ExitStack() as ctx:
        sb = lambda name, shape, dt=F32: ctx.enter_context(nc.sbuf_tensor(name, shape, dt))
        qT = [sb(f"a_qT{e}", [P, SEQ], F32R) for e in range(2)]
        kT = [sb(f"a_kT{e}", [P, SEQ], F32R) for e in range(2)]
        kX = [sb(f"a_kX{e}", [P, SEQ], F32R) for e in range(2)]
        v = [sb(f"a_v{e}", [P, QT, P], F32R) for e in range(2)]
        rows_q = sb("a_rows_q", [P, QT, P])
        rows_k = sb("a_rows_k", [P, QT, P])
        bias = [sb(f"a_bias{e}", [P, SEQ]) for e in range(2)]
        probs = [sb(f"a_probs{b}", [P, QB, QB * P * (b + 1)]) for b in range(NB)]
        pT_hi = [sb(f"a_pTh{i}", [P, QB * P], F32R) for i in range(4)]
        pT_lo = [sb(f"a_pTl{i}", [P, QB * P], F32R) for i in range(4)]
        ident = sb("a_ident", [P, P])
        mask = sb("a_mask", [P, P])
        ident_r = sb("a_ident_r", [P, P], F32R)
        mask_r = sb("a_mask_r", [P, P], F32R)
        nmax = sb("a_nmax", [P, QT, QT // QB])
        total = sb("a_total", [P, QT, 2])
        inv = sb("a_inv", [P, QB])
        inv2 = sb("a_inv2", [P, 2 * QB], F32R)
        invT = sb("a_invT", [2 * QB, P])
        pick = sb("a_pick", [2 * QB, QB, P])
        spread = sb("a_spread", [2 * QB, QB, P], F32R)
        ones = sb("a_ones", [2 * QB, P], F32R)
        rest = sb("a_rest", [HD, QB * P])
        both = sb("a_both", [HD, QB * P])
        out = sb("a_out", [HD, 2, QB * P])
        ps_s = [ctx.enter_context(nc.psum_tensor(f"a_pss{i}", [P, WIDE], F32)) for i in range(2)]
        ps_t = [ctx.enter_context(nc.psum_tensor(f"a_pst{i}", [P, QB * P], F32)) for i in range(3)]
        ps_o = [ctx.enter_context(nc.psum_tensor(f"a_pso{i}", [P, QB * P], F32)) for i in range(2)]
        ps_x = ctx.enter_context(nc.psum_tensor("a_psx", [P, QB * P], F32))

        names = ("divisors_out waited rows_in v_in0 v_in1 bias_in0 bias_in1 swapped0 swapped1 made consts ready rows_turned "
                 "prepared scored chunk_out exped turned hi_ready lo_ready valued inv_chain inv2_ready "
                 "inv_turned invT_ready spread_ready divisors rest_ready summed divided stored0 stored1").split()
        S = {n: sems("a_" + n) for n in names}
        v_in, bias_in = [S["v_in0"], S["v_in1"]], [S["bias_in0"], S["bias_in1"]]
        swapped, stored = [S["swapped0"], S["swapped1"]], [S["stored0"], S["stored1"]]

        number = lambda j, idx: PAIR * j + idx
        block_no = lambda j, blk: 2 * NB * j + blk
        head_no = lambda j, head: 2 * j + head
        parity = lambda head: head % 2
        pair_of = lambda j, head: j + head // 2

        def block_end(blk):
            return SLOTS * (blk // NB) + block_start(blk % NB + 1)

        def diag_of(idx):
            b, kt = TURNS_OF[idx % SLOTS]
            return max(0, kt - QB * b)

        block = ctx.enter_context(nc.Block())

        @block.sync
        def _(sp):
            def load_rows(j, head):
                h = head_no(j, head)
                wait_past(sp, S["rows_turned"], 8 * h)
                for to, name in ((rows_q, "q"), (rows_k, "k")):
                    src = t[name + "_split"][0:SEQ, bass.ds(h, 1), :].rearrange("(n p) o d -> p (n o) d", p=P)
                    sp.dma_start(to[:], src.bitcast(F32)).then_inc(S["rows_in"], 16)

            def load_bias(j, head):
                h, e = head_no(j, head), parity(head)
                wait_past(sp, S["chunk_out"], SLOTS * (h - 1))
                sp.dma_start(bias[e][:], t["nF_p"][bass.ds(h, 1), :].broadcast_to([P, SEQ])).then_inc(bias_in[e], 16)

            def load_v(j, head):
                h, e = head_no(j, head), parity(head)
                wait_past(sp, S["valued"], SLOTS * (h - 1))
                src = t["v_split"][0:SEQ, bass.ds(h, 1), :].rearrange("(n p) o d -> p (n o) d", p=P)
                sp.dma_start(v[e][:].bitcast(F32), src.bitcast(F32)).then_inc(v_in[e], 16)

            def swap(j, head):
                h, e = head_no(j, head), parity(head)
                sp.wait_ge(S["prepared"], 8 * h + 8)
                if head >= 2 or not isinstance(j, int) or j > 0:
                    sp.wait_ge(S["scored"], SLOTS * (h - 1))
                for a, b in ((0, HD), (HD, 0)):
                    sp.dma_start(kX[e][a:a + HD, :].bitcast(F32), kT[e][b:b + HD, :].bitcast(F32)).then_inc(swapped[e], 16)

            load_rows(0, 0)
            load_bias(0, 0)
            load_v(0, 0)
            load_bias(0, 1)
            swap(0, 0)
            load_rows(0, 1)
            swap(0, 1)

            def body(j, last):
                for what, n, _ in attention_steps(j, last):
                    if what == "load_rows":
                        load_rows(j, n)
                    elif what == "load_bias":
                        load_bias(j, n)
                    elif what == "load_v":
                        load_v(j, n)
                    elif what == "swap":
                        swap(j, n)
                    elif what == "divide":
                        s = n % 2
                        sp.wait_ge(S["divided"], block_no(j, n) + 1)
                        h = head_no(j, n // NB) if n >= 0 else 2 * j - 1
                        rows = bass.ds(POOL + HD * h, HD)
                        b = n % NB
                        sp.dma_start(t["mixT"][rows, QB * P * b:QB * P * (b + 1)], out[:, s, :]).then_inc(stored[s], 16)
            pairs(sp, body)
            for s in range(2):
                sp.wait_ge(stored[s], 16 * HEADS * NB // 2)

        @block.gpsimd
        def _(pool):
            pool.memset(ident[:], 0.0).then_inc(S["made"], 1)
            pool.memset(mask[:], 0.0).then_inc(S["made"], 1)
            pool.memset(pick[:], 1.0).then_inc(S["made"], 1)
            pool.wait_ge(S["made"], 3)
            pool.affine_select(out=ident[:], in_=ident[:], compare_op=ALU.not_equal, fill=1.0, base=0,
                               pattern=[[-1, P]], channel_multiplier=1).then_inc(S["consts"], 1)
            pool.affine_select(out=mask[:], in_=mask[:], compare_op=ALU.is_ge, fill=-1e30, base=0,
                               pattern=[[-1, P]], channel_multiplier=1).then_inc(S["consts"], 1)
            pool.affine_select(out=pick[:], in_=pick[:], compare_op=ALU.is_ge, fill=0.0, base=0,
                               pattern=[[-1, QB], [0, P]], channel_multiplier=1).then_inc(S["consts"], 1)
            pool.wait_ge(S["consts"], 3)
            for d in range(1, QB):
                pool.affine_select(out=pick[:], in_=pick[:], compare_op=ALU.not_equal, fill=0.0, base=-d,
                                   pattern=[[-1, QB], [0, P]], channel_multiplier=1).then_inc(S["consts"], 1)
                pool.wait_ge(S["consts"], 3 + d)
            for d in range(QB + 1, 2 * QB):
                pool.affine_select(out=pick[:], in_=pick[:], compare_op=ALU.not_equal, fill=0.0, base=-d,
                                   pattern=[[-1, QB], [0, P]], channel_multiplier=1).then_inc(S["consts"], 1)
                pool.wait_ge(S["consts"], 2 + d)

            def body(j, last):
                for what, n, _ in attention_steps(j, last):
                    if what == "inverse_turn":
                        m = block_no(j, n)
                        pool.wait_ge(S["invT_ready"], m + 1)
                        wait_past(pool, S["divisors"], m)
                        pool.tensor_tensor(spread[:], invT[:].unsqueeze(1).broadcast_to([2 * QB, QB, P]), pick[:],
                                           ALU.mult).then_inc(S["spread_ready"], 1)
                    elif what == "divide":
                        m = block_no(j, n)
                        pool.wait_ge(S["divisors_out"], m + 1)
                        pool.wait_ge(S["summed"], m + 1)
                        pool.tensor_tensor(out[:, n % 2, :], out[:, n % 2, :], both[:], ALU.mult).then_inc(S["divided"], 1)
            pairs(pool, body)

        @block.scalar
        def _(act):
            def prepare(j, head, g):
                h, e = head_no(j, head), parity(head)
                act.wait_ge(S["rows_turned"], 8 * h + g + 1)
                to, cols = (qT if g < 4 else kT)[e], slice(512 * (g % 4), 512 * (g % 4) + 512)
                if g == 0:
                    wait_past(act, S["scored"], SLOTS * (h - 1))
                if g == 4:
                    wait_past(act, swapped[e], 32 * pair_of(j, head))
                act.activation(to[:, cols], ps_x[:], ACT.Copy).then_inc(S["prepared"], 1)

            def exponential(j, idx, piece):
                i, c = CHUNKS_OF[idx % SLOTS]
                act.wait_ge(S["chunk_out"], number(j, idx) + 1)
                a, w = piece * PIECE, min((piece + 1) * PIECE, (i + 1) * P)
                p = probs[i // QB][:, i % QB, a:w]
                act.activation(p, p, ACT.Exp, scale=-1.0, bias=nmax[:, i, c:c + 1],
                               accum_out=total[:, i, piece:piece + 1]).then_inc(S["exped"], 1)

            def high(j, idx):
                n = number(j, idx)
                act.wait_ge(S["turned"], n + 1)
                wait_past(act, S["valued"], n - 3)
                a = P * diag_of(idx)
                act.activation(pT_hi[idx % 4][:, a:], ps_t[turn_bank(idx)][:, a:], ACT.Copy).then_inc(S["hi_ready"], 1)

            def step(j, what, n, g):
                if what == "prepare":
                    prepare(j, n, g)
                elif what == "exp":
                    exponential(j, n, g)
                elif what == "turn":
                    high(j, n)
                elif what == "sum":
                    m = block_no(j, n)
                    act.wait_ge(S["valued"], number(j, block_end(n)))
                    wait_past(act, S["summed"], m)
                    act.activation(rest[:], ps_o[n % 2][HD:P, :], ACT.Copy).then_inc(S["rest_ready"], 1)
                elif what == "divide":
                    m = block_no(j, n)
                    act.wait_ge(S["divisors"], m + 1)
                    wait_past(act, stored[n % 2], 16 * (NB * j + n // 2))
                    act.activation(out[:, n % 2, :], ps_x[0:HD, :], ACT.Copy).then_inc(S["divisors_out"], 1)
                elif what == "inverse_turn":
                    m = block_no(j, n)
                    act.wait_ge(S["inv_turned"], m + 1)
                    wait_past(act, S["spread_ready"], m)
                    act.activation(invT[:], ps_x[0:2 * QB, 0:P], ACT.Copy).then_inc(S["invT_ready"], 1)

            def body(j, last):
                for what, n, g in attention_steps(j, last):
                    step(j, what, n, g)
            act.wait_ge(S["ready"], 4)
            for what, n, g in lead_in():
                step(0, what, n, g)
            pairs(act, body)

        @block.vector
        def _(dve):
            def score(j, idx):
                i, c = CHUNKS_OF[idx % SLOTS]
                b, n, head = i // QB, number(j, idx), idx // SLOTS
                e = parity(head)
                if i % QB == 0 and c == 0:
                    before = SLOTS * (head_no(j, head) - 1) + block_start(b + 1)
                    wait_past(dve, S["turned"], before)
                    if b == 0:
                        dve.wait_ge(bias_in[e], 16 * (pair_of(j, head) + 1))
                if c:
                    dve.wait_ge(S["chunk_out"], n)
                dve.wait_ge(S["scored"], n + 1)
                dve.sem_inc(S["waited"], 1)
                x0, x1 = c * WIDE, min((c + 1) * WIDE, (i + 1) * P)
                dve.tensor_tensor_reduce(out=probs[b][:, i % QB, x0:x1], in0=ps_s[idx % 2][:, 0:x1 - x0],
                                         in1=bias[e][:, x0:x1], scale=-1.0,
                                         scalar=nmax[:, i, c - 1:c] if c else 3e38, op0=ALU.add, op1=ALU.min,
                                         accum_out=nmax[:, i, c:c + 1]).then_inc(S["chunk_out"], 1)

            def low(j, idx):
                n = number(j, idx)
                dve.wait_ge(S["hi_ready"], n + 1)
                a = P * diag_of(idx)
                dve.tensor_tensor(pT_lo[idx % 4][:, a:], ps_t[turn_bank(idx)][:, a:], pT_hi[idx % 4][:, a:].bitcast(F32),
                                  ALU.subtract).then_inc(S["lo_ready"], 1)

            def step(j, what, n, g):
                if what == "score":
                    score(j, n)
                elif what == "rest":
                    low(j, n)
                elif what == "sum":
                    m = block_no(j, n)
                    dve.wait_ge(S["rest_ready"], m + 1)
                    wait_past(dve, S["divided"], m)
                    dve.tensor_tensor(both[:], ps_o[n % 2][0:HD, :], rest[:], ALU.add).then_inc(S["summed"], 1)
                elif what == "inverse":
                    m, b = block_no(j, n), n % NB
                    if g:
                        dve.wait_ge(S["inv_chain"], 3 * m + g)
                    if g == 0:
                        dve.wait_ge(S["exped"], EXPS * head_no(j, n // NB) + exps_before(QB * (b + 1)))
                        wait_past(dve, S["inv2_ready"], m)
                        rows = slice(QB * b, QB * (b + 1))
                        dve.tensor_tensor(inv[:], total[:, rows, 0], total[:, rows, 1], ALU.add
                                          ).then_inc(S["inv_chain"], 1)
                    elif g == 1:
                        dve.reciprocal(inv[:], inv[:]).then_inc(S["inv_chain"], 1)
                    elif g == 2:
                        wait_past(dve, S["inv_turned"], m)
                        dve.tensor_copy(inv2[:, 0:QB], inv[:]).then_inc(S["inv_chain"], 1)
                    else:
                        dve.tensor_tensor(inv2[:, QB:], inv[:], inv2[:, 0:QB].bitcast(F32), ALU.subtract
                                          ).then_inc(S["inv2_ready"], 1)

            def body(j, last):
                for what, n, g in attention_steps(j, last):
                    step(j, what, n, g)
            dve.memset(total[:], 0.0).then_inc(S["ready"], 1)
            dve.wait_ge(S["consts"], 3)
            dve.tensor_scalar(ones[:], ident[0:2 * QB, :], 0.0, 1.0, ALU.mult, ALU.add).then_inc(S["ready"], 1)
            dve.tensor_copy(ident_r[:], ident[:]).then_inc(S["ready"], 1)
            dve.tensor_copy(mask_r[:], mask[:]).then_inc(S["ready"], 1)
            for what, n, g in lead_in():
                step(0, what, n, g)
            pairs(dve, body)

        @block.tensor
        def _(pe):
            def prepare(j, head, g):
                h = head_no(j, head)
                if g == 0:
                    pe.wait_ge(S["rows_in"], 32 * (h + 1))
                    if head >= 2:
                        pe.wait_ge(S["invT_ready"], block_no(j, NB * (head - 2) + NB - 1) + 1)
                wait_past(pe, S["prepared"], 8 * h + g)
                rows = (rows_q if g < 4 else rows_k)
                for i in range(4):
                    last = pe.transpose(ps_x[:, P * i:P * i + P], rows[:, 4 * (g % 4) + i, :], ident[:])
                last.then_inc(S["rows_turned"], 1)

            def score(j, idx):
                i, c = CHUNKS_OF[idx % SLOTS]
                n, head = number(j, idx), idx // SLOTS
                e = parity(head)
                if i == 0:
                    pe.wait_ge(S["prepared"], 8 * head_no(j, head) + 8)
                    pe.wait_ge(swapped[e], 32 * (pair_of(j, head) + 1))
                wait_past(pe, S["chunk_out"], n - 1)
                x0, x1 = c * WIDE, min((c + 1) * WIDE, (i + 1) * P)
                o = ps_s[idx % 2]
                q = qT[e][:, P * i:P * i + P]
                pe.matmul(o[:, 0:x1 - x0], q, kT[e][:, x0:x1], start=True, stop=False)
                if c == i // QB:
                    pe.matmul(o[:, x1 - x0 - P:x1 - x0], ident_r[:], mask_r[:], start=False, stop=False)
                pe.matmul(o[:, 0:x1 - x0], q, kX[e][:, x0:x1], start=False, stop=True).then_inc(S["scored"], 1)

            def turn(j, idx):
                n = number(j, idx)
                b, kt = TURNS_OF[idx % SLOTS]
                if kt == 0:
                    pe.wait_ge(S["exped"], EXPS * head_no(j, idx // SLOTS) + exps_before(QB * (b + 1)))
                wait_past(pe, S["lo_ready"], n + 1 - bank_reuse(idx))
                for q in range(diag_of(idx), QB):
                    last = pe.transpose(ps_t[turn_bank(idx)][:, P * q:P * q + P], probs[b][:, q, P * kt:P * kt + P], ident[:])
                last.then_inc(S["turned"], 1)

            def values(j, idx):
                n, head = number(j, idx), idx // SLOTS
                b, kt = TURNS_OF[idx % SLOTS]
                e = parity(head)
                blk = NB * head + b
                if kt == 0:
                    wait_past(pe, S["summed"], block_no(j, blk) - 1)
                    if b == 0:
                        pe.wait_ge(v_in[e], 16 * (pair_of(j, head) + 1))
                pe.wait_ge(S["lo_ready"], n + 1)
                a, o = P * diag_of(idx), ps_o[blk % 2]
                final = kt == QB * (b + 1) - 1
                pe.matmul(o[:, a:], v[e][:, kt, :], pT_hi[idx % 4][:, a:], start=(kt == 0), stop=False)
                pe.matmul(o[:, a:], v[e][:, kt, :], pT_lo[idx % 4][:, a:], start=False, stop=final).then_inc(S["valued"], 1)

            def step(j, last, what, n, g):
                if what == "prepare":
                    prepare(j, n, g)
                elif what == "score":
                    score(j, n)
                elif what == "turn":
                    turn(j, n)
                elif what == "values":
                    values(j, n)
                elif what == "inverse_turn":
                    m = block_no(j, n)
                    pe.wait_ge(S["inv2_ready"], m + 1)
                    wait_past(pe, S["divisors_out"], m)
                    if isinstance(m, int) and m == 0:
                        pe.wait_ge(S["prepared"], 16)
                    pe.transpose(ps_x[0:2 * QB, 0:P], inv2[:].bitcast(F32), ident[:]).then_inc(S["inv_turned"], 1)
                elif what == "divisors":
                    m = block_no(j, n)
                    pe.wait_ge(S["spread_ready"], m + 1)
                    if n % NB == NB - 1 and (not last or n < 0):
                        h = head_no(j, n // NB) if n >= 0 else 2 * j - 1
                        pe.wait_ge(S["prepared"], 8 * (h + 3))
                    pe.matmul(ps_x[:], ones[:], spread[:].rearrange("r q p -> r (q p)"), start=True, stop=True
                              ).then_inc(S["divisors"], 1)

            def body(j, last):
                for what, n, g in attention_steps(j, last):
                    step(j, last, what, n, g)
            pe.wait_ge(S["consts"], 2 * QB + 1)
            pe.wait_ge(S["ready"], 4)
            for what, n, g in lead_in():
                step(0, False, what, n, g)
            pairs(pe, body)


def stream_attention(nc, t, sems):
    PAIRS = HG // 2
    CT = PAST // P
    KEYS = PAST + NEW
    R = HG * NEW
    PR = 2 * NEW
    GROUPS = 2 * STREAMS
    with ExitStack() as ctx:
        sb = lambda name, shape, dt=F32: ctx.enter_context(nc.sbuf_tensor(name, shape, dt))
        qs = sb("s_q", [P, ATT])
        ks = sb("s_k", [P, ATT])
        qd = sb("s_qd", [P, HEADS // 2, STREAMS, PR])
        kn = sb("s_kn", [P, HEADS // 2, STREAMS * NEW])
        q_now = [sb(f"s_qn{i}", [P, PAIRS, PR]) for i in range(2)]
        k_now = [sb(f"s_kn{i}", [P, PAIRS, NEW]) for i in range(2)]
        k_rows = sb("s_krows", [P, 2, CT, QKV_W])
        v_rows = sb("s_vrows", [P, 2, CT, QKV_W])
        v_new = sb("s_vnew", [NEW, 2, QKV_W])
        kT = [sb(f"s_kT{i}", [P, PAIRS, PAST]) for i in range(2)]
        bias = sb("s_bias", [R, 2, KEYS])
        probs = sb("s_probs", [R, 2, KEYS])
        pT = sb("s_pT", [P, CT + 1, R])
        mask = sb("s_mask", [R, NEW])
        ident = sb("s_ident", [P, P])
        nmax = sb("s_nmax", [R, 2])
        total = sb("s_total", [R, 2])
        inv = sb("s_inv", [R, 2])
        o_sb = sb("s_o", [R, P])
        mix = sb("s_mix", [P, HEADS // 2, STREAMS, NEW])
        ps_k = [ctx.enter_context(nc.psum_tensor(f"s_psk{i}", [P, 4 * P], F32)) for i in range(2)]
        ps_s = ctx.enter_context(nc.psum_tensor("s_pss", [P, 3 * 512], F32))
        ps_p = [ctx.enter_context(nc.psum_tensor(f"s_psp{i}", [P, 4, P], F32)) for i in range(2)]
        ps_o = ctx.enter_context(nc.psum_tensor("s_pso", [P, 512], F32))

        names = ("waited waited_v new_in mask_in k_in0 k_in1 v_in0 v_in1 bias_in0 bias_in1 made consts qd_zero turned0 out0 "
                 "k_turned kT_act kT_dve now_ready scored bias_ready least exped inv_ready p_turned p_act p_dve "
                 "valued o_ready o_turned spread stored").split()
        S = {n: sems("s_" + n) for n in names}
        k_in, v_in, bias_in = ([S[f"{n}_in{i}"] for i in range(2)] for n in ("k", "v", "bias"))

        def groups(eng, body):
            body(0)
            body(1)
            with eng.Fori(2, STREAMS) as b:
                body(b)

        block = ctx.enter_context(nc.Block())

        @block.sync
        def _(sp):
            sp.dma_start(qs[:], t["q_nat"][SEQ:ROWS, :]).then_inc(S["new_in"], 16)
            sp.dma_start(ks[:], t["k_s"]).then_inc(S["new_in"], 16)
            sp.wait_ge(S["consts"], 2)
            for m in range(1, HG):
                sp.dma_start(mask[NEW * m:NEW * (m + 1), :], mask[0:NEW, :]).then_inc(S["mask_in"], 16)

            def body(b):
                for s in range(2):
                    g = 2 * b + s
                    wait_past(sp, S["k_turned"], 6 * (g - 1))
                    src = t["cache_k"][0, bass.ds(b, 1), :, s * HG:(s + 1) * HG, :]
                    sp.dma_start(k_rows[:, s], src.rearrange("o (n p) h d -> p (o n) (h d)", p=P)).then_inc(k_in[s], 16)
                    wait_past(sp, S["least"], g - 1)
                    for m in range(HG):
                        sp.dma_start(bias[NEW * m:NEW * (m + 1), s, :],
                                     t["nF_s"][bass.ds(b * HEADS + s * HG + m, 1), :].broadcast_to([NEW, KEYS])
                                     ).then_inc(bias_in[s], 16)
            groups(sp, body)
            sp.wait_ge(S["spread"], GROUPS)
            sp.dma_start(t["mixT"][POOL:D, SEQ:ROWS].rearrange("(a p) n -> p a n", p=P),
                         mix[:].rearrange("p a b n -> p a (b n)")).then_inc(S["stored"], 16)
            sp.wait_ge(S["stored"], 16)

        @block.gpsimd
        def _(pool):
            pool.memset(mask[:], 0.0).then_inc(S["made"], 1)
            pool.memset(ident[:], 0.0).then_inc(S["made"], 1)
            pool.memset(qd[:], 0.0).then_inc(S["qd_zero"], 1)
            pool.wait_ge(S["made"], 2)
            pool.affine_select(out=mask[0:NEW, :], in_=mask[0:NEW, :], compare_op=ALU.is_ge, fill=-1e30, base=0,
                               pattern=[[-1, NEW]], channel_multiplier=1).then_inc(S["consts"], 1)
            pool.affine_select(out=ident[:], in_=ident[:], compare_op=ALU.not_equal, fill=1.0, base=0,
                               pattern=[[-1, P]], channel_multiplier=1).then_inc(S["consts"], 1)
            pool.wait_ge(S["mask_in"], 16 * (HG - 1))

            def body(b):
                for s in range(2):
                    g = 2 * b + s
                    cols = slice(s * QKV_W, (s + 1) * QKV_W)
                    if not (isinstance(b, int) and b == 0):
                        pool.wait_ge(S["valued"], g - 1)
                        pool.sem_inc(S["waited_v"], 1)
                    src = t["cache_v"][0, bass.ds(b, 1), :, s * HG:(s + 1) * HG, :]
                    pool.dma_start(v_rows[:, s], src.rearrange("o (n p) h d -> p (o n) (h d)", p=P)).then_inc(v_in[s], 16)
                    pool.dma_start(v_new[:, s], t["v_s"][bass.ds(b * NEW, NEW), cols]).then_inc(v_in[s], 16)
                    pool.wait_ge(bias_in[s], 16 * HG * (b + 1))
                    pool.tensor_tensor(bias[:, s, PAST:KEYS], bias[:, s, PAST:KEYS], mask[:], ALU.add
                                       ).then_inc(S["bias_ready"], 1)
            groups(pool, body)

        @block.scalar
        def _(act):
            def soft(g, s):
                act.wait_ge(S["least"], g + 1)
                act.activation(probs[:, s, :], probs[:, s, :], ACT.Exp, scale=-1.0, bias=nmax[:, s:s + 1],
                               accum_out=total[:, s:s + 1]).then_inc(S["exped"], 1)

            def keys(g, s):
                wait_past(act, S["scored"], g - 1)
                for u in range(0, 6, 2):
                    act.wait_ge(S["k_turned"], 6 * g + u + 1)
                    act.activation(kT[s][:, u // 2, 0:512], ps_k[0][:], ACT.Copy).then_inc(S["kT_act"], 1)

            def values(g, s):
                wait_past(act, S["valued"], g)
                act.wait_ge(S["p_turned"], 3 * g + 1)
                act.activation(pT[:, 0:4, :], ps_p[0][:, :, 0:R], ACT.Copy).then_inc(S["p_act"], 1)
                act.wait_ge(S["p_turned"], 3 * g + 3)
                act.activation(pT[0:NEW, CT, :], ps_p[0][0:NEW, 0, 0:R], ACT.Copy).then_inc(S["p_act"], 1)

            def divide(g, s):
                act.wait_ge(S["valued"], g + 1)
                act.wait_ge(S["inv_ready"], g + 1)
                wait_past(act, S["o_turned"], g)
                act.activation(o_sb[:], ps_o[0:R, 0:P], ACT.Copy, scale=inv[:, s:s + 1]).then_inc(S["o_ready"], 1)

            def body(b):
                for s in range(2):
                    g = 2 * b + s
                    keys(g, s)
                    if not (isinstance(b, int) and b == 0):
                        divide(g - 2, s)
                    if not (isinstance(b, int) and b == 0 and s == 0):
                        values(g - 1, 1 - s)
                    soft(g, s)
            groups(act, body)
            divide(GROUPS - 2, 0)
            values(GROUPS - 1, 1)
            divide(GROUPS - 1, 1)

        @block.vector
        def _(dve):
            def keys(g, b, s):
                wait_past(dve, S["scored"], g - 1)
                a = slice(PAIRS * s, PAIRS * (s + 1))
                dve.tensor_copy(q_now[s][:], qd[:, a, bass.ds(b, 1), :].rearrange("p a o r -> p a (o r)"))
                dve.tensor_copy(k_now[s][:], kn[:, a, bass.ds(b * NEW, NEW)]).then_inc(S["now_ready"], 1)
                for u in range(1, 6, 2):
                    dve.wait_ge(S["k_turned"], 6 * g + u + 1)
                    dve.tensor_copy(kT[s][:, u // 2, 512:1024], ps_k[1][:]).then_inc(S["kT_dve"], 1)

            def soft(g, s):
                dve.wait_ge(S["scored"], g + 1)
                dve.wait_ge(S["bias_ready"], g + 1)
                wait_past(dve, S["p_turned"], 3 * (g - 1))
                dve.sem_inc(S["waited"], 1)
                dve.tensor_tensor_reduce(out=probs[:, s, :], in0=ps_s[0:R, 0:KEYS], in1=bias[:, s, :], scale=-1.0,
                                         scalar=3e38, op0=ALU.add, op1=ALU.min, accum_out=nmax[:, s:s + 1]
                                         ).then_inc(S["least"], 1)

            def values(g, s):
                dve.wait_ge(S["exped"], g + 1)
                dve.reciprocal(inv[:, s:s + 1], total[:, s:s + 1]).then_inc(S["inv_ready"], 1)
                wait_past(dve, S["valued"], g)
                dve.wait_ge(S["p_turned"], 3 * g + 2)
                dve.tensor_copy(pT[:, 4:8, :], ps_p[1][:, :, 0:R]).then_inc(S["p_dve"], 1)

            def spread(g, b, s):
                dve.wait_ge(S["o_turned"], g + 1)
                src = ps_o[:, P:P + R].rearrange("p (a h q) -> p a h q", a=PAIRS, h=2)
                a = slice(PAIRS * s, PAIRS * (s + 1))
                for h in range(2):
                    part = slice(HD * h, HD * h + HD)
                    last = dve.tensor_copy(mix[part, a, bass.ds(b, 1), :].rearrange("p a o q -> p a (o q)"),
                                           src[part, :, h, :])
                last.then_inc(S["spread"], 1)

            for n in range(2):
                for half in range(2):
                    m = 2 * n + half
                    dve.wait_ge(S["turned0"], m + 1)
                    a = slice(PAIRS * half, PAIRS * (half + 1))
                    bank = ps_k[m % 2][:, 0:PAIRS * P].rearrange("p (a b r) -> p a b r", a=PAIRS, b=STREAMS)
                    if n == 0:
                        if half == 0:
                            dve.wait_ge(S["qd_zero"], 1)
                        for h in range(2):
                            part = slice(HD * h, HD * h + HD)
                            last = dve.tensor_copy(qd[part, a, :, NEW * h:NEW * (h + 1)], bank[part])
                    else:
                        last = dve.tensor_copy(kn[:, a, :].rearrange("p a (b r) -> p a b r", b=STREAMS), bank)
                    last.then_inc(S["out0"], 1)
            dve.wait_ge(S["out0"], 4)

            def body(b):
                for s in range(2):
                    g = 2 * b + s
                    keys(g, b, s)
                    soft(g, s)
                    if not (isinstance(b, int) and b == 0):
                        spread(g - 2, b - 1, s)
                    if not (isinstance(b, int) and b == 0 and s == 0):
                        values(g - 1, 1 - s)
            groups(dve, body)
            spread(GROUPS - 2, STREAMS - 1, 0)
            values(GROUPS - 1, 1)
            spread(GROUPS - 1, STREAMS - 1, 1)

        @block.tensor
        def _(pe):
            def keys(g, b, s):
                pe.wait_ge(k_in[s], 16 * (b + 1))
                for u in range(6):
                    a, part = u // 2, u % 2
                    wait_past(pe, S["kT_dve" if part else "kT_act"], 3 * g + a)
                    for i in range(4):
                        last = pe.transpose(ps_k[part][:, P * i:P * i + P],
                                            k_rows[:, s, 4 * part + i, P * a:P * a + P], ident[:])
                    last.then_inc(S["k_turned"], 1)

            def scores(g, s):
                pe.wait_ge(S["kT_act"], 3 * g + 3)
                pe.wait_ge(S["kT_dve"], 3 * g + 3)
                pe.wait_ge(S["now_ready"], g + 1)
                wait_past(pe, S["least"], g)
                for x0, x1 in ((0, 512), (512, 1024), (1024, KEYS)):
                    for a in range(PAIRS):
                        rhs = kT[s][:, a, x0:x1] if x1 <= PAST else k_now[s][:, a, :]
                        last = pe.matmul(ps_s[PR * a:PR * a + PR, x0:x1], q_now[s][:, a, :], rhs, start=True, stop=True,
                                         tile_position=(0, PR * a))
                last.then_inc(S["scored"], 1)

            def turn(g, s):
                pe.wait_ge(S["exped"], g + 1)
                wait_past(pe, S["p_act"], 2 * g)
                for i in range(4):
                    last = pe.transpose(ps_p[0][:, i, 0:R], probs[:, s, P * i:P * i + P], ident[0:R, 0:R])
                last.then_inc(S["p_turned"], 1)
                wait_past(pe, S["p_dve"], g)
                for i in range(4):
                    last = pe.transpose(ps_p[1][:, i, 0:R], probs[:, s, P * (4 + i):P * (5 + i)], ident[0:R, 0:R])
                last.then_inc(S["p_turned"], 1)
                pe.wait_ge(S["p_act"], 2 * g + 1)
                pe.transpose(ps_p[0][0:NEW, 0, 0:R], probs[:, s, PAST:KEYS], ident[0:R, 0:R]).then_inc(S["p_turned"], 1)

            def values(g, b, s):
                pe.wait_ge(v_in[s], 32 * (b + 1))
                pe.wait_ge(S["p_dve"], g + 1)
                pe.wait_ge(S["p_act"], 2 * g + 2)
                wait_past(pe, S["spread"], g)
                for i in range(CT + 1):
                    for a in range(PAIRS):
                        m = P if i < CT else NEW
                        rhs = v_rows[:, s, i, P * a:P * a + P] if i < CT else v_new[:, s, P * a:P * a + P]
                        last = pe.matmul(ps_o[PR * a:PR * a + PR, 0:P], pT[0:m, i, PR * a:PR * a + PR], rhs,
                                         start=(i == 0), stop=(i == CT), tile_position=(0, PR * a))
                last.then_inc(S["valued"], 1)

            def turn_out(g):
                pe.wait_ge(S["o_ready"], g + 1)
                pe.transpose(ps_o[:, P:P + R], o_sb[:], ident[0:R, 0:R]).then_inc(S["o_turned"], 1)

            pe.wait_ge(S["consts"], 2)
            pe.wait_ge(S["new_in"], 32)
            for n, rows in enumerate((qs, ks)):
                for half in range(2):
                    m = 2 * n + half
                    wait_past(pe, S["out0"], m - 1)
                    for a in range(PAIRS):
                        pair = PAIRS * half + a
                        last = pe.transpose(ps_k[m % 2][:, P * a:P * a + P], rows[:, P * pair:P * pair + P], ident[:])
                    last.then_inc(S["turned0"], 1)
            pe.wait_ge(S["out0"], 4)

            def body(b):
                for s in range(2):
                    g = 2 * b + s
                    keys(g, b, s)
                    if not (isinstance(b, int) and b == 0):
                        values(g - 2, b - 1, s)
                    scores(g, s)
                    if not (isinstance(b, int) and b == 0):
                        turn_out(g - 2)
                    if not (isinstance(b, int) and b == 0 and s == 0):
                        turn(g - 1, 1 - s)
            groups(pe, body)
            values(GROUPS - 2, STREAMS - 1, 0)
            turn_out(GROUPS - 2)
            turn(GROUPS - 1, 1)
            values(GROUPS - 1, STREAMS - 1, 1)
            turn_out(GROUPS - 1)


def out_projection(nc, t, sems):
    N = QT + 1
    HALVES, W = 2, 512
    with ExitStack() as ctx:
        sb = lambda name, shape, dt=F32: ctx.enter_context(nc.sbuf_tensor(name, shape, dt))
        w_raw = sb("out_wraw", [P, 2, D])
        w_hi = sb("out_whi", [P, KT, D], F32R)
        w_lo = sb("out_wlo", [P, KT, D], F32R)
        m = [sb(f"out_m{i}", [P, KT, P]) for i in range(2)]
        m_hi = [sb(f"out_mhi{i}", [P, KT, P], F32R) for i in range(2)]
        m_lo = [sb(f"out_mlo{i}", [P, KT, P], F32R) for i in range(2)]
        x = sb("out_x", [P, 2, D])
        x2 = sb("out_x2", [P, 2, D])
        h = sb("out_h", [P, 2, D])
        hT_hi = [sb(f"out_hThi{i}", [P, KT, P], F32R) for i in range(2)]
        hT_lo = [sb(f"out_hTlo{i}", [P, KT, P], F32R) for i in range(2)]
        mod2 = sb("out_mod", [P, 2, 3 * D])
        gate, shift, scale = (mod2[:, :, i * D:(i + 1) * D] for i in range(3))
        ssq = sb("out_ssq", [P, 2])
        rstd = sb("out_rstd", [P, 2])
        eps = sb("out_eps", [P, 1])
        ident = sb("out_ident", [P, P])
        ps_o = [ctx.enter_context(nc.psum_tensor(f"out_pso{i}", [P, D], F32)) for i in range(2)]
        ps_t = [ctx.enter_context(nc.psum_tensor(f"out_pst{i}", [P, KT, P], F32)) for i in range(2)]

        waited = sems("out_waited")
        consts_in, eps_ready = sems("out_consts_in"), sems("out_eps_ready")
        ident0, ident_ready = sems("out_ident0"), sems("out_ident_ready")
        w_in = [sems(f"out_w_in{i}") for i in range(2)]
        w_hi_ready, w_ready = sems("out_w_hi_ready"), sems("out_w_ready")
        m_in = [sems(f"out_m_in{i}") for i in range(2)]
        x_in = [sems(f"out_x_in{i}") for i in range(2)]
        m_hi_ready, m_ready, projected = sems("out_m_hi_ready"), sems("out_m_ready"), sems("out_projected")
        gated, x2_ready, squared, rms_ready = sems("out_gated"), sems("out_x2_ready"), sems("out_squared"), sems("out_rms_ready")
        rstd_ready, h_scaled, h_ready = sems("out_rstd_ready"), sems("out_h_scaled"), sems("out_h_ready")
        hT_psum, hT_hi_ready, hT_ready = sems("out_hT_psum"), sems("out_hT_hi_ready"), sems("out_hT_ready")
        x2_stored = [sems(f"out_x2_stored{i}") for i in range(2)]
        hT_stored = [sems(f"out_hT_stored{i}") for i in range(2)]

        def number(i, k):
            return 2 * i + k

        def uses(i, k):
            return i + k // 2

        def rows(i, k):
            n = number(i, k)
            return slice(n * P, (n + 1) * P) if isinstance(n, int) else bass.ds(n * P, P)

        def exists(i, k):
            return not isinstance(i, int) or number(i, k) < N

        def which(i, k):
            return 1 if isinstance(i, int) and number(i, k) == N - 1 else 0

        def over_tiles(eng, step):
            for k in range(2):
                step(0, k)
            with eng.Fori(1, N // 2 - 2) as i:
                for k in range(2):
                    step(i, k)
            for k in range(2):
                step(N // 2 - 2, k)
            for k in range(3):
                step(N // 2 - 1, k)

        block = ctx.enter_context(nc.Block())

        @block.sync
        def _(sp):
            def load_mix(i, k):
                wait_past(sp, m_ready, number(i, k) - 1)
                src = t["mixT"].rearrange("(k p) r -> p k r", p=P)
                sp.dma_start(m[k % 2][:], src[:, :, rows(i, k)]).then_inc(m_in[k % 2], 16)

            def load_x(i, k):
                wait_past(sp, x2_ready, number(i, k) - 1)
                if which(i, k):
                    src = t["x_sample"].rearrange("b n d -> (b n) d")
                else:
                    src = t["x_prompt"][0, rows(i, k), :]
                sp.dma_start(x[:, k % 2, :], src).then_inc(x_in[k % 2], 16)

            def store_x2(i, k):
                sp.wait_ge(x2_ready, number(i, k) + 1)
                sp.dma_start(t["x2"][rows(i, k), :], x2[:, k % 2, :]).then_inc(x2_stored[k % 2], 16)

            def store_hT(i, k):
                sp.wait_ge(hT_ready, number(i, k) + 1)
                sp.sem_inc(waited, 1)
                for name, part in (("h2T_hi", hT_hi), ("h2T_lo", hT_lo)):
                    dst = t[name].rearrange("(k p) r -> p k r", p=P).bitcast(F32)
                    sp.dma_start(dst[:, :, rows(i, k)], part[k % 2][:].bitcast(F32)).then_inc(hT_stored[k % 2], 16)

            load_mix(0, 0)
            for k in range(2):
                sp.dma_start(w_raw[:, k, :], t["w_out"][0, k * P:(k + 1) * P, :]).then_inc(w_in[k], 16)
            load_x(0, 0)
            load_mix(0, 1)
            for k in range(2, KT):
                sp.wait_ge(w_ready, k - 1)
                sp.dma_start(w_raw[:, k % 2, :], t["w_out"][0, k * P:(k + 1) * P, :]).then_inc(w_in[k % 2], 16)
            sp.dma_start(mod2[:, 0, :], t["mod"][0:1, 2 * D:5 * D].broadcast_to([P, 3 * D])).then_inc(consts_in, 16)
            for s in range(STREAMS):
                sp.dma_start(mod2[NEW * s:NEW * (s + 1), 1, :],
                             t["mod"][1 + s:2 + s, 2 * D:5 * D].broadcast_to([NEW, 3 * D])).then_inc(consts_in, 16)
            load_x(0, 1)
            store_x2(0, 0)

            load_mix(0, 2)
            load_x(0, 2)

            def step(i, k):
                if exists(i, k + 3):
                    load_mix(i, k + 3)
                    load_x(i, k + 3)
                if exists(i, k + 1):
                    store_x2(i, k + 1)
                store_hT(i, k)
            over_tiles(sp, step)
            for s in range(2):
                tiles = (N + 1 - s) // 2
                sp.wait_ge(x2_stored[s], 16 * tiles)
                sp.wait_ge(hT_stored[s], 32 * tiles)

        @block.gpsimd
        def _(pool):
            pool.memset(ident[:], 0.0).then_inc(ident0, 1)
            pool.wait_ge(ident0, 1)
            pool.affine_select(out=ident[:], in_=ident[:], compare_op=ALU.not_equal, fill=1.0, base=0,
                               pattern=[[-1, P]], channel_multiplier=1).then_inc(ident_ready, 1)

        @block.scalar
        def _(act):
            def split_mix(i, k):
                act.wait_ge(m_in[k % 2], 16 * (uses(i, k) + 1))
                wait_past(act, projected, number(i, k) - 1)
                act.activation(m_hi[k % 2][:], m[k % 2][:], ACT.Copy).then_inc(m_hi_ready, 1)

            def norm(i, k):
                n, s = number(i, k), k % 2
                act.wait_ge(x2_ready, n + 1)
                wait_past(act, hT_psum, n - 1)
                act.activation(h[:, s, :], x2[:, s, :], ACT.Square, accum_out=ssq[:, s:s + 1]).then_inc(squared, 1)
                act.wait_ge(squared, n + 1)
                act.activation(rstd[:, s:s + 1], ssq[:, s:s + 1], ACT.Sqrt, scale=1.0 / D, bias=eps[:]).then_inc(rms_ready, 1)

            def transposed(i, k):
                n, s = number(i, k), k % 2
                act.wait_ge(hT_psum, n + 1)
                if not (isinstance(i, int) and n < 2):
                    act.wait_ge(hT_stored[s], 32 * uses(i, k))
                act.activation(hT_hi[s][:], ps_t[s][:], ACT.Copy).then_inc(hT_hi_ready, 1)

            split_mix(0, 0)
            for k in range(KT):
                act.wait_ge(w_in[k % 2], 16 * (k // 2 + 1))
                act.activation(w_hi[:, k, :], w_raw[:, k % 2, :], ACT.Copy).then_inc(w_hi_ready, 1)
            split_mix(0, 1)
            act.wait_ge(eps_ready, 1)
            norm(0, 0)

            def step(i, k):
                if exists(i, k + 2):
                    split_mix(i, k + 2)
                if exists(i, k + 1):
                    norm(i, k + 1)
                transposed(i, k)
            over_tiles(act, step)

        @block.vector
        def _(dve):
            def split_mix(i, k):
                s = k % 2
                dve.wait_ge(m_hi_ready, number(i, k) + 1)
                dve.tensor_tensor(m_lo[s][:], m[s][:], m_hi[s][:].bitcast(F32), ALU.subtract).then_inc(m_ready, 1)

            def residual(i, k):
                n, s = number(i, k), k % 2
                dve.wait_ge(projected, n + 1)
                if not (isinstance(i, int) and n < 2):
                    dve.wait_ge(x2_stored[s], 16 * uses(i, k))
                    dve.wait_ge(squared, n - 1)
                dve.tensor_tensor(x2[:, s, :], ps_o[s][:], gate[:, which(i, k), :], ALU.mult).then_inc(gated, 1)
                dve.wait_ge(gated, n + 1)
                dve.wait_ge(x_in[s], 16 * (uses(i, k) + 1))
                dve.tensor_tensor(x2[:, s, :], x2[:, s, :], x[:, s, :], ALU.add).then_inc(x2_ready, 1)

            def norm(i, k):
                n, s = number(i, k), k % 2
                dve.wait_ge(rms_ready, n + 1)
                dve.reciprocal(rstd[:, s:s + 1], rstd[:, s:s + 1]).then_inc(rstd_ready, 1)
                dve.wait_ge(rstd_ready, n + 1)
                dve.scalar_tensor_tensor(h[:, s, :], x2[:, s, :], rstd[:, s:s + 1], scale[:, which(i, k), :],
                                         ALU.mult, ALU.mult).then_inc(h_scaled, 1)
                dve.wait_ge(h_scaled, n + 1)
                dve.tensor_tensor(h[:, s, :], h[:, s, :], shift[:, which(i, k), :], ALU.add).then_inc(h_ready, 1)

            def transposed(i, k):
                s = k % 2
                dve.wait_ge(hT_hi_ready, number(i, k) + 1)
                dve.tensor_tensor(hT_lo[s][:], ps_t[s][:], hT_hi[s][:].bitcast(F32), ALU.subtract).then_inc(hT_ready, 1)

            dve.memset(eps[:], EPS).then_inc(eps_ready, 1)
            split_mix(0, 0)
            for k in range(KT):
                dve.wait_ge(w_hi_ready, k + 1)
                dve.tensor_tensor(w_lo[:, k, :], w_raw[:, k % 2, :], w_hi[:, k, :].bitcast(F32),
                                  ALU.subtract).then_inc(w_ready, 1)
            split_mix(0, 1)
            dve.wait_ge(consts_in, 16 * (1 + STREAMS))
            residual(0, 0)
            norm(0, 0)

            def step(i, k):
                if exists(i, k + 2):
                    split_mix(i, k + 2)
                if exists(i, k + 1):
                    residual(i, k + 1)
                    norm(i, k + 1)
                transposed(i, k)
            over_tiles(dve, step)

        @block.tensor
        def _(pe):
            def project(i, k):
                n, s = number(i, k), k % 2
                pe.wait_ge(m_ready, n + 1)
                wait_past(pe, gated, n - 1)
                for c in range(KT):
                    if isinstance(i, int) and n == 0:
                        pe.wait_ge(w_ready, c + 1)
                    for j, (a, w) in enumerate(((m_hi, w_hi), (m_hi, w_lo), (m_lo, w_hi))):
                        for half in range(HALVES):
                            cols = slice(half * W, (half + 1) * W)
                            last = pe.matmul(ps_o[s][:, cols], a[s][:, c, :], w[:, c, cols],
                                             start=(c == 0 and j == 0), stop=(c == KT - 1 and j == 2))
                last.then_inc(projected, 1)

            def transpose(i, k):
                n, s = number(i, k), k % 2
                pe.wait_ge(h_ready, n + 1)
                wait_past(pe, hT_ready, n - 1)
                for c in range(KT):
                    last = pe.transpose(ps_t[s][:, c, :], h[:, s, c * P:(c + 1) * P], ident[:])
                last.then_inc(hT_psum, 1)

            pe.wait_ge(ident_ready, 1)
            project(0, 0)

            def step(i, k):
                if exists(i, k + 1):
                    project(i, k + 1)
                transpose(i, k)
            over_tiles(pe, step)


def channel_mixing(nc, t, sems):
    NB, RB = 4, ROWS // 4
    HW = RB // 2
    G = 2
    STEPS = FF // P // G
    PIECES = [(0, P), (P, P), (2 * P, P), (3 * P, RB - 4 * P), (RB - P, P)]
    NPC = len(PIECES)
    USES = STEPS * KT + NPC
    CREDIT = KT + 1
    EARLY = 3
    PARTS = 4
    with ExitStack() as ctx:
        sb = lambda name, shape, dt=F32: ctx.enter_context(nc.sbuf_tensor(name, shape, dt))
        hT = [sb(f"c_hT{i}", [P, KT, RB], F32R) for i in range(2)]
        up_raw = sb("c_up_raw", [P, KT, G * P])
        up_hi = [sb(f"c_up_hi{i}", [P, KT, G * P], F32R) for i in range(2)]
        up_lo = [sb(f"c_up_lo{i}", [P, KT, G * P], F32R) for i in range(2)]
        dn_raw = sb("c_dn_raw", [P, G, D])
        dn_hi = [sb(f"c_dn_hi{i}", [P, G, D], F32R) for i in range(2)]
        dn_lo = [sb(f"c_dn_lo{i}", [P, G, D], F32R) for i in range(2)]
        r = sb("c_relu", [P, G, RB])
        a_hi = [sb(f"c_a_hi{i}", [P, G, RB], F32R) for i in range(2)]
        a_lo = [sb(f"c_a_lo{i}", [P, G, RB], F32R) for i in range(2)]
        ffT = sb("c_ffT", [P, KT, RB])
        x2 = sb("c_x2", [P, NPC, D])
        gated = sb("c_gated", [P, 2, D])
        gate = sb("c_gate", [P, 2, D])
        ident = sb("c_ident", [P, P])
        ps_u = [ctx.enter_context(nc.psum_tensor(f"c_psu{i}", [P, 2, 512], F32)) for i in range(G)]
        ps_d = [ctx.enter_context(nc.psum_tensor(f"c_psd{i}", [P, 2, 512], F32)) for i in range(2)]

        gates_in, ident0, ident_ready = sems("c_gates_in"), sems("c_ident0"), sems("c_ident_ready")
        hT_in = [sems(f"c_hT_in{i}") for i in range(PARTS)]
        waited = sems("c_waited")
        up_in, dn_in = sems("c_up_in"), sems("c_dn_in")
        up_hi_ready, up_ready = sems("c_up_hi_ready"), sems("c_up_ready")
        dn_hi_ready, dn_ready = sems("c_dn_hi_ready"), sems("c_dn_ready")
        up_done = sems("c_up_done")
        relu_done, squared, a_hi_ready = sems("c_relu_done"), sems("c_squared"), sems("c_a_hi_ready")
        a_ready = sems("c_a_ready")
        down_done = sems("c_down_done")
        dn_free = sems("c_dn_free")
        zeroed = sems("c_zeroed")
        ff_transposed, y_ready = sems("c_ff_transposed"), sems("c_y_ready")
        x2_in, y_stored = sems("c_x2_in"), sems("c_y_stored")

        def over_blocks(eng, body):
            with eng.Fori(0, NB - 1) as b:
                body(b, False)
            body(NB - 1, True)

        def over_steps(eng, b, unit):
            with eng.Fori(0, STEPS // 2 - 1) as i:
                for p in range(2):
                    unit(b * STEPS + 2 * i + p, p)

        block = ctx.enter_context(nc.Block())

        @block.sync
        def _(sp):
            def load_hT(b):
                for k in (slice(i, i + KT // PARTS) for i in range(0, KT, KT // PARTS)):
                    for part, name in ((0, "h2T_hi"), (1, "h2T_lo")):
                        src = t[name].rearrange("(k p) r -> p k r", p=P).bitcast(F32)
                        cols = slice(b * RB, (b + 1) * RB) if isinstance(b, int) else bass.ds(b * RB, RB)
                        sp.dma_start(hT[part][:, k, :].bitcast(F32), src[:, k, cols]).then_inc(hT_in[k.start // (KT // PARTS)], 16)

            def load_up(S, s):
                wait_past(sp, up_ready, S)
                cols = slice(s * G * P, (s + 1) * G * P) if isinstance(s, int) else bass.ds(s * G * P, G * P)
                sp.dma_start(up_raw[:], t["w_up"][0].rearrange("(k p) f -> p k f", p=P)[:, :, cols]
                             ).then_inc(up_in, 16)

            def load_down(S, s):
                wait_past(sp, dn_ready, S)
                rws = slice(s * G * P, (s + 1) * G * P) if isinstance(s, int) else bass.ds(s * G * P, G * P)
                sp.dma_start(dn_raw[:], t["w_down"][0][rws, :].rearrange("(g p) d -> p g d", p=P)
                             ).then_inc(dn_in, 16)

            load_up(0, 0)
            load_hT(0)
            sp.dma_start(gate[:, 0, :], t["mod"][0:1, 5 * D:].broadcast_to([P, D])).then_inc(gates_in, 16)
            for s in range(STREAMS):
                sp.dma_start(gate[NEW * s:NEW * (s + 1), 1, :],
                             t["mod"][1 + s:2 + s, 5 * D:].broadcast_to([NEW, D])).then_inc(gates_in, 16)
            load_up(1, 1)
            load_down(0, 0)

            def body(b, last):
                with sp.Fori(0, STEPS // 2 - 1) as i:
                    for p in range(2):
                        s = 2 * i + p
                        load_up(b * STEPS + s + 2, s + 2)
                        load_down(b * STEPS + s + 1, s + 1)
                first = (b + 1) * STEPS
                if not last:
                    load_up(first, 0)
                load_down(first - 1, STEPS - 1)
                if not last:
                    sp.wait_ge(up_done, G * first)
                    load_hT(b + 1)
                    load_up(first + 1, 1)
                    load_down(first, 0)
            over_blocks(sp, body)

        @block.gpsimd
        def _(pool):
            def load_x2(b):
                for q, (off, w) in enumerate(PIECES):
                    pool.dma_start(x2[0:w, q, :], t["x2"][bass.ds(b * RB + off, w), :]).then_inc(x2_in, 16)

            pool.memset(ident[:], 0.0).then_inc(ident0, 1)
            pool.wait_ge(ident0, 1)
            pool.affine_select(out=ident[:], in_=ident[:], compare_op=ALU.not_equal, fill=1.0, base=0,
                               pattern=[[-1, P]], channel_multiplier=1).then_inc(ident_ready, 1)
            pool.memset(ffT[:], 0.0).then_inc(zeroed, 1)
            load_x2(0)

            def body(b, last):
                pool.wait_ge(x2_in, 16 * NPC * (b + 1))
                for q, (off, w) in enumerate(PIECES):
                    pool.wait_ge(dn_free, USES * b + STEPS * KT + q + 1 + CREDIT)
                    pool.tensor_tensor(x2[0:w, q, :], x2[0:w, q, :], gated[0:w, q % 2, :], ALU.add).then_inc(y_ready, 1)
                    pool.wait_ge(y_ready, NPC * b + q + 1)
                    if last and q == NPC - 1:
                        dst = t["y_sample"].rearrange("b n d -> (b n) d")
                    else:
                        dst = t["y_prompt"][0, bass.ds(b * RB + off, w), :]
                    pool.dma_start(dst, x2[0:w, q, :]).then_inc(y_stored, 16)
                if not last:
                    pool.wait_ge(ff_transposed, NPC * (b + 1))
                    pool.sem_inc(waited, 1)
                    pool.memset(ffT[:], 0.0).then_inc(zeroed, 1)
                pool.wait_ge(y_stored, 16 * NPC * (b + 1))
                if not last:
                    load_x2(b + 1)
            over_blocks(pool, body)

        @block.scalar
        def _(act):
            def split_up(S, p):
                act.wait_ge(up_in, 16 * (S + 1))
                wait_past(act, up_done, G * (S - 1))
                act.activation(up_hi[p][:], up_raw[:], ACT.Copy).then_inc(up_hi_ready, 1)

            def split_down(S, p):
                act.wait_ge(dn_in, 16 * (S + 1))
                if not isinstance(S, int) or S > 0:
                    act.wait_ge(down_done, KT * (S - 1) + 1)
                act.activation(dn_hi[p][:], dn_raw[:], ACT.Copy).then_inc(dn_hi_ready, 1)

            def relu_squared(S, p, g):
                n = G * S + g
                act.wait_ge(up_done, n + 1)
                if not isinstance(S, int) or S > 0:
                    act.wait_ge(a_ready, n - G + 1)
                act.activation(r[:, g, :].rearrange("p (h n) -> p h n", h=2), ps_u[g][:, :, 0:HW],
                               ACT.Relu).then_inc(relu_done, 1)
                act.wait_ge(relu_done, n + 1)
                act.activation(r[:, g, :], r[:, g, :], ACT.Square).then_inc(squared, 1)
                act.wait_ge(squared, n + 1)
                if not isinstance(S, int) or S > 0:
                    act.wait_ge(down_done, KT * (S - 1) + 1)
                act.activation(a_hi[p][:, g, :], r[:, g, :], ACT.Copy).then_inc(a_hi_ready, 1)

            split_up(0, 0)
            split_up(1, 1)
            split_down(0, 0)
            for g in range(G):
                relu_squared(0, 0, g)

            def unit(S, p):
                split_up(S + 2, p)
                relu_squared(S + 1, 1 - p, 0)
                split_down(S + 1, 1 - p)
                relu_squared(S + 1, 1 - p, 1)

            def body(b, last):
                over_steps(act, b, unit)
                S = (b + 1) * STEPS - 2
                if not last:
                    split_up(S + 2, 0)
                relu_squared(S + 1, 1, 0)
                split_down(S + 1, 1)
                relu_squared(S + 1, 1, 1)
                if not last:
                    split_up(S + 3, 1)
                    split_down(S + 2, 0)
                    for g in range(G):
                        relu_squared(S + 2, 0, g)
            over_blocks(act, body)

        @block.vector
        def _(dve):
            def split_up(S, p):
                dve.wait_ge(up_hi_ready, S + 1)
                dve.tensor_tensor(up_lo[p][:], up_raw[:], up_hi[p][:].bitcast(F32), ALU.subtract).then_inc(up_ready, 1)

            def split_down(S, p):
                dve.wait_ge(dn_hi_ready, S + 1)
                dve.tensor_tensor(dn_lo[p][:], dn_raw[:], dn_hi[p][:].bitcast(F32), ALU.subtract).then_inc(dn_ready, 1)

            def rest(S, p, g):
                dve.wait_ge(a_hi_ready, G * S + g + 1)
                dve.tensor_tensor(a_lo[p][:, g, :], r[:, g, :], a_hi[p][:, g, :].bitcast(F32),
                                  ALU.subtract).then_inc(a_ready, 1)

            def accumulate(b, S, tiles=range(KT)):
                for d in tiles:
                    use = S * KT + b * NPC + d
                    dve.wait_ge(down_done, S * KT + d + 2)
                    if d == 0:
                        dve.wait_ge(zeroed, b + 1)
                    dve.wait_ge(dn_free, use - KT + 1 + CREDIT)
                    out = ffT[:, d, :].rearrange("p (h n) -> p h n", h=2)
                    dve.tensor_tensor(out, out, ps_d[d % 2][:, :, 0:HW], ALU.add).then_inc(dn_free, 1)

            dve.memset(gated[:], 0.0).then_inc(dn_free, CREDIT)
            split_up(0, 0)
            split_up(1, 1)
            split_down(0, 0)
            for g in range(G):
                rest(0, 0, g)
            dve.wait_ge(gates_in, 16 * (1 + STREAMS))

            def body(b, last):
                def unit(S, p):
                    split_up(S + 2, p)
                    rest(S + 1, 1 - p, 0)
                    split_down(S + 1, 1 - p)
                    accumulate(b, S, range(0, EARLY))
                    rest(S + 1, 1 - p, 1)
                    accumulate(b, S, range(EARLY, KT))
                over_steps(dve, b, unit)
                S = (b + 1) * STEPS - 2
                if not last:
                    split_up(S + 2, 0)
                rest(S + 1, 1, 0)
                split_down(S + 1, 1)
                accumulate(b, S, range(0, EARLY))
                rest(S + 1, 1, 1)
                accumulate(b, S, range(EARLY, KT))
                accumulate(b, S + 1)
                for q, (off, w) in enumerate(PIECES):
                    dve.wait_ge(ff_transposed, NPC * b + q + 1)
                    if q == 0:
                        dve.wait_ge(x2_in, 16 * NPC * (b + 1))
                    elif q >= 2:
                        dve.wait_ge(y_ready, NPC * b + q - 1)
                    whose = 1 if last and q == NPC - 1 else 0
                    dve.tensor_tensor(gated[0:w, q % 2, :], ps_d[q % 2][0:w].rearrange("p a n -> p (a n)"),
                                      gate[0:w, whose, :], ALU.mult).then_inc(dn_free, 1)
                if not last:
                    split_up(S + 3, 1)
                    split_down(S + 2, 0)
                    for g in range(G):
                        rest(S + 2, 0, g)
            over_blocks(dve, body)

        @block.tensor
        def _(pe):
            def up(S, p, block_start=None):
                pe.wait_ge(up_ready, S + 1)
                for g in range(G):
                    if not isinstance(S, int) or S > 0:
                        pe.wait_ge(relu_done, G * (S - 1) + g + 1)
                    f = slice(g * P, (g + 1) * P)
                    for k in range(KT):
                        if block_start is not None and g == 0 and k % (KT // PARTS) == 0:
                            pe.wait_ge(hT_in[k // (KT // PARTS)], 32 * (block_start + 1))
                        for j, (w, x) in enumerate(((up_hi, hT[0]), (up_hi, hT[1]), (up_lo, hT[0]))):
                            for half in range(2):
                                last = pe.matmul(ps_u[g][:, half, 0:HW], w[p][:, k, f],
                                                 x[:, k, half * HW:(half + 1) * HW],
                                                 start=(k == 0 and j == 0), stop=(k == KT - 1 and j == 2))
                    last.then_inc(up_done, 1)

            def down(b, S, p):
                pe.wait_ge(dn_ready, S + 1)
                pe.wait_ge(a_ready, G * (S + 1))
                for d in range(KT):
                    use = S * KT + b * NPC + d
                    pe.wait_ge(dn_free, use - (0 if d == 0 else 1) + CREDIT)
                    cols = slice(d * P, (d + 1) * P)
                    for g in range(G):
                        for j, (w, a) in enumerate(((dn_hi, a_hi), (dn_hi, a_lo), (dn_lo, a_hi))):
                            for half in range(2):
                                last = pe.matmul(ps_d[d % 2][:, half, 0:HW], w[p][:, g, cols],
                                                 a[p][:, g, half * HW:(half + 1) * HW],
                                                 start=(g == 0 and j == 0), stop=(g == G - 1 and j == 2))
                    last.then_inc(down_done, 1)

            def transpose_back(b):
                for q, (off, w) in enumerate(PIECES):
                    use = (b + 1) * STEPS * KT + b * NPC + q
                    pe.wait_ge(dn_free, use - (0 if q == 0 else 1) + CREDIT)
                    for d in range(KT):
                        last = pe.transpose(ps_d[q % 2][0:w, d // 4, d % 4 * P:(d % 4 + 1) * P],
                                            ffT[:, d, off:off + w], ident[:])
                    last.then_inc(ff_transposed, 1)

            pe.wait_ge(ident_ready, 1)
            pe.sem_inc(down_done, 1)
            up(0, 0, 0)

            def body(b, last):
                def unit(S, p):
                    up(S + 1, 1 - p)
                    down(b, S, p)
                over_steps(pe, b, unit)
                S = (b + 1) * STEPS - 2
                up(S + 1, 1)
                down(b, S, 0)
                down(b, S + 1, 1)
                transpose_back(b)
                if not last:
                    up(S + 2, 0, b + 1)
            over_blocks(pe, body)


def build(nc, ins, outs):
    t = dict(ins)
    t.update(outs)
    inner = lambda name, shape, dt=F32: nc.dram_tensor(name, shape, dt).ap()
    t["mod"] = inner("mod", [1 + STREAMS, 6 * D])
    t["cT"] = inner("cT", [P, KT, C])
    for name in ("q_split", "k_split", "v_split"):
        t[name] = inner(name, [ROWS, HEADS, 2 * HD], F32R)
    t["q_nat"] = inner("q_nat", [ROWS, ATT])
    t["u"] = inner("u", [ROWS, POOL])
    t["nF_p"] = inner("nF_p", [HEADS, SEQ])
    t["nF_s"] = inner("nF_s", [STREAMS * HEADS, PAST + NEW])
    t["mixT"] = inner("mixT", [D, ROWS])
    t["x2"] = inner("x2", [ROWS, D])
    t["h2T_hi"] = inner("h2T_hi", [D, ROWS], F32R)
    t["h2T_lo"] = inner("h2T_lo", [D, ROWS], F32R)
    for stage in (modulation, projection, pooling, prompt_attention, stream_attention,
                  out_projection, channel_mixing):
        taken = []

        def sems(name):
            taken.append(nc.alloc_semaphore(name=name))
            return taken[-1]
        stage(nc, t, sems)
        nc.clear_and_free_semaphores(taken)
        nc.all_engine_barrier()


_INS = ["x_prompt", "x_sample", "c_prompt", "c_sample", "cache_k", "cache_v", "cache_logf", "cache_pool",
        "w_mod", "b_mod", "w_in", "b_f", "q_gain", "k_gain", "w_pool", "pool_scale", "w_out", "w_up", "w_down"]
_OUTS = [("y_prompt", (1, 2048, 1024), (1, 2048, 1024)), ("y_sample", (8, 16, 1024), (8, 16, 1024)),
         ("k_p", (2048, 768), (1, 1, 2048, 12, 64)), ("v_p", (2048, 768), (1, 1, 2048, 12, 64)),
         ("logf_p", (2048, 12), (1, 1, 2048, 12)), ("pool_p", (15, 256), (1, 1, 15, 256)),
         ("k_s", (128, 768), (1, 8, 16, 12, 64)), ("v_s", (128, 768), (1, 8, 16, 12, 64)),
         ("logf_s", (128, 12), (1, 8, 16, 12)), ("pool_s", (8, 15, 256), (1, 8, 15, 256))]


def kernel(**inputs):
    import numpy as _np
    import concourse.bacc as _bacc
    from concourse.bass_utils import run_bass_kernel_spmd as _run

    nc = _bacc.Bacc("TRN2", target_bir_lowering=False, num_devices=1)
    arrays, ins, outs = {}, {}, {}
    for name in _INS:
        a = _np.ascontiguousarray(inputs[name])
        arrays[f"in_{name}_dram"] = a
        ins[name] = nc.dram_tensor(f"in_{name}_dram", a.shape, F32, kind="ExternalInput").ap()
    for i, (name, shape, _) in enumerate(_OUTS):
        outs[name] = nc.dram_tensor(f"out_{i}_dram", shape, F32, kind="ExternalOutput").ap()
    build(nc, ins, outs)
    r = _run(nc, [arrays], core_ids=[0])
    return tuple(r.results[0][f"out_{i}_dram"].reshape(shape) for i, (_, _, shape) in enumerate(_OUTS))
```
